# Optimizing a Trainium2 kernel written in Bass

```python
import math, functools
import jax, jax.numpy as jnp
from jax import lax
import numpy as np

D_MODEL = 1024
BATCH = 1
SEQ = 1024
DEPTH = 1
DEC_BATCH = 8
DEC_SEQ = 4
PAST_LEN = 2048
PAGE_SIZE = 128

D_MIX = D_MODEL
D_A = D_MIX // 2
D_B = D_MIX - D_A
H_A = 4
DV_A = D_A // H_A
DK_A = DV_A // 2
H_B = 4
DH_B = D_B // H_B
CONV_W = 4
CHUNK = 64
Q_BLOCK = 128
PLE_DIM = 256
EPS = 1e-6
D_IN = 4 * D_A + 3 * D_B
SPLITS = [D_A, 2 * D_A, 3 * D_A, 4 * D_A, 4 * D_A + D_B, 4 * D_A + 2 * D_B]

kernel_name = "hymba_diffattn_mlstm_step"

def rmsnorm(x, g):
    xf = x.astype(jnp.float32)
    y = xf * lax.rsqrt(jnp.mean(xf * xf, axis=-1, keepdims=True) + EPS)
    return (y * g.astype(jnp.float32)).astype(x.dtype)

def headwise_rmsnorm(x, g):
    return rmsnorm(x, g.reshape(x.shape[-2:]))

def diff_attend(q, k, v, q_pos, k_pos, lam):
    s = jnp.einsum('bqhmd,bkhmd->bhmqk', q.astype(jnp.float32), k.astype(jnp.float32)) * (DK_A ** -0.5)
    mask = k_pos[None, :] <= q_pos[:, None]
    p = jax.nn.softmax(jnp.where(mask, s, -jnp.inf), axis=-1)
    w = p[:, :, 0] - lam * p[:, :, 1]
    return jnp.einsum('bhqk,bkhd->bqhd', w, v.astype(jnp.float32))

def attend_prompt(q, k, v, lam):
    B, S = q.shape[:2]
    nb = S // Q_BLOCK
    qb = q.reshape(B, nb, Q_BLOCK, H_A, 2, DK_A).swapaxes(0, 1)
    q_pos = jnp.arange(S).reshape(nb, Q_BLOCK)
    k_pos = jnp.arange(S)
    out = lax.map(lambda t: diff_attend(t[0], k, v, t[1], k_pos, lam), (qb, q_pos))
    return out.swapaxes(0, 1).reshape(B, S, H_A, DV_A)

def attend_paged(q, k, v, lam, cache_k, cache_v, page_table):
    DB, T = q.shape[:2]
    P = page_table.shape[1] * PAGE_SIZE
    pk = cache_k[page_table].reshape(DB, P, H_A, 2, DK_A)
    pv = cache_v[page_table].reshape(DB, P, H_A, DV_A)
    k_all = jnp.concatenate([pk, k.astype(pk.dtype)], axis=1)
    v_all = jnp.concatenate([pv, v.astype(pv.dtype)], axis=1)
    q_pos = P + jnp.arange(T)
    k_pos = jnp.arange(P + T)
    return diff_attend(q, k_all, v_all, q_pos, k_pos, lam)

def causal_conv(xb, buf, w, b):
    S = xb.shape[1]
    xpad = jnp.concatenate([buf.astype(xb.dtype), xb], axis=1)
    out = b + sum(xpad[:, j:j + S] * w[j] for j in range(CONV_W))
    return out, xpad[:, -(CONV_W - 1):]

def mlstm_scan(q, k, v, ig, lf, C0, n0, m0):
    B, S, H, DH = q.shape
    L = math.gcd(S, CHUNK)
    nc = S // L
    f32 = jnp.float32

    def chunks4(a):
        return a.astype(f32).reshape(B, nc, L, H, DH).transpose(1, 0, 3, 2, 4)

    def chunks3(a):
        return a.astype(f32).reshape(B, nc, L, H).transpose(1, 0, 3, 2)

    tril = jnp.tril(jnp.ones((L, L), dtype=bool))

    def step(carry, xs):
        C, n, m = carry
        qc, kc, vc, ic, fc = xs
        b = jnp.cumsum(fc, axis=-1)
        Dm = jnp.where(tril, b[..., :, None] - b[..., None, :] + ic[..., None, :], -jnp.inf)
        inter = b + m[..., None]
        m_t = jnp.maximum(inter, jnp.max(Dm, axis=-1))
        wD = jnp.exp(Dm - m_t[..., None])
        w_in = jnp.exp(inter - m_t)
        sqk = jnp.einsum('bhtd,bhsd->bhts', qc, kc) * wD
        num = w_in[..., None] * jnp.einsum('bhtd,bhde->bhte', qc, C) + jnp.einsum('bhts,bhse->bhte', sqk, vc)
        den = w_in * jnp.einsum('bhtd,bhd->bht', qc, n) + jnp.sum(sqk, axis=-1)
        h = num / jnp.maximum(jnp.abs(den), jnp.exp(-m_t))[..., None]
        bL = b[..., -1]
        g = bL[..., None] - b + ic
        m_new = jnp.maximum(bL + m, jnp.max(g, axis=-1))
        decay = jnp.exp(bL + m - m_new)
        wg = jnp.exp(g - m_new[..., None])
        C_new = decay[..., None, None] * C + jnp.einsum('bhs,bhsd,bhse->bhde', wg, kc, vc)
        n_new = decay[..., None] * n + jnp.einsum('bhs,bhsd->bhd', wg, kc)
        return (C_new, n_new, m_new), h

    carry0 = (C0.astype(f32), n0.astype(f32), m0.astype(f32))
    (C1, n1, m1), h = lax.scan(step, carry0, (chunks4(q), chunks4(k), chunks4(v), chunks3(ig), chunks3(lf)))
    h = h.transpose(1, 0, 3, 2, 4).reshape(B, S, H, DH)
    return h, C1, n1, m1

def hybrid_layer(x, p, attend, conv_buf, C0, n0, m0, lam_init, w):
    B, S, _ = x.shape
    h = rmsnorm(x, w['pre_g'])
    u = h @ w['w_in']
    qa, ka, va, za, xb, ob, zb = jnp.split(u, SPLITS, axis=-1)
    q = qa.reshape(B, S, H_A, 2, DK_A)
    k = ka.reshape(B, S, H_A, 2, DK_A)
    v = va.reshape(B, S, H_A, DV_A)
    f32 = jnp.float32
    lam = (jnp.exp(jnp.sum(w['lq1'].astype(f32) * w['lk1'].astype(f32)))
           - jnp.exp(jnp.sum(w['lq2'].astype(f32) * w['lk2'].astype(f32))) + lam_init)
    a = attend(q, k, v, lam)
    a = headwise_rmsnorm(a, w['attn_g']) * (1.0 - lam_init)
    a = a.reshape(B, S, D_A).astype(x.dtype) * jax.nn.silu(za)
    xc, new_buf = causal_conv(xb, conv_buf, w['conv_w'], w['conv_b'])
    xch = jax.nn.silu(xc).reshape(B, S, H_B, DH_B)
    qb = jnp.einsum('bshd,hde->bshe', xch, w['wq_b'])
    kb = jnp.einsum('bshd,hde->bshe', xch, w['wk_b']) * (DH_B ** -0.5)
    vb = jnp.einsum('bshd,hde->bshe', xb.reshape(B, S, H_B, DH_B), w['wv_b'])
    gates = jnp.concatenate([qb, kb, vb], axis=-1).reshape(B, S, 3 * D_B) @ w['w_if'] + w['b_if']
    ig = gates[..., :H_B].astype(f32)
    lf = jax.nn.log_sigmoid(gates[..., H_B:].astype(f32))
    hb, C1, n1, m1 = mlstm_scan(qb, kb, vb, ig, lf, C0, n0, m0)
    hb = hb * jax.nn.sigmoid(ob.reshape(B, S, H_B, DH_B).astype(f32))
    hb = headwise_rmsnorm(hb, w['mlstm_g']) + w['mlstm_skip'].reshape(H_B, DH_B) * xch
    bo = hb.reshape(B, S, D_B).astype(x.dtype) * jax.nn.silu(zb)
    y = jnp.concatenate([a, bo], axis=-1) @ w['w_out']
    x = x + rmsnorm(y, w['post_g'])
    gate = jax.nn.sigmoid(x @ w['ple_gate'])
    x = x + rmsnorm(gate * (p.astype(x.dtype) @ w['ple_w']), w['ple_g'])
    return x, (k.reshape(B, S, H_A, 2 * DK_A), v, new_buf, C1, n1, m1)

def setup_inputs(seed: int = 0) -> dict:
    key = jax.random.key(seed)
    ks = jax.random.split(key, 40)
    f32 = jnp.float32

    def nrm(k, shape, scale):
        return jax.random.normal(k, shape, f32) * scale

    n_pages = PAST_LEN // PAGE_SIZE
    n_used = DEC_BATCH * n_pages
    n_pool = n_used + n_used // 4
    page_table = jax.random.permutation(ks[0], n_pool)[:n_used].reshape(DEC_BATCH, n_pages).astype(jnp.int32)
    f_bias = jnp.broadcast_to(jnp.linspace(3.0, 6.0, H_B), (DEPTH, H_B)) + nrm(ks[1], (DEPTH, H_B), 0.1)
    i_bias = nrm(ks[2], (DEPTH, H_B), 0.1)
    return {
        'x_prompt': nrm(ks[3], (BATCH, SEQ, D_MODEL), 1.0),
        'x_sample': nrm(ks[4], (DEC_BATCH, DEC_SEQ, D_MODEL), 1.0),
        'cache_k': nrm(ks[5], (DEPTH, n_pool, PAGE_SIZE, H_A, 2 * DK_A), 1.0),
        'cache_v': nrm(ks[6], (DEPTH, n_pool, PAGE_SIZE, H_A, DV_A), 1.0),
        'state_conv': nrm(ks[7], (DEPTH, DEC_BATCH, CONV_W - 1, D_B), 1.0),
        'state_C': nrm(ks[8], (DEPTH, DEC_BATCH, H_B, DH_B, DH_B), DH_B ** -0.5),
        'state_n': nrm(ks[9], (DEPTH, DEC_BATCH, H_B, DH_B), 1.0),
        'state_m': nrm(ks[10], (DEPTH, DEC_BATCH, H_B), 1.0),
        'page_table': page_table,
        'p_prompt': nrm(ks[11], (DEPTH, BATCH, SEQ, PLE_DIM), 1.0),
        'p_sample': nrm(ks[12], (DEPTH, DEC_BATCH, DEC_SEQ, PLE_DIM), 1.0),
        'norm_pre_g': 1.0 + nrm(ks[13], (DEPTH, D_MODEL), 0.05),
        'norm_post_g': 1.0 + nrm(ks[14], (DEPTH, D_MODEL), 0.05),
        'w_in': nrm(ks[15], (DEPTH, D_MODEL, D_IN), D_MODEL ** -0.5),
        'lam_q1': nrm(ks[16], (DEPTH, DK_A), 0.1),
        'lam_k1': nrm(ks[17], (DEPTH, DK_A), 0.1),
        'lam_q2': nrm(ks[18], (DEPTH, DK_A), 0.1),
        'lam_k2': nrm(ks[19], (DEPTH, DK_A), 0.1),
        'attn_norm_g': 1.0 + nrm(ks[20], (DEPTH, D_A), 0.05),
        'conv_w': nrm(ks[21], (DEPTH, CONV_W, D_B), CONV_W ** -0.5),
        'conv_b': nrm(ks[22], (DEPTH, D_B), 0.02),
        'w_q_b': nrm(ks[23], (DEPTH, H_B, DH_B, DH_B), DH_B ** -0.5),
        'w_k_b': nrm(ks[24], (DEPTH, H_B, DH_B, DH_B), DH_B ** -0.5),
        'w_v_b': nrm(ks[25], (DEPTH, H_B, DH_B, DH_B), DH_B ** -0.5),
        'w_if': nrm(ks[26], (DEPTH, 3 * D_B, 2 * H_B), 0.3 * (3 * D_B) ** -0.5),
        'b_if': jnp.concatenate([i_bias, f_bias], axis=-1),
        'mlstm_norm_g': 1.0 + nrm(ks[27], (DEPTH, D_B), 0.05),
        'mlstm_skip': 1.0 + nrm(ks[28], (DEPTH, D_B), 0.05),
        'w_out': nrm(ks[29], (DEPTH, D_MIX, D_MODEL), D_MIX ** -0.5),
        'ple_w': nrm(ks[30], (DEPTH, PLE_DIM, D_MODEL), PLE_DIM ** -0.5),
        'ple_gate_w': nrm(ks[31], (DEPTH, D_MODEL, D_MODEL), D_MODEL ** -0.5),
        'ple_norm_g': 1.0 + nrm(ks[32], (DEPTH, D_MODEL), 0.05),
    }

def reference(x_prompt, x_sample, cache_k, cache_v, state_conv, state_C, state_n, state_m, page_table,
              p_prompt, p_sample, norm_pre_g, norm_post_g, w_in, lam_q1, lam_k1, lam_q2, lam_k2,
              attn_norm_g, conv_w, conv_b, w_q_b, w_k_b, w_v_b, w_if, b_if, mlstm_norm_g, mlstm_skip,
              w_out, ple_w, ple_gate_w, ple_norm_g):
    B = x_prompt.shape[0]
    xp, xs = x_prompt, x_sample
    outs_p, outs_s = [], []
    for l in range(DEPTH):
        w = {'pre_g': norm_pre_g[l], 'post_g': norm_post_g[l], 'w_in': w_in[l],
             'lq1': lam_q1[l], 'lk1': lam_k1[l], 'lq2': lam_q2[l], 'lk2': lam_k2[l],
             'attn_g': attn_norm_g[l], 'conv_w': conv_w[l], 'conv_b': conv_b[l],
             'wq_b': w_q_b[l], 'wk_b': w_k_b[l], 'wv_b': w_v_b[l], 'w_if': w_if[l], 'b_if': b_if[l],
             'mlstm_g': mlstm_norm_g[l], 'mlstm_skip': mlstm_skip[l], 'w_out': w_out[l],
             'ple_w': ple_w[l], 'ple_gate': ple_gate_w[l], 'ple_g': ple_norm_g[l]}
        lam_init = 0.8 - 0.6 * math.exp(-0.3 * l)
        conv0 = jnp.zeros((B, CONV_W - 1, D_B), xp.dtype)
        C0 = jnp.zeros((B, H_B, DH_B, DH_B), jnp.float32)
        n0 = jnp.zeros((B, H_B, DH_B), jnp.float32)
        m0 = jnp.zeros((B, H_B), jnp.float32)
        xp, st_p = hybrid_layer(xp, p_prompt[l], attend_prompt, conv0, C0, n0, m0, lam_init, w)
        attend_sample = functools.partial(attend_paged, cache_k=cache_k[l], cache_v=cache_v[l], page_table=page_table)
        xs, st_s = hybrid_layer(xs, p_sample[l], attend_sample, state_conv[l], state_C[l], state_n[l], state_m[l], lam_init, w)
        outs_p.append(st_p)
        outs_s.append(st_s)
    kp, vp, cp, Cp, np_, mp = [jnp.stack([o[i] for o in outs_p]) for i in range(6)]
    ks_, vs_, cs_, Cs_, ns_, ms_ = [jnp.stack([o[i] for o in outs_s]) for i in range(6)]
    return (xp, xs, kp, vp, cp, Cp, np_, mp, ks_, vs_, cs_, Cs_, ns_, ms_)


_drawn_inputs = setup_inputs


def setup_inputs(seed=0):
    import zlib

    import numpy as np

    out = dict(_drawn_inputs(seed))
    spreads = {}
    factors = {}
    for name, (base, spread) in spreads.items():
        noise = np.random.default_rng([zlib.crc32(name.encode()), seed]).standard_normal(out[name].shape)
        drawn = base * np.exp(spread * noise) if base else spread * noise
        out[name] = __import__('jax').numpy.asarray(drawn.astype(out[name].dtype))
    for name, factor in factors.items():
        out[name] = (out[name] * factor).astype(out[name].dtype)
    return out
```

```python
import concourse.bass as bass
from concourse import mybir
from contextlib import ExitStack

F32 = mybir.dt.float32
F32R = mybir.dt.float32r
I32 = mybir.dt.int32
ALU = mybir.AluOpType
ACT = mybir.ActivationFunctionType
AX = mybir.AxisListType

P = 128
D = 1024
H = 4
DH = 128
SEQ = 1024
NSEQ, STEPS = 8, 4
SMP = NSEQ * STEPS
TOK = SEQ + SMP
KC = D // P
NT = 28
CH = SEQ // P
PAGE = 128
PAGES = 16
PAST = PAGE * PAGES
POOL = 160
GP = 2
GROUPS = PAGES // GP
PLE = 256
EPS = 1e-6
NEG = -1e30
LOWEST = -3.4e38
THIRD = TOK // 3
LAM_INIT = 0.8 - 0.6
KSCALE = DH ** -0.5
QSCALE = 64 ** -0.5
PARAMS = 11
QA, KA, VA, ZA, XB, OB, ZB = (4 * n for n in range(7))
SECTIONS = [(QA, 12, ACT.Copy), (XB, 4, ACT.Copy), (OB, 4, ACT.Sigmoid), (ZA, 4, ACT.Silu), (ZB, 4, ACT.Silu)]
XT = [(t * P, P) for t in range(CH)] + [(SEQ, SMP)]


def bc(ap, n):
    return ap.rearrange("p (h o) -> p h o", o=1).broadcast_to([ap.shape[0], ap.shape[1], n])


def lead(ap, n):
    return ap.rearrange("p (o t) -> p o t", o=1).broadcast_to([ap.shape[0], n, ap.shape[1]])


CONV_STEPS = 2 * 4 * H
NARROW = 4 * H
WT_BEFORE = [sum((v // H + 4) // 4 for v in range(u)) for u in range(CH * H + 1)]


def program(nc, io):
    ctx = ExitStack()
    with ctx:
        def sb(name, shape, dt=F32):
            return ctx.enter_context(nc.sbuf_tensor(name, shape, dt))

        def sem(name):
            return ctx.enter_context(nc.semaphore(name))

        ps = ctx.enter_context(nc.psum_tensor("ps", [P, 8, 512], F32))

        ident = sb("ident", [P, P])
        ones = sb("ones", [P, P])
        mask_t = sb("mask_t", [P, P])
        mask_q = sb("mask_q", [P, P])
        mask_s = sb("mask_s", [SMP, SMP])
        seqmask = sb("seqmask", [SMP, NSEQ])
        place_q = sb("place_q", [P, H, 60])
        mask_new = sb("mask_new", [P, 60])
        small = sb("small", [P, 160])
        sumsq, rstd, mhalf = small[:, 0:9], small[:, 16:25], small[:, 32:33]
        vec = small[:, 64:96]
        conv_w, conv_b, attn_g, mlstm_g, skip = vec[:, 0:16], vec[:, 16:20], vec[:, 20:24], vec[:, 24:28], vec[:, 28:32]
        bias_i, bias_f = small[0:H, 33:34], small[32:32 + H, 33:34]
        lam_e = small[:, 34:36]
        lam, neg_lam, sign, row_t, row_4 = (small[:, 36 + n:37 + n] for n in range(5))
        ag = small[:, 44:48]
        mcol = small[0:H, 48:48 + CH + 1]
        coef = small[:, 96:104]
        den_s = small[:, 104:112]
        gmax = small[:, 112:121]
        negmax_s = small[:, 121:122]
        ss4, rs4, rd4 = small[:, 124:128], small[:, 128:132], small[:, 132:136]
        map_scale = small[:, 144:146]
        eps = small[:, 146:147]
        aL, dec4 = small[0:H, 136:137], small[:, 140:144]
        wif = sb("wif", [P, 12, 36])
        U = sb("U", [P, NT, TOK])

        base = (nc.sbuf_base + 31) // 32 * 32
        u_base = base - NT * TOK * 4
        top = [base]

        def place(name, shape, dt=F32, offset=None):
            size = 4
            for n in shape[1:]:
                size *= n
            size = (size + 31) // 32 * 32
            if offset is None:
                offset = top[0]
                top[0] += size
            return nc.alloc_sbuf_tensor_at(name, shape, dt, offset=offset)

        hhi = place("hhi", [P, KC, TOK], F32R)
        hlo = place("hlo", [P, KC, TOK], F32R)
        wst = place("wst", [P, 4, 4, P])
        whi = place("whi", [P, 2, 4, P], F32R)
        wlo = place("wlo", [P, 2, 4, P], F32R)
        xrow, hrow, square, gpre = U[:, 0:2, 0:D], U[:, 2:4, 0:D], U[:, 4, 0:D], U[:, 5, 0:D]
        vrow, lamv, lamp = U[0:32, 6, 0:P], U[:, 7, 0:256], U[:, 8, 0:128]
        iot = U[:, 9, 0:8].bitcast(I32)
        iof = U[:, 10, 0:8]

        top[0] = base
        xch = place("xch", [P, H, TOK])
        wqkv = place("wqkv", [P, 3, H, DH])
        qbT = place("qbT", [P, H, P])
        kbT = place("kbT", [P, H, P])
        vbT = place("vbT", [P, H, P])
        vaug = place("vaug", [P, H, DH + 1])
        kw = place("kw", [P, H, DH])
        E = place("E", [P, H, P])
        Ablk = place("Ablk", [P, H, P])
        nd = place("nd", [P, H, DH + 1])
        Caug = place("Caug", [P, H, DH + 1])
        G = place("G", [P, P])
        GT = place("GT", [P, P])
        AO = place("AO", [P, DH])
        AS = place("AS", [P, P])
        q8 = place("q8", [P, NSEQ, H, 8])
        q8cur = place("q8cur", [P, H, 32])
        Dg = place("Dg", [P, H])
        gat = place("gat", [H, 8, P])
        pT = place("pT", [P, PAGES + 1, 32])
        vS = place("vS", [SMP, 512])
        ptab = place("ptab", [1, NSEQ * PAGES], I32)
        stream_a = top[0]
        kTs = place("kTs", [P, 2, H, GP * PAGE])
        S = place("S", [P, PAST + SMP])
        ring_k = top[0]
        Kr = place("Kr", [P, 4, 512])
        ring_v = top[0]
        Vr = place("Vr", [P, 4, 512])
        assert top[0] <= nc.sbuf_usable_end, top[0]
        Cs = place("Cs", [P, NSEQ * H, DH + 1], offset=stream_a)
        top[0] = ring_k
        xpad = place("xpad", [P, H, NSEQ, 7])
        nrow = place("nrow", [SMP, DH])
        kwm = place("kwm", [SMP, 2, H, DH], offset=ring_k)
        crow = place("crow", [24, 512])
        top[0] = max(top[0], ring_k + 2 * H * DH * 4)
        nout = place("nout", [SMP, DH])
        kS = place("kS", [SMP, 512])
        xbS = place("xbS", [SMP, 512])
        xbP = place("xbP", [3, 512])
        qmask = place("qmask", [P, NSEQ, H, SMP])
        AblkS = place("AblkS", [P, H, SMP])
        DgS = place("DgS", [P, H, NSEQ])
        decS = place("decS", [P, H, NSEQ])
        g5 = place("g5", [H, 8, NSEQ, 5])
        gs = place("gs", [H, 6, SMP])
        assert top[0] <= nc.sbuf_usable_end

        top[0] = base
        wout = place("wout", [P, KC, D])
        vtok = place("vtok", [P, CH, 512])
        ktok = place("ktok", [P, 2, 512])
        pp = place("pp", [P, 2, 2, SEQ])
        wT = place("wT", [P, CH, P])
        qz = place("qz", [P, 3, 2, P])
        on = place("on", [P, 2, P])
        plew = place("plew", [P, 2, D])
        st = place("st", [P, 2, 16])
        assert top[0] <= nc.sbuf_usable_end
        wgate = place("wgate", [P, KC, D], offset=u_base + XB * TOK * 4)
        top[0] = u_base
        gpost = place("gpost", [P, D])
        gple = place("gple", [P, D])
        xin = place("xin", [P, 2, D])
        x1 = place("x1", [P, 2, D])
        x1T = place("x1T", [P, KC, P])
        pws = place("pws", [P, D])
        sg = place("sg", [P, D])
        prow = place("prow", [P, PLE])
        pTt = place("pTt", [P, 2, P])
        sqt = place("sqt", [P, D])
        assert top[0] <= u_base + ZA * TOK * 4

        names = """ident_ready masks_ready gpre_in sumsq_ready rstd_ready h_ready hT_ready hhi_ready hlo_ready whi_ready
            wlo_ready w_used u_stored ag_ready iota_ready lam_sum wif_in wqkv_in ptab_in crow_in cs_in
            nrow_in conv_step silu_ready zero_ready q8_ready s_proj s_qk_stored s_kvtok s_gate_step
            s_gate_exp s_rows s_GT_stored s_kwm s_cu s_C s_h_gated s_bo_t pT_ready pT_act pT_dve
            proj_ready qk_stored v_stored k_used v_used kT_act kT_dve scores_ready s_stored negmax_ready
            p_ready coef_ready o_ready ao_ready comb_ready as_added q8cur_ready gates_ready kvtok_ready
            sqk_ready vaug_stored gate_step gate_exp rows_exp GT_ready AB_ready gt_stored kw_ready
            arg_ready E_ready W_ready inter_ready intra_ready nd_scaled nd_ready cu_ready C_done obT_ready
            ob_copied h_gated sq_ready hrs_ready hn_ready hTr_ready bo_t bo_done xsk_ready kt_ready
            vt_ready kt_stored vt_stored out_v_prompt qz_ready sc0 sc1 masked rmax pexp w_done wT_ready
            wT_stored pv_ready psq prs on_ready onT_ready a_done wout_in wgate_in plew_in g_in y_ready
            y_sq y_rs y_n y_x prow_T prow_stored pw_ready pw_stored x1T_ready x1T_stored gate_ready
            gate_sig t_done t_sq t_rs t_n out_ready params_in out_sample out_state mean_ready w_step
            soft_step""".split()
        s = {n: sem(n) for n in names}
        once = {"pe": """vecT_ready krow_ready vrow_ready xbrow_ready last3_ready hist_ready nT_ready s_gates s_sqk s_GT
            s_AB s_inter s_intra s_obT s_nrow s_hT as_T_ready as_T2""",
                "act": """lam_exp vec_ready hist_stored krow_stored vrow_stored xbrow_stored last3_stored n_stored s_vaug
            s_E s_nd_scaled s_nout s_sq as_norm as_n2""",
                "dve": """lam_ready xpad_new s_v_stored s_kw s_arg s_W s_nd s_hn s_bo den_step as_done""",
                "pool": """wif_zero s_rs as_hrs"""}
        signal, done = {}, {}
        for engine, steps in once.items():
            steps_done = sem(f"{engine}_once")
            for n, name in enumerate(steps.split()):
                signal[name], done[name] = (steps_done, 1), (steps_done, n + 1)
        x_in = [sem("x_in0"), sem("x_in1")]
        w_in = [sem(f"w_in{n}") for n in range(4)]
        k_in = [sem(f"k_in{n}") for n in range(2)]
        v_in = [sem(f"v_in{n}") for n in range(2)]
        k_out = [sem("k_out0"), sem("k_out1")]
        xt_in = [sem("xt_in0"), sem("xt_in1")]
        pr_in = sem("pr_in")
        y_out = [sem("y_out0"), sem("y_out1")]

        def score_row(u, m):
            first, banks = (2 * (u % 2) + m, 1) if u < NARROW else (2 * m, 2)
            return ps[:, first:first + banks, :].rearrange("p a b -> p (a b)")

        def head_bank(u):
            return 5 + u % 2 if u < NARROW else 6

        block = ctx.enter_context(nc.Block())

        @block.sync
        def _(sp):
            def put(name, out, in_, **more):
                sp.dma_start(out, in_, **more).then_inc(s[name], 16)

            sp.dma_start(gpre, io["norm_pre_g"][0:1, :].broadcast_to([P, D])).then_inc(s["gpre_in"], 16)
            xs = io["x_sample"].rearrange("b t d -> (b t) d")

            def load_x(t):
                t0, n = XT[t]
                src = io["x_prompt"][0, t0:t0 + n, :] if t < CH else xs
                sp.dma_start(xrow[0:n, t % 2, :], src).then_inc(x_in[t % 2], 16)

            load_x(0)
            load_x(1)
            sp.dma_start(vrow[0:16, :], io["conv_w"][0].rearrange("j (c p) -> (j c) p", p=P)).then_inc(s["params_in"], 16)
            for n, name in enumerate(("conv_b", "attn_norm_g", "mlstm_norm_g", "mlstm_skip")):
                sp.dma_start(vrow[16 + 4 * n:20 + 4 * n, :], io[name][0].rearrange("(c p) -> c p", p=P)
                             ).then_inc(s["params_in"], 16)
            for n, name in enumerate(("lam_q1", "lam_k1", "lam_q2", "lam_k2")):
                sp.dma_start(lamv[:, 64 * n:64 * n + 64], io[name][0:1, :].broadcast_to([P, 64])).then_inc(s["params_in"], 16)
            sp.dma_start(bias_i, io["b_if"][0, 0:H].rearrange("(h o) -> h o", o=1)).then_inc(s["params_in"], 16)
            sp.dma_start(bias_f, io["b_if"][0, H:2 * H].rearrange("(h o) -> h o", o=1)).then_inc(s["params_in"], 16)
            for t in range(2, 9):
                sp.wait_ge(s["h_ready"], t - 1)
                load_x(t)

            w_dram = io["w_in"][0].rearrange("(k p) n -> p k n", p=P)

            def load_w(q, tile, hf, slot, wait):
                if wait:
                    sp.wait_ge(s["wlo_ready"], q - 3)
                sp.dma_start(wst[:, slot, :, :], w_dram[:, 4 * hf:4 * hf + 4, bass.ds(tile * P, P)]
                             ).then_inc(w_in[slot], 16)

            n = 0
            for first, count, _ in SECTIONS:
                if n == 0:
                    for m in range(2):
                        for hf in range(2):
                            load_w(0, first + m, hf, 2 * m + hf, False)
                with sp.Fori(n // 2 + (n == 0), (n + count) // 2) as pair:
                    b = pair * 2
                    for m in range(2):
                        for hf in range(2):
                            load_w(2 * (b + m) + hf, b + (m + first - n), hf, 2 * m + hf, True)
                if n == 0:
                    sp.wait_ge(*done["wif_zero"])
                    gates = io["w_if"][0].rearrange("(c p) n -> p c n", p=P)
                    sp.dma_start(wif[:, :, 0:H], gates[:, :, 0:H]).then_inc(s["wif_in"], 16)
                    sp.dma_start(wif[:, :, 32:32 + H], gates[:, :, H:2 * H]).then_inc(s["wif_in"], 16)
                n += count

            sp.wait_ge(s["w_used"], 2 * NT)
            sp.dma_start(crow[:, :], io["state_conv"][0].rearrange("b j d -> (b j) d")).then_inc(s["crow_in"], 16)
            for j, name in enumerate(("w_q_b", "w_k_b", "w_v_b")):
                sp.dma_start(wqkv[:, j, :, :], io[name][0].rearrange("h d e -> d h e")).then_inc(s["wqkv_in"], 16)
            sp.dma_start(nrow[:, :], io["state_n"][0].rearrange("b h d -> (b h) d")).then_inc(s["nrow_in"], 16)
            sp.dma_start(g5[:, 1, :, 0], io["state_m"][0].rearrange("b h -> h b"), allow_slow_non_contiguous=True).then_inc(s["cs_in"], 16)
            sp.dma_start(Cs[:, :, 0:DH], io["state_C"][0].rearrange("b h d e -> d (b h) e")).then_inc(s["cs_in"], 16)
            sp.dma_start(ptab[:, :], io["page_table"].rearrange("(o b) n -> o (b n)", o=1)).then_inc(s["ptab_in"], 16)

            sp.wait_ge(*done["krow_stored"])
            put("out_sample", io["k_sample"][0].rearrange("b t h d -> (b t) (h d)"), kS[:, :])
            sp.wait_ge(*done["vrow_stored"])
            put("out_sample", io["v_sample"][0].rearrange("b t h d -> (b t) (h d)"), vS[:, :])
            sp.wait_ge(*done["xbrow_stored"])
            for b in range(NSEQ):
                put("out_sample", io["conv_sample"][0, b], xbS[STEPS * b + 1:STEPS * b + STEPS, :])
            sp.wait_ge(*done["last3_stored"])
            put("out_sample", io["conv_prompt"][0, 0], xbP[:, :])
            sp.wait_ge(s["s_gate_step"], 11)
            put("out_sample", io["m_sample"][0].rearrange("b h -> h b"), g5[:, 4, :, STEPS],
                allow_slow_non_contiguous=True)
            sp.wait_ge(s["s_C"], NSEQ)
            put("out_sample", io["C_sample"][0].rearrange("b h d e -> d (b h) e"), Cs[:, :, 0:DH])
            sp.wait_ge(*done["s_nout"])
            put("out_sample", io["n_sample"][0].rearrange("b h d -> (b h) d"), nout[:, :])
            sp.wait_ge(*done["s_bo"])
            sp.wait_ge(s["out_sample"], 16 * (NSEQ + 6))

            sp.wait_ge(s["ptab_in"], 16)
            ck = io["cache_k"][0].rearrange("n p h d -> n p (h d)")
            cv = io["cache_v"][0].rearrange("n p h d -> n p (h d)")

            def page(cache, buf, slot, seq, n, signal):
                num = sp.value_load(ptab[0:1, bass.ds(seq * PAGES + n, 1)], min_val=0, max_val=POOL - 1)
                sp.dma_start(buf[:, slot, :], cache[bass.ds(num, 1), :, :].rearrange("o p d -> (o p) d")
                             ).then_inc(signal, 16)

            def stream_pages(i, first, last):
                for g in range(GROUPS):
                    if not last:
                        if not (first and g < 2):
                            sp.wait_ge(s["k_used"], i * GROUPS + (g - 1))
                        for n in range(GP):
                            page(ck, Kr, (GP * g + n) % 4, i, GP * g + n, k_in[g % 2])
                    if not first:
                        if not (isinstance(i, int) and i == 1 and g < 2):
                            sp.wait_ge(s["v_used"], (i - 1) * GROUPS + (g - 1))
                        for n in range(GP):
                            page(cv, Vr, (GP * g + n) % 4, i - 1, GP * g + n, v_in[g % 2])

            stream_pages(0, True, False)
            stream_pages(1, False, False)
            with sp.Fori(2, NSEQ) as i:
                stream_pages(i, False, False)
            stream_pages(NSEQ, False, True)

            sp.wait_ge(s["C_done"], CH)
            put("out_state", io["C_prompt"][0, 0].rearrange("h d e -> d h e"), Caug[:, :, 0:DH])
            put("out_state", io["n_prompt"][0, 0].rearrange("h d -> d h"), Caug[:, :, DH],
                allow_slow_non_contiguous=True)
            put("out_state", io["m_prompt"][0, 0].rearrange("(h o) -> h o", o=1), mcol[:, CH:CH + 1])
            sp.wait_ge(s["out_state"], 48)
            sp.wait_ge(*done["as_done"])
            kp = io["k_prompt"][0, 0].rearrange("t h d -> t (h d)")
            vp = io["v_prompt"][0, 0].rearrange("t h d -> t (h d)")
            for t in range(CH):
                sp.wait_ge(s["kt_stored"], t + 1)
                sp.dma_start(kp[t * P:(t + 1) * P, :], ktok[:, t % 2, :]).then_inc(k_out[t % 2], 16)
                sp.wait_ge(s["vt_stored"], t + 1)
                put("out_v_prompt", vp[t * P:(t + 1) * P, :], vtok[:, t, :])
            put("wout_in", wout[:, :, :], io["w_out"][0].rearrange("(k p) n -> p k n", p=P))
            put("wgate_in", wgate[:, :, :], io["ple_gate_w"][0].rearrange("(k p) n -> p k n", p=P))
            put("plew_in", plew[:, :, :], io["ple_w"][0].rearrange("(k p) n -> p k n", p=P))

            sp.wait_ge(s["a_done"], CH * H)
            put("g_in", gpost[:, :], io["norm_post_g"][0:1, :].broadcast_to([P, D]))
            put("g_in", gple[:, :], io["ple_norm_g"][0:1, :].broadcast_to([P, D]))
            pin = io["p_sample"][0].rearrange("b t d -> (b t) d")
            yout = io["y_sample"].rearrange("b t d -> (b t) d")

            def load_tail(j):
                t0, n = XT[j]
                if j >= 2:
                    sp.wait_ge(s["y_x"], j - 1)
                sp.dma_start(xin[0:n, j % 2, :], io["x_prompt"][0, t0:t0 + n, :] if j < CH else xs
                             ).then_inc(xt_in[j % 2], 16)
                if j >= 1:
                    sp.wait_ge(s["prow_T"], j)
                sp.dma_start(prow[0:n, :], io["p_prompt"][0, 0, t0:t0 + n, :] if j < CH else pin).then_inc(pr_in, 16)

            load_tail(0)
            load_tail(1)
            for j, (t0, n) in enumerate(XT):
                if j + 2 < 9:
                    load_tail(j + 2)
                sp.wait_ge(s["out_ready"], j + 1)
                sp.dma_start(io["y_prompt"][0, t0:t0 + n, :] if j < CH else yout, x1[0:n, j % 2, :]
                             ).then_inc(y_out[j % 2], 16)
            for n in range(2):
                sp.wait_ge(k_out[n], 16 * CH // 2)
            sp.wait_ge(s["out_v_prompt"], 16 * CH)
            sp.wait_ge(y_out[0], 16 * 5)
            sp.wait_ge(y_out[1], 16 * 4)

        @block.gpsimd
        def _(pool):
            nc.gpsimd.memset(ident[:, :], 0.0).then_inc(s["zero_ready"], 1)
            nc.gpsimd.memset(ones[:, :], 1.0).then_inc(s["zero_ready"], 1)
            nc.gpsimd.memset(mhalf, -0.5).then_inc(s["zero_ready"], 1)
            nc.gpsimd.memset(eps, EPS).then_inc(s["zero_ready"], 1)
            pool.wait_ge(s["zero_ready"], 4)
            nc.gpsimd.affine_select(out=ident[:, :], in_=ident[:, :], compare_op=ALU.not_equal, fill=1.0, base=0,
                                    pattern=[[-1, P]], channel_multiplier=1).then_inc(s["ident_ready"], 1)

            def root(mean, out, wait, count, done):
                rows, cols = out.shape
                pool.wait_ge(*wait)
                nc.gpsimd.tensor_tensor(out, mean, eps[0:rows, :].broadcast_to([rows, cols]), ALU.add
                                        ).then_inc(s["mean_ready"], 1)
                pool.wait_ge(s["mean_ready"], count)
                nc.gpsimd.tensor_tensor(out, out, mhalf[0:rows, :].broadcast_to([rows, cols]), ALU.pow
                                        ).then_inc(*(s[done], 1) if done in s else signal[done])

            for t, (t0, n) in enumerate(XT):
                root(sumsq[0:n, t:t + 1], rstd[0:n, t:t + 1], (s["sumsq_ready"], t + 1), t + 1, "rstd_ready")

            nc.gpsimd.memset(wif[:, :, :], 0.0).then_inc(*signal["wif_zero"])
            nc.gpsimd.memset(mask_t[:, :], 0.0).then_inc(s["zero_ready"], 1)
            nc.gpsimd.memset(mask_q[:, :], 0.0).then_inc(s["zero_ready"], 1)
            nc.gpsimd.memset(place_q[:, :, :], 0.0).then_inc(s["zero_ready"], 1)
            nc.gpsimd.memset(mask_new[:, :], NEG).then_inc(s["zero_ready"], 1)
            nc.gpsimd.memset(seqmask[:, :], 1.0).then_inc(s["zero_ready"], 1)
            nc.gpsimd.memset(map_scale, QSCALE).then_inc(s["zero_ready"], 1)
            nc.gpsimd.iota(iot[:, 0:1], pattern=[[0, 1]], base=0, channel_multiplier=1).then_inc(s["iota_ready"], 1)
            nc.gpsimd.iota(iot[:, 3:8], pattern=[[1, 5]], base=-1, channel_multiplier=0).then_inc(s["iota_ready"], 1)
            pool.wait_ge(s["zero_ready"], 4 + 6)
            nc.gpsimd.affine_select(out=mask_t[:, :], in_=mask_t[:, :], compare_op=ALU.is_ge, fill=NEG, base=0,
                                    pattern=[[1, P]], channel_multiplier=-1).then_inc(s["masks_ready"], 1)
            nc.gpsimd.affine_select(out=mask_q[:, :], in_=mask_q[:, :], compare_op=ALU.is_ge, fill=NEG, base=0,
                                    pattern=[[-1, P]], channel_multiplier=1).then_inc(s["masks_ready"], 1)
            nc.gpsimd.affine_select(out=place_q[:, :, 28:32], in_=place_q[:, :, 28:32], compare_op=ALU.not_equal,
                                    fill=1.0, base=0, pattern=[[-32, H], [-1, STEPS]], channel_multiplier=1
                                    ).then_inc(s["masks_ready"], 1)
            nc.gpsimd.affine_select(out=seqmask[:, :], in_=seqmask[:, :], compare_op=ALU.is_ge, fill=0.0, base=0,
                                    pattern=[[-STEPS, NSEQ]], channel_multiplier=1).then_inc(s["masks_ready"], 1)
            pool.wait_ge(s["masks_ready"], 4)
            nc.gpsimd.affine_select(out=place_q[:, :, 28:32], in_=place_q[:, :, 28:32], compare_op=ALU.not_equal,
                                    fill=1.0, base=-STEPS, pattern=[[-32, H], [-1, STEPS]], channel_multiplier=1
                                    ).then_inc(s["masks_ready"], 1)
            nc.gpsimd.affine_select(out=seqmask[:, :], in_=seqmask[:, :], compare_op=ALU.is_ge, fill=0.0,
                                    base=STEPS - 1, pattern=[[STEPS, NSEQ]], channel_multiplier=-1
                                    ).then_inc(s["masks_ready"], 1)
            nc.gpsimd.affine_select(out=mask_s.rearrange("s (b t) -> s b t", t=STEPS),
                                    in_=mask_t[0:SMP, 0:SMP].rearrange("s (b t) -> s b t", t=STEPS),
                                    compare_op=ALU.is_ge, fill=NEG, base=0, pattern=[[-STEPS, NSEQ], [0, STEPS]],
                                    channel_multiplier=1).then_inc(s["masks_ready"], 1)

            nc.gpsimd.affine_select(out=map_scale[:, 0:1], in_=map_scale[:, 0:1], compare_op=ALU.is_ge, fill=0.0,
                                    base=63, pattern=[[0, 1]], channel_multiplier=-1).then_inc(s["masks_ready"], 1)
            nc.gpsimd.affine_select(out=map_scale[:, 1:2], in_=map_scale[:, 1:2], compare_op=ALU.is_ge, fill=0.0,
                                    base=-64, pattern=[[0, 1]], channel_multiplier=1).then_inc(s["masks_ready"], 1)

            pool.wait_ge(s["w_used"], 2 * NT)
            for z in (qmask, Ablk, AblkS, Dg, DgS, G, q8cur, Caug, AS, vaug):
                nc.gpsimd.memset(z[:], 1.0 if z is vaug else 0.0).then_inc(s["zero_ready"], 1)
            pool.wait_ge(s["zero_ready"], 4 + 6 + 10)
            pool.wait_ge(s["u_stored"], NT)
            pool.wait_ge(s["masks_ready"], 9)
            for m in range(2):
                for h in range(H):
                    nc.gpsimd.tensor_scalar(q8[:, :, h, 4 * m:4 * m + 4],
                                            U[:, QA + h, SEQ:TOK].rearrange("p (b t) -> p b t", t=STEPS),
                                            map_scale[:, m:m + 1], 0.0, ALU.mult, ALU.add).then_inc(s["q8_ready"], 1)
            pool.wait_ge(s["s_qk_stored"], 1)
            for b in range(NSEQ):
                nc.gpsimd.tensor_copy(qmask[:, b, :, STEPS * b:STEPS * (b + 1)], qbT[:, :, STEPS * b:STEPS * (b + 1)]
                                      ).then_inc(s["q8_ready"], 1)
            root(ss4[0:SMP, :], rs4[0:SMP, :], done["s_sq"], 10, "s_rs")

            pool.wait_ge(s["q8_ready"], 2 * H)

            def stream_pool(i):
                t0 = i * P
                if not (isinstance(i, int) and i == 0):
                    pool.wait_ge(s["scores_ready"], i * (GROUPS + 1))
                nc.gpsimd.tensor_copy(q8cur[:, :, 0:8], q8[:, bass.ds(i, 1), :, :].rearrange("p o h c -> p (o h) c")
                                      ).then_inc(s["q8cur_ready"], 1)
                pool.wait_ge(s["proj_ready"], 3 * i + 3)
                x = xch[:, :, bass.ds(t0, P)]
                nc.gpsimd.tensor_tensor(x, x, bc(skip, P), ALU.mult).then_inc(s["xsk_ready"], 1)
                pool.wait_ge(s["sqk_ready"], i + 1)
                nc.gpsimd.tensor_copy(kbT[:, :, :], U[:, OB:OB + H, bass.ds(t0, P)]).then_inc(s["ob_copied"], 1)
                root(ss4, rs4, (s["sq_ready"], i + 1), i + 11, "hrs_ready")

            stream_pool(0)
            with pool.Fori(1, CH) as i:
                stream_pool(i)

            root(ss4[:, 0:1], rs4[:, 0:1], done["as_norm"], 11 + CH, "as_hrs")

            pool.wait_ge(*done["as_done"])
            pool.wait_ge(s["out_state"], 48)

            def queries(u):
                i, h = divmod(u, H)
                if u >= 3:
                    pool.wait_ge(s["sc1"], u - 2)
                for m in range(2):
                    nc.gpsimd.tensor_scalar(qz[:, u % 3, m, :], U[:, QA + h, i * P:(i + 1) * P],
                                            map_scale[:, m:m + 1], 0.0, ALU.mult, ALU.add).then_inc(s["qz_ready"], 1)

            queries(0)
            queries(1)
            queries(2)
            for u in range(CH * H):
                if u + 3 < CH * H:
                    queries(u + 3)
                root(st[:, u % 2, 4:5], st[:, u % 2, 5:6], (s["psq"], u + 1), 12 + CH + u, "prs")

            means = 11 + CH + CH * H

            def roots(j):
                n = XT[j][1]
                root(sumsq[0:n, j:j + 1], rstd[0:n, j:j + 1], (s["y_sq"], j + 1), means + max(2 * j, 1), "y_rs")

            roots(0)
            for j, (t0, n) in enumerate(XT):
                if j < 8:
                    roots(j + 1)
                root(st[0:n, 0, 6:7], st[0:n, 0, 7:8], (s["t_sq"], j + 1),
                     means + min(2 * j + 3, 18), "t_rs")

        @block.scalar
        def _(act):
            def store_hi(t):
                t0, n = XT[t]
                act.wait_ge(s["hT_ready"], t + 1)
                for b in range(2):
                    last = nc.scalar.activation(hhi[:, 4 * b:4 * b + 4, t0:t0 + n],
                                                ps[:, 2 * (t % 2) + b, :].rearrange("p (k t) -> p k t", k=4)[:, :, 0:n],
                                                ACT.Copy)
                last.then_inc(s["hhi_ready"], 1)

            for t, (t0, n) in enumerate(XT):
                act.wait_ge(x_in[t % 2], 16 * (t // 2 + 1))
                if t >= 1:
                    act.wait_ge(s["sumsq_ready"], t)
                nc.scalar.activation(square[0:n, :], xrow[0:n, t % 2, :], ACT.Square, scale=D ** -0.5,
                                     accum_out=sumsq[0:n, t:t + 1]).then_inc(s["sumsq_ready"], 1)
                if t >= 1:
                    store_hi(t - 1)
            store_hi(8)
            act.wait_ge(s["lam_sum"], 2)
            nc.scalar.activation(lam_e, lam_e, ACT.Exp).then_inc(*signal["lam_exp"])
            act.wait_ge(*done["vecT_ready"])
            nc.scalar.activation(vec, ps[:, 4, 0:32], ACT.Copy).then_inc(*signal["vec_ready"])

            def split(q, half, slot, arrived, wait=True):
                act.wait_ge(w_in[slot], arrived)
                if wait:
                    act.wait_ge(s["w_used"], q - 1)
                nc.scalar.activation(whi[:, half, :, :], wst[:, slot, :, :], ACT.Copy).then_inc(s["whi_ready"], 1)

            def store(n, tile, bank, fn):
                act.wait_ge(s["w_used"], 2 * n + 2)
                nc.scalar.activation(U[:, bass.ds(tile, 1), :].rearrange("p a (c t) -> p (a c) t", c=3),
                                     ps[:, bank:bank + 3, 0:THIRD], fn).then_inc(s["u_stored"], 1)

            for m in range(2):
                split(0, m, m, 16, False)
            act.wait_ge(*done["lam_ready"])
            n = 0
            for first, count, fn in SECTIONS:
                last_section = n + count == NT
                with act.Fori(n // 2, (n + count) // 2 - last_section) as pair:
                    b = pair * 2
                    split(2 * b + 2, 0, 2, pair * 16 + 16)
                    split(2 * b + 3, 1, 3, pair * 16 + 16)
                    store(b, b + (first - n), 0, fn)
                    split(2 * b + 4, 0, 0, pair * 16 + 32)
                    split(2 * b + 5, 1, 1, pair * 16 + 32)
                    store(b + 1, b + (1 + first - n), 3, fn)
                n += count
                if last_section:
                    split(2 * NT - 2, 0, 2, NT // 2 * 16)
                    split(2 * NT - 1, 1, 3, NT // 2 * 16)
                    store(NT - 2, first + count - 2, 0, fn)
                    store(NT - 1, first + count - 1, 3, fn)

            def copy(out, in_, name, fn=ACT.Copy, **more):
                nc.scalar.activation(out, in_, fn, **more).then_inc(*(s[name], 1) if name in s else signal[name])

            act.wait_ge(*done["hist_ready"])
            copy(xpad[:, :, :, 0:3], ps[:, 0, 0:96].rearrange("p (h b j) -> p h b j", h=H, b=NSEQ), "hist_stored")
            act.wait_ge(*done["krow_ready"])
            copy(kS[:, :], ps[0:SMP, 1, :], "krow_stored")
            act.wait_ge(*done["vrow_ready"])
            copy(vS[:, :], ps[0:SMP, 2, :], "vrow_stored")
            act.wait_ge(*done["xbrow_ready"])
            copy(xbS[:, :], ps[0:SMP, 3, :], "xbrow_stored")
            act.wait_ge(*done["last3_ready"])
            copy(xbP[:, :], ps[0:3, 4, :], "last3_stored")
            act.wait_ge(*done["nT_ready"])
            act.wait_ge(s["cs_in"], 32)
            copy(Cs[:, :, DH], ps[:, 5, 0:SMP], "n_stored")
            for h in range(H):
                act.wait_ge(s["conv_step"], CONV_STEPS)
                copy(xch[:, h, :], xch[:, h, :], "silu_ready", ACT.Silu)
            nc.scalar.preload_act_table_set("natural_log_exp_and_others")
            act.wait_ge(s["s_proj"], 1)
            copy(qbT[:, :, 0:SMP], ps[:, 6, 0:P].rearrange("p (h t) -> p h t", h=H), "s_qk_stored")
            act.wait_ge(s["s_proj"], 2)
            copy(kbT[:, :, 0:SMP], ps[:, 7, 0:P].rearrange("p (h t) -> p h t", h=H), "s_qk_stored", scale=KSCALE)
            act.wait_ge(s["s_kvtok"], 2)
            act.wait_ge(s["zero_ready"], 4 + 6 + 10)
            copy(vaug[0:SMP, :, 0:DH], ps[0:SMP, 3, :].rearrange("p (h d) -> p h d", h=H), "s_vaug")
            act.wait_ge(s["s_gate_step"], 7)
            copy(gs[:, 2, :], gs[:, 1, :], "s_gate_exp", ACT.Exp, scale=-1.0)
            act.wait_ge(s["s_gate_exp"], 1)
            copy(gs[:, 3, :], gs[:, 2, :], "s_gate_exp", ACT.Ln, bias=1.0)
            act.wait_ge(s["s_gate_step"], 15)
            copy(G[32:36, 0:SMP], gs[:, 4, :], "s_rows", ACT.Exp)
            copy(G[64:68, 0:SMP], gs[:, 5, :], "s_rows", ACT.Exp)
            copy(G[96:100, 0:SMP].rearrange("p (b t) -> p b t", t=STEPS), g5[:, 4, :, 1:5], "s_rows", ACT.Exp, scale=-1.0)
            act.wait_ge(*done["s_GT"])
            copy(GT[0:SMP, :], ps[0:SMP, 5, 0:P], "s_GT_stored")
            copy(decS[:, :, :].rearrange("p h b -> p (h b)"), ps[:, 5, P:P + SMP], "s_GT_stored", ACT.Exp)
            act.wait_ge(*done["s_arg"])
            copy(E[0:SMP, :, 0:SMP], E[0:SMP, :, 0:SMP], "s_E", ACT.Exp)
            act.wait_ge(*done["s_inter"])
            act.wait_ge(s["s_GT_stored"], 1)
            for h in range(H):
                last = nc.scalar.activation(nd[0:SMP, h, :], ps[0:SMP, (7, 0)[h // 2], 129 * (h % 2):129 * (h % 2) + 129],
                                            ACT.Copy, scale=GT[0:SMP, 32 + h:33 + h])
            last.then_inc(*signal["s_nd_scaled"])
            act.wait_ge(*done["s_nrow"])
            copy(nout[:, :], ps[0:SMP, 5, 0:DH], "s_nout")
            act.wait_ge(s["s_h_gated"], 5)
            for h in range(H):
                last = nc.scalar.activation(E[0:SMP, h, :], nd[0:SMP, h, 0:DH], ACT.Square, scale=DH ** -0.5,
                                            accum_out=ss4[0:SMP, h:h + 1])
            last.then_inc(*signal["s_sq"])

            act.wait_ge(*done["s_bo"])

            def stream_act(i, first, last):
                G0 = i * GROUPS
                if not first:
                    for u in (0, 2, 4):
                        act.wait_ge(s["pT_ready"], (i - 1) * 5 + (u + 1))
                        if u < 4:
                            copy(pT[:, 4 * u:4 * u + 4, :].rearrange("p k (h r) -> p k h r", h=H),
                                 ps[:, 0, :].rearrange("p (k h r) -> p k h r", k=4, h=H)[:, :, :, 0:8], "pT_act")
                        else:
                            copy(pT[0:SMP, 16, :].rearrange("p (h r) -> p h r", h=H),
                                 ps[0:SMP, 0, 0:P].rearrange("p (h r) -> p h r", h=H)[:, :, 0:8], "pT_act")

                def keys(g):
                    if last:
                        return
                    act.wait_ge(s["k_used"], G0 + (g + 1))
                    if g >= 2:
                        act.wait_ge(s["scores_ready"], i * 9 + (g - 1))
                    elif not first:
                        act.wait_ge(s["scores_ready"], i * 9 - (2 - g))
                    copy(kTs[:, g % 2, 0:2, :], ps[:, 0, :].rearrange("p (h k) -> p h k", h=2), "kT_act")

                if not last:
                    act.wait_ge(s["proj_ready"], 3 * i + 1)
                    copy(qbT[:, :, :], ps[:, 4, :].rearrange("p (h t) -> p h t", h=H), "qk_stored")
                    act.wait_ge(s["proj_ready"], 3 * i + 2)
                    if not first:
                        act.wait_ge(s["obT_ready"], i)
                    copy(kbT[:, :, :], ps[:, 5, :].rearrange("p (h t) -> p h t", h=H), "qk_stored", scale=KSCALE)
                keys(0)
                keys(1)
                if not last:
                    act.wait_ge(s["kvtok_ready"], i + 1)
                    if not first:
                        act.wait_ge(s["cu_ready"], i)
                    copy(vaug[:, :, 0:DH], ps[:, 5, :].rearrange("p (h d) -> p h d", h=H), "vaug_stored")
                    act.wait_ge(s["gate_step"], i * 12 + 3)
                    copy(gat[:, 2, :], gat[:, 1, :], "gate_exp", ACT.Exp, scale=-1.0)
                    act.wait_ge(s["gate_exp"], 2 * i + 1)
                    copy(gat[:, 3, :], gat[:, 2, :], "gate_exp", ACT.Ln, bias=1.0)
                keys(2)
                if not last:
                    act.wait_ge(s["gate_step"], i * 12 + 12)
                    copy(G[32:36, :], gat[:, 6, :], "rows_exp", ACT.Exp, bias=mcol[:, bass.ds(i, 1)])
                    copy(G[64:68, :], gat[:, 7, :], "rows_exp", ACT.Exp, bias=aL)
                    copy(G[96:100, :], gat[:, 4, :], "rows_exp", ACT.Exp, scale=-1.0)
                keys(3)
                if not last:
                    act.wait_ge(s["GT_ready"], i + 1)
                    copy(GT[:, :], ps[:, 7, 0:P], "gt_stored")
                    copy(dec4, ps[:, 7, P:P + H], "gt_stored", ACT.Exp)
                keys(4)
                if not last:
                    act.wait_ge(s["arg_ready"], i + 1)
                    copy(E[:, :, :], E[:, :, :], "E_ready", ACT.Exp)
                keys(5)
                if not last:
                    act.wait_ge(s["inter_ready"], i + 1)
                    if not first:
                        act.wait_ge(s["bo_done"], i)
                    for h in range(H):
                        lastop = nc.scalar.activation(nd[:, h, :], ps[:, 4 + h // 2, 129 * (h % 2):129 * (h % 2) + 129],
                                                      ACT.Copy, scale=GT[:, 32 + h:33 + h])
                    lastop.then_inc(s["nd_scaled"], 1)
                keys(6)
                keys(7)
                if not last:
                    act.wait_ge(s["h_gated"], i * 5 + 5)
                    for h in range(H):
                        lastop = nc.scalar.activation(E[:, h, :], nd[:, h, 0:DH], ACT.Square, scale=DH ** -0.5, accum_out=ss4[:, h:h + 1])
                    lastop.then_inc(s["sq_ready"], 1)
                if not first:
                    act.wait_ge(s["o_ready"], i)
                    act.wait_ge(s["coef_ready"], i)
                    if not (isinstance(i, int) and i == 1):
                        act.wait_ge(s["comb_ready"], i - 1)
                    copy(AO[:, :], ps[:, 3, 0:DH], "ao_ready", scale=coef[:, bass.ds(i - 1, 1)])
                if not last:
                    act.wait_ge(s["negmax_ready"], i + 1)
                    nc.scalar.activation(S[:, :], S[:, :], ACT.Exp, bias=negmax_s, accum_out=den_s[:, bass.ds(i, 1)]
                                         ).then_inc(s["p_ready"], 1)

            stream_act(0, True, False)
            stream_act(1, False, False)
            with act.Fori(2, NSEQ) as i:
                stream_act(i, False, False)
            stream_act(NSEQ, False, True)

            act.wait_ge(*done["as_T_ready"])
            nc.scalar.activation(GT[:, :], ps[:, 4, 0:P], ACT.Square, scale=DH ** -0.5, accum_out=ss4[:, 0:1]).then_inc(*signal["as_norm"])
            act.wait_ge(*done["as_hrs"])
            copy(AO[:, :], ps[:, 4, 0:P], "as_n2", scale=rs4[:, 0:1])

            act.wait_ge(*done["as_done"])
            for t in range(CH):
                act.wait_ge(s["kt_ready"], t + 1)
                if t >= 2:
                    act.wait_ge(k_out[t % 2], 16 * (t // 2))
                copy(ktok[:, t % 2, :], ps[:, 2 * (t % 2), :], "kt_stored")

            def head_exp(u):
                i, h = divmod(u, H)
                n = (i + 1) * P
                for m in range(2):
                    act.wait_ge(s["rmax"], 2 * u + m + 1)
                    if u >= 2:
                        act.wait_ge(s["wT_ready"], WT_BEFORE[u - 1])
                    nc.scalar.activation(pp[:, u % 2, m, 0:n], score_row(u, m)[:, 0:n],
                                         ACT.Exp, bias=st[:, u % 2, m:m + 1], accum_out=st[:, u % 2, 2 + m:3 + m]
                                         ).then_inc(s["pexp"], 1)

            def weights_out(u):
                i, h = divmod(u, H)
                for c in range(0, i + 1, 4):
                    k = min(4, i + 1 - c)
                    act.wait_ge(s["wT_ready"], WT_BEFORE[u] + c // 4 + 1)
                    if u >= 1:
                        act.wait_ge(s["pv_ready"], u)
                    copy(wT[:, c:c + k, :], ps[:, 4 + (c // 4), 0:k * P].rearrange("p (k q) -> p k q", k=k), "wT_stored")

            def head_out(u):
                act.wait_ge(s["pv_ready"], u + 1)
                if u >= 2:
                    act.wait_ge(s["onT_ready"], u - 1)
                head = ps[:, head_bank(u), 0:DH]
                nc.scalar.activation(on[:, u % 2, :], head, ACT.Square, scale=DH ** -0.5, accum_out=st[:, u % 2, 4:5]
                                     ).then_inc(s["psq"], 1)
                act.wait_ge(s["prs"], u + 1)
                copy(on[:, u % 2, :], head, "on_ready", scale=st[:, u % 2, 5:6])

            head_exp(0)
            for u in range(CH * H):
                if u + 1 < NARROW:
                    head_exp(u + 1)
                weights_out(u)
                if NARROW <= u + 1 < CH * H:
                    head_exp(u + 1)
                head_out(u)

            def y_square(j):
                n = XT[j][1]
                act.wait_ge(s["y_ready"], j + 1)
                if j >= 2:
                    act.wait_ge(s["t_sq"], j - 1)
                nc.scalar.activation(sqt[0:n, :], ps[0:n, 0:2, :].rearrange("p a b -> p (a b)"), ACT.Square, scale=D ** -0.5,
                                     accum_out=sumsq[0:n, j:j + 1]).then_inc(s["y_sq"], 1)

            def p_store(j):
                n = XT[j][1]
                act.wait_ge(s["prow_T"], j + 1)
                copy(pTt[:, :, 0:n], ps[:, 6, 0:2 * P].rearrange("p (k t) -> p k t", k=2)[:, :, 0:n], "prow_stored")
                act.wait_ge(s["pw_ready"], j + 1)
                if j >= 1:
                    act.wait_ge(s["t_done"], j)
                copy(pws[0:n, :], ps[0:n, 6:8, :].rearrange("p a b -> p (a b)"), "pw_stored")
                act.wait_ge(s["x1T_ready"], j + 1)
                for b in range(2):
                    last = nc.scalar.activation(x1T[:, 4 * b:4 * b + 4, 0:n],
                                                ps[:, 2 + b, :].rearrange("p (k t) -> p k t", k=4)[:, :, 0:n], ACT.Copy)
                last.then_inc(s["x1T_stored"], 1)

            def gate_out(j):
                n = XT[j][1]
                act.wait_ge(s["gate_ready"], j + 1)
                if j >= 1:
                    act.wait_ge(s["out_ready"], j)
                copy(sg[0:n, :], ps[0:n, 4:6, :].rearrange("p a b -> p (a b)"), "gate_sig", ACT.Sigmoid)
                act.wait_ge(s["t_done"], j + 1)
                act.wait_ge(s["y_sq"], min(j + 2, 9))
                nc.scalar.activation(sqt[0:n, :], sg[0:n, :], ACT.Square, scale=D ** -0.5, accum_out=st[0:n, 0, 6:7]).then_inc(s["t_sq"], 1)

            y_square(0)
            p_store(0)
            for j in range(9):
                if j + 1 < 9:
                    y_square(j + 1)
                gate_out(j)
                if j + 1 < 9:
                    p_store(j + 1)

        @block.vector
        def _(dve):
            dve.wait_ge(s["gpre_in"], 16)

            def store_lo(t):
                t0, n = XT[t]
                dve.wait_ge(s["hhi_ready"], t + 1)
                for b in range(2):
                    last = nc.vector.tensor_tensor(hlo[:, 4 * b:4 * b + 4, t0:t0 + n],
                                                   ps[:, 2 * (t % 2) + b, :].rearrange("p (k t) -> p k t", k=4)[:, :, 0:n],
                                                   hhi[:, 4 * b:4 * b + 4, t0:t0 + n].bitcast(F32), ALU.subtract)
                last.then_inc(s["hlo_ready"], 1)

            for t, (t0, n) in enumerate(XT):
                dve.wait_ge(s["rstd_ready"], t + 1)
                if t >= 2:
                    dve.wait_ge(s["hT_ready"], t - 1)
                nc.vector.scalar_tensor_tensor(out=hrow[0:n, t % 2, :], in0=xrow[0:n, t % 2, :],
                                               scalar=rstd[0:n, t:t + 1], in1=gpre[0:n, :],
                                               op0=ALU.mult, op1=ALU.mult).then_inc(s["h_ready"], 1)
                if t >= 1:
                    store_lo(t - 1)
            store_lo(8)

            dve.wait_ge(s["params_in"], 16 * PARAMS)
            for n in range(2):
                nc.vector.tensor_tensor_reduce(lamp[:, 64 * n:64 * n + 64], lamv[:, 128 * n:128 * n + 64],
                                               lamv[:, 128 * n + 64:128 * n + 128], 1.0, 0.0, ALU.mult, ALU.add,
                                               lam_e[:, n:n + 1]).then_inc(s["lam_sum"], 1)
            dve.wait_ge(s["iota_ready"], 2)
            nc.vector.tensor_scalar(iot[:, 1:2], iot[:, 0:1], 3, None, ALU.bitwise_and).then_inc(s["lam_sum"], 1)
            nc.vector.tensor_scalar(iot[:, 2:3], iot[:, 0:1], 4, None, ALU.bitwise_and).then_inc(s["lam_sum"], 1)
            dve.wait_ge(s["lam_sum"], 4)
            nc.vector.tensor_copy(iof[:, 0:8], iot[:, 0:8]).then_inc(s["lam_sum"], 1)
            dve.wait_ge(*done["lam_exp"])
            nc.vector.tensor_scalar(lam, lam_e[:, 0:1], lam_e[:, 1:2], LAM_INIT, ALU.subtract, ALU.add
                                    ).then_inc(s["lam_sum"], 1)
            dve.wait_ge(s["lam_sum"], 6)
            nc.vector.tensor_scalar(neg_lam, lam, -1.0, None, ALU.mult).then_inc(s["lam_sum"], 1)
            nc.vector.tensor_scalar(row_4, lam, 1.0, -0.25, ALU.add, ALU.mult).then_inc(s["lam_sum"], 1)
            dve.wait_ge(s["lam_sum"], 8)
            nc.vector.tensor_scalar(sign, iof[:, 2:3], row_4, 1.0, ALU.mult, ALU.add).then_inc(s["lam_sum"], 1)
            dve.wait_ge(s["masks_ready"], 7)
            nc.vector.tensor_scalar(mask_new[:, 28:32], iof[:, 4:8], iof[:, 1:2], NEG, ALU.is_gt, ALU.mult
                                    ).then_inc(*signal["lam_ready"])
            dve.wait_ge(*done["vec_ready"])
            nc.vector.tensor_scalar(ag, attn_g, 1.0 - LAM_INIT, None, ALU.mult).then_inc(s["ag_ready"], 1)
            nc.vector.memset(mcol[:, 0:1], 0.0).then_inc(s["ag_ready"], 1)

            def rest(q, half, slot):
                dve.wait_ge(s["whi_ready"], q + 1)
                nc.vector.tensor_tensor(wlo[:, half, :, :], wst[:, slot, :, :], whi[:, half, :, :].bitcast(F32),
                                        ALU.subtract).then_inc(s["wlo_ready"], 1)

            with dve.Fori(0, NT // 2) as pair:
                for n in range(4):
                    rest(pair * 4 + n, n % 2, n)

            dve.wait_ge(s["w_used"], 2 * NT)
            dve.wait_ge(s["u_stored"], NT)
            nc.vector.tensor_copy(xpad[:, :, :, 3:7], U[:, XB:XB + H, SEQ:TOK].rearrange("p h (b t) -> p h b t", t=STEPS)
                                  ).then_inc(*signal["xpad_new"])
            steps = 0
            for j in (3, 2, 1, 0):
                for h in range(H):
                    w, back = conv_w[:, 4 * j + h:4 * j + h + 1], 3 - j
                    if j == 3:
                        nc.vector.tensor_scalar(xch[:, h, 0:SEQ], U[:, XB + h, 0:SEQ], w, conv_b[:, h:h + 1],
                                                ALU.mult, ALU.add).then_inc(s["conv_step"], 1)
                    else:
                        dve.wait_ge(s["conv_step"], steps - 3)
                        nc.vector.scalar_tensor_tensor(out=xch[:, h, back:SEQ], in0=U[:, XB + h, 0:SEQ - back], scalar=w,
                                                       in1=xch[:, h, back:SEQ], op0=ALU.mult, op1=ALU.add
                                                       ).then_inc(s["conv_step"], 1)
                    steps += 1
            dve.wait_ge(*done["hist_stored"])
            dve.wait_ge(*done["xpad_new"])
            for j in (3, 2, 1, 0):
                for h in range(H):
                    w = conv_w[:, 4 * j + h:4 * j + h + 1]
                    out = xch[:, h, SEQ:TOK].rearrange("p (b t) -> p b t", t=STEPS)
                    if j == 3:
                        nc.vector.tensor_scalar(out, xpad[:, h, :, 3:7], w, conv_b[:, h:h + 1], ALU.mult, ALU.add
                                                ).then_inc(s["conv_step"], 1)
                    else:
                        dve.wait_ge(s["conv_step"], steps - 3)
                        nc.vector.scalar_tensor_tensor(out=out, in0=xpad[:, h, :, j:j + 4], scalar=w, in1=out,
                                                       op0=ALU.mult, op1=ALU.add).then_inc(s["conv_step"], 1)
                    steps += 1

            step = [0]

            def gstep(ins):
                step[0] += 1
                ins.then_inc(s["s_gate_step"], 1)

            def gwait(n):
                dve.wait_ge(s["s_gate_step"], n)

            gstep(nc.vector.memset(g5[:, 0, :, :], 0.0))
            gstep(nc.vector.memset(g5[:, 3, :, :], NEG))
            gstep(nc.vector.memset(g5[:, 2, :, :], 1.0))
            gwait(3)
            gstep(nc.vector.memset(g5[:, 2, :, 0:1], 0.0))
            dve.wait_ge(s["s_proj"], 3)
            nc.vector.tensor_copy(vbT[:, :, 0:SMP], ps[:, 0, 0:P].rearrange("p (h t) -> p h t", h=H)).then_inc(*signal["s_v_stored"])
            dve.wait_ge(*done["s_gates"])
            by_seq = lambda ap: ap.rearrange("p (b t) -> p b t", t=STEPS)
            gstep(nc.vector.tensor_scalar(g5[:, 1, :, 1:5], by_seq(ps[0:H, 1, 0:SMP]), bias_i, None, ALU.add))
            gstep(nc.vector.tensor_scalar(gs[:, 0, :], ps[32:32 + H, 1, 0:SMP], bias_f, None, ALU.add))
            gwait(6)
            gstep(nc.vector.scalar_tensor_tensor(out=gs[:, 1, :], in0=gs[:, 0, :], scalar=-1.0, in1=gs[:, 0, :],
                                                 op0=ALU.mult, op1=ALU.max))
            dve.wait_ge(s["s_gate_exp"], 2)
            gstep(nc.vector.scalar_tensor_tensor(out=g5[:, 3, :, 1:5], in0=by_seq(gs[:, 0, :]), scalar=0.0,
                                                 in1=by_seq(gs[:, 3, :]), op0=ALU.min, op1=ALU.subtract))
            gwait(8)
            gstep(nc.vector.tensor_copy(g5[:, 0, :, 1:5], g5[:, 3, :, 1:5]))
            gwait(9)
            dve.wait_ge(s["cs_in"], 32)
            flat = lambda r: g5[:, r, :, :].rearrange("p b t -> p (b t)")
            gstep(nc.vector.tensor_tensor_scan(flat(5), flat(2), flat(0), 0.0, ALU.mult, ALU.add))
            gstep(nc.vector.tensor_tensor_scan(flat(4), flat(3), flat(1), 0.0, ALU.add, ALU.max))
            gwait(11)
            gstep(nc.vector.tensor_tensor(flat(6), flat(5), flat(4), ALU.subtract))
            gstep(nc.vector.tensor_tensor(flat(7), flat(1), flat(5), ALU.subtract))
            gwait(13)
            gstep(nc.vector.tensor_tensor(by_seq(gs[:, 4, :]), g5[:, 6, :, 1:5], g5[:, 1, :, 0:1].broadcast_to([H, NSEQ, STEPS]),
                                          ALU.add))
            gstep(nc.vector.tensor_tensor(by_seq(gs[:, 5, :]), g5[:, 7, :, 1:5], g5[:, 6, :, 4:5].broadcast_to([H, NSEQ, STEPS]),
                                          ALU.add))
            dve.wait_ge(s["zero_ready"], 4 + 6 + 10)
            gstep(nc.vector.tensor_copy(by_seq(G[0:H, 0:SMP]), g5[:, 7, :, 1:5]))
            gstep(nc.vector.tensor_copy(by_seq(gs[:, 0, :]), g5[:, 6, :, 1:5]))
            gwait(17)
            gstep(nc.vector.tensor_tensor(AblkS[0:H, :, :], lead(gs[:, 0, :], H), bc(ident[0:H, 0:H], SMP), ALU.mult))
            gstep(nc.vector.tensor_tensor(DgS[0:H, :, :], lead(by_seq(gs[:, 4, :])[:, :, 3], H), bc(ident[0:H, 0:H], NSEQ),
                                          ALU.mult))
            dve.wait_ge(s["s_kvtok"], 2)
            dve.wait_ge(s["s_GT_stored"], 2)
            nc.vector.tensor_tensor(kw[0:SMP, :, :], ps[0:SMP, 2, :].rearrange("p (h d) -> p h d", h=H),
                                    bc(GT[0:SMP, 64:68], DH), ALU.mult).then_inc(*signal["s_kw"])
            dve.wait_ge(*done["s_AB"])
            for h in range(H):
                last = nc.vector.scalar_tensor_tensor(out=E[0:SMP, h, 0:SMP], in0=ps[0:SMP, 6, h * SMP:(h + 1) * SMP],
                                                      scalar=GT[0:SMP, h:h + 1], in1=mask_s[:, :], op0=ALU.add, op1=ALU.add)
            last.then_inc(*signal["s_arg"])
            dve.wait_ge(*done["s_E"])
            dve.wait_ge(*done["s_sqk"])
            nc.vector.tensor_tensor(E[0:SMP, :, 0:SMP], ps[0:SMP, 4, 0:P].rearrange("p (h t) -> p h t", h=H),
                                    E[0:SMP, :, 0:SMP], ALU.mult).then_inc(*signal["s_W"])
            dve.wait_ge(*done["s_kw"])

            def own_keys(b):
                nc.vector.tensor_scalar(kwm[:, b % 2, :, :], kw[0:SMP, :, :], seqmask[:, b:b + 1], None, ALU.mult
                                        ).then_inc(s["s_kwm"], 1)

            own_keys(0)
            own_keys(1)
            dve.wait_ge(*done["s_intra"])
            dve.wait_ge(*done["s_nd_scaled"])
            for n, bank in enumerate((3, 5)):
                half = nd[0:SMP, 2 * n:2 * n + 2, :].rearrange("p h d -> p (h d)")
                last = nc.vector.tensor_tensor(half, half, ps[0:SMP, bank, 0:258], ALU.add)
            last.then_inc(*signal["s_nd"])
            for b in range(NSEQ):
                dve.wait_ge(s["s_cu"], b + 1)
                for h in range(H):
                    bank = ((1, 2), (4, 6))[b % 2][h // 2]
                    c = Cs[:, H * b + h, :]
                    last = nc.vector.scalar_tensor_tensor(out=c, in0=c, scalar=decS[:, h, b:b + 1],
                                                          in1=ps[:, bank, 129 * (h % 2):129 * (h % 2) + 129],
                                                          op0=ALU.mult, op1=ALU.add)
                last.then_inc(s["s_C"], 1)
                if b + 2 < NSEQ:
                    own_keys(b + 2)

            def divide(n, step, base, nd_sem, nd_count, ob_sem, ob_count, bank):
                dve.wait_ge(nd_sem, nd_count)
                nc.vector.scalar_tensor_tensor(out=rd4[0:n, :], in0=nd[0:n, :, DH], scalar=-1.0, in1=GT[0:n, 96:100],
                                               op0=ALU.mult, op1=ALU.max).then_inc(step, 1)
                dve.wait_ge(step, base + 1)
                nc.vector.tensor_tensor(rd4[0:n, :], rd4[0:n, :], nd[0:n, :, DH], ALU.max).then_inc(step, 1)
                dve.wait_ge(step, base + 2)
                nc.vector.reciprocal(rd4[0:n, :], rd4[0:n, :]).then_inc(step, 1)
                dve.wait_ge(step, base + 3)
                nc.vector.tensor_tensor(nd[0:n, :, 0:DH], nd[0:n, :, 0:DH], bc(rd4[0:n, :], DH), ALU.mult).then_inc(step, 1)
                dve.wait_ge(step, base + 4)
                dve.wait_ge(ob_sem, ob_count)
                nc.vector.tensor_tensor(nd[0:n, :, 0:DH], nd[0:n, :, 0:DH],
                                        ps[0:n, bank, :].rearrange("p (h d) -> p h d", h=H), ALU.mult).then_inc(step, 1)

            divide(SMP, s["s_h_gated"], 0, *done["s_nd"], *done["s_obT"], 7)
            dve.wait_ge(s["s_proj"], 2)
            for h in range(H):
                nc.vector.tensor_scalar(xch[:, h, SEQ:TOK], xch[:, h, SEQ:TOK], skip[:, h:h + 1], None, ALU.mult
                                        ).then_inc(s["s_bo_t"], 1)
            dve.wait_ge(*done["s_rs"])
            nc.vector.tensor_tensor(nd[0:SMP, :, 0:DH], nd[0:SMP, :, 0:DH], bc(rs4[0:SMP, :], DH), ALU.mult
                                    ).then_inc(*signal["s_hn"])
            dve.wait_ge(*done["s_hT"])
            dve.wait_ge(s["s_bo_t"], H)
            for h in range(H):
                nc.vector.scalar_tensor_tensor(out=AO[:, h * SMP:(h + 1) * SMP], in0=ps[:, 0, h * SMP:(h + 1) * SMP],
                                               scalar=mlstm_g[:, h:h + 1], in1=xch[:, h, SEQ:TOK],
                                               op0=ALU.mult, op1=ALU.add).then_inc(s["s_bo_t"], 1)
            dve.wait_ge(s["s_bo_t"], 2 * H)
            nc.vector.tensor_tensor(U[:, ZB:ZB + H, SEQ:TOK], U[:, ZB:ZB + H, SEQ:TOK],
                                    AO[:, :].rearrange("p (h t) -> p h t", h=H), ALU.mult).then_inc(*signal["s_bo"])

            nc.vector.memset(ps[:, 3, 0:DH], 0.0).then_inc(*signal["den_step"])

            def stream_dve(i, first, last):
                G0, t0 = i * GROUPS, i * P
                if not first:
                    for u in (1, 3):
                        dve.wait_ge(s["pT_ready"], (i - 1) * 5 + (u + 1))
                        nc.vector.tensor_copy(pT[:, 4 * u:4 * u + 4, :].rearrange("p k (h r) -> p k h r", h=H),
                                              ps[:, 1, :].rearrange("p (k h r) -> p k h r", k=4, h=H)[:, :, :, 0:8]
                                              ).then_inc(s["pT_dve"], 1)

                def keys(g):
                    if last:
                        return
                    dve.wait_ge(s["k_used"], G0 + (g + 1))
                    if g >= 2:
                        dve.wait_ge(s["scores_ready"], i * 9 + (g - 1))
                    elif not first:
                        dve.wait_ge(s["scores_ready"], i * 9 - (2 - g))
                    nc.vector.tensor_copy(kTs[:, g % 2, 2:4, :], ps[:, 1, :].rearrange("p (h k) -> p h k", h=2)
                                          ).then_inc(s["kT_dve"], 1)

                def scores(g):
                    if last:
                        return
                    dve.wait_ge(s["scores_ready"], i * 9 + (g + 1))
                    k = GP * PAGE
                    nc.vector.tensor_scalar(S[:, g * k:(g + 1) * k], ps[:, 2, 0:k], 1.0, LOWEST, ALU.mult, ALU.max,
                                            accum_out=gmax[:, g:g + 1]).then_inc(s["s_stored"], 1)

                if not last:
                    dve.wait_ge(s["proj_ready"], 3 * i + 3)
                    nc.vector.tensor_copy(vbT[:, :, :], ps[:, 6, :].rearrange("p (h t) -> p h t", h=H)
                                          ).then_inc(s["v_stored"], 1)
                keys(0)
                keys(1)
                scores(0)
                gs0 = i * 12
                if not last:
                    dve.wait_ge(s["gates_ready"], i + 1)
                    nc.vector.tensor_scalar(gat[:, 7, :], ps[0:H, 7, 0:P], bias_i, None, ALU.add).then_inc(s["gate_step"], 1)
                    nc.vector.tensor_scalar(gat[:, 0, :], ps[32:32 + H, 7, 0:P], bias_f, None, ALU.add
                                            ).then_inc(s["gate_step"], 1)
                    dve.wait_ge(s["gate_step"], gs0 + 2)
                    nc.vector.scalar_tensor_tensor(out=gat[:, 1, :], in0=gat[:, 0, :], scalar=-1.0, in1=gat[:, 0, :],
                                                   op0=ALU.mult, op1=ALU.max).then_inc(s["gate_step"], 1)
                keys(2)
                scores(1)
                if not last:
                    dve.wait_ge(s["gate_exp"], 2 * i + 2)
                    nc.vector.scalar_tensor_tensor(out=gat[:, 1, :], in0=gat[:, 0, :], scalar=0.0, in1=gat[:, 3, :],
                                                   op0=ALU.min, op1=ALU.subtract).then_inc(s["gate_step"], 1)
                    dve.wait_ge(s["gate_step"], gs0 + 4)
                    nc.vector.tensor_tensor_scan(gat[:, 5, :], ones[0:H, :], gat[:, 1, :], 0.0, ALU.mult, ALU.add
                                                 ).then_inc(s["gate_step"], 1)
                    nc.vector.tensor_tensor_scan(gat[:, 4, :], gat[:, 1, :], gat[:, 7, :], mcol[:, bass.ds(i, 1)],
                                                 ALU.add, ALU.max).then_inc(s["gate_step"], 1)
                    dve.wait_ge(s["gate_step"], gs0 + 6)
                    nc.vector.tensor_tensor(gat[:, 6, :], gat[:, 5, :], gat[:, 4, :], ALU.subtract).then_inc(s["gate_step"], 1)
                    nc.vector.tensor_tensor(gat[:, 7, :], gat[:, 7, :], gat[:, 5, :], ALU.subtract).then_inc(s["gate_step"], 1)
                    nc.vector.tensor_copy(mcol[:, bass.ds(i + 1, 1)], gat[:, 4, P - 1:P]).then_inc(s["gate_step"], 1)
                    dve.wait_ge(s["gate_step"], gs0 + 9)
                    if not first:
                        dve.wait_ge(s["AB_ready"], i)
                    nc.vector.tensor_tensor(Ablk[0:H, :, :], lead(gat[:, 6, :], H), bc(ident[0:H, 0:H], P), ALU.mult
                                            ).then_inc(s["gate_step"], 1)
                    nc.vector.tensor_copy(G[0:H, :], gat[:, 7, :]).then_inc(s["gate_step"], 1)
                    nc.vector.tensor_copy(aL, gat[:, 6, P - 1:P]).then_inc(s["gate_step"], 1)
                    dve.wait_ge(s["gate_step"], gs0 + 12)
                    nc.vector.tensor_scalar(Dg[0:H, :], ident[0:H, 0:H], aL, None, ALU.mult).then_inc(s["kw_ready"], 1)
                    dve.wait_ge(s["kw_ready"], 3 * i + 1)
                    nc.vector.scalar_tensor_tensor(out=Dg[0:H, :], in0=ident[0:H, 0:H], scalar=mcol[:, bass.ds(i, 1)],
                                                   in1=Dg[0:H, :], op0=ALU.mult, op1=ALU.add).then_inc(s["kw_ready"], 1)
                keys(3)
                scores(2)
                if not last:
                    dve.wait_ge(s["gt_stored"], 2 * i + 2)
                    nc.vector.tensor_tensor(kw[:, :, :], ps[:, 4, :].rearrange("p (h d) -> p h d", h=H), bc(GT[:, 64:68], DH),
                                            ALU.mult).then_inc(s["kw_ready"], 1)
                    dve.wait_ge(s["AB_ready"], i + 1)
                    for h in range(H):
                        lastop = nc.vector.scalar_tensor_tensor(out=E[:, h, :], in0=ps[:, 5, h * P:(h + 1) * P],
                                                                scalar=GT[:, h:h + 1], in1=mask_t[:, :],
                                                                op0=ALU.add, op1=ALU.add)
                    lastop.then_inc(s["arg_ready"], 1)
                keys(4)
                scores(3)
                if not last:
                    dve.wait_ge(s["E_ready"], i + 1)
                    nc.vector.tensor_tensor(E[:, :, :], ps[:, 6, :].rearrange("p (h t) -> p h t", h=H), E[:, :, :], ALU.mult
                                            ).then_inc(s["W_ready"], 1)
                keys(5)
                scores(4)
                if not last:
                    dve.wait_ge(s["intra_ready"], i + 1)
                    dve.wait_ge(s["nd_scaled"], i + 1)
                    for n in range(2):
                        half = nd[:, 2 * n:2 * n + 2, :].rearrange("p h d -> p (h d)")
                        lastop = nc.vector.tensor_tensor(half, half, ps[:, 6 + n, 0:258], ALU.add)
                    lastop.then_inc(s["nd_ready"], 1)
                keys(6)
                scores(5)
                keys(7)
                scores(6)
                if not last:
                    dve.wait_ge(s["cu_ready"], i + 1)
                    for h in range(H):
                        lastop = nc.vector.scalar_tensor_tensor(out=Caug[:, h, :], in0=Caug[:, h, :], scalar=dec4[:, h:h + 1],
                                                                in1=ps[:, 4 + h // 2, 129 * (h % 2):129 * (h % 2) + 129],
                                                                op0=ALU.mult, op1=ALU.add)
                    lastop.then_inc(s["C_done"], 1)
                    divide(P, s["h_gated"], i * 5, s["nd_ready"], i + 1, s["obT_ready"], i + 1, 6)
                    scores(7)
                    dve.wait_ge(s["scores_ready"], i * 9 + 9)
                    nc.vector.tensor_tensor(S[:, PAST:PAST + SMP], ps[:, 2, 0:SMP],
                                            mask_new[:, bass.ds(i * (-STEPS) + 28, SMP)], ALU.add).then_inc(s["s_stored"], 1)
                    dve.wait_ge(s["s_stored"], i * 9 + 9)
                    nc.vector.tensor_reduce(gmax[:, GROUPS:GROUPS + 1], S[:, PAST:PAST + SMP], AX.X, ALU.max
                                            ).then_inc(s["soft_step"], 1)
                    dve.wait_ge(s["soft_step"], 2 * i + 1)
                    nc.vector.tensor_reduce(negmax_s, gmax[:, :], AX.X, ALU.max, negate=True).then_inc(s["negmax_ready"], 1)
                    dve.wait_ge(s["hrs_ready"], i + 1)
                    nc.vector.tensor_tensor(nd[:, :, 0:DH], nd[:, :, 0:DH], bc(rs4, DH), ALU.mult).then_inc(s["hn_ready"], 1)
                    dve.wait_ge(s["p_ready"], i + 1)
                    nc.vector.reciprocal(coef[:, bass.ds(i, 1)], den_s[:, bass.ds(i, 1)]).then_inc(s["soft_step"], 1)
                    dve.wait_ge(s["soft_step"], 2 * i + 2)
                    nc.vector.tensor_scalar(coef[:, bass.ds(i, 1)], coef[:, bass.ds(i, 1)], sign, None, ALU.mult
                                            ).then_inc(s["coef_ready"], 1)
                    dve.wait_ge(s["hTr_ready"], i + 1)
                    dve.wait_ge(s["xsk_ready"], i + 1)
                    for h in range(H):
                        lastop = nc.vector.scalar_tensor_tensor(out=nd[:, h, 0:P], in0=ps[:, 7, h * P:(h + 1) * P],
                                                                scalar=mlstm_g[:, h:h + 1], in1=xch[:, h, bass.ds(t0, P)],
                                                                op0=ALU.mult, op1=ALU.add)
                    lastop.then_inc(s["bo_t"], 1)
                    dve.wait_ge(s["bo_t"], i + 1)
                    z = U[:, ZB:ZB + H, bass.ds(t0, P)]
                    nc.vector.tensor_tensor(z, z, nd[:, :, 0:P], ALU.mult).then_inc(s["bo_done"], 1)
                if not first:
                    dve.wait_ge(s["comb_ready"], i)
                    nc.vector.tensor_tensor(AS[:, :], AS[:, :], ps[:, 2, 0:P], ALU.add).then_inc(s["as_added"], 1)

            stream_dve(0, True, False)
            stream_dve(1, False, False)
            with dve.Fori(2, NSEQ) as i:
                stream_dve(i, False, False)
            stream_dve(NSEQ, False, True)

            dve.wait_ge(*done["as_T2"])
            for h in range(H):
                z = U[:, ZA + h, SEQ:TOK]
                last = nc.vector.scalar_tensor_tensor(out=z, in0=ps[:, 5, h * SMP:(h + 1) * SMP], scalar=ag[:, h:h + 1],
                                                      in1=z, op0=ALU.mult, op1=ALU.mult)
            last.then_inc(*signal["as_done"])

            for t in range(CH):
                dve.wait_ge(s["vt_ready"], t + 1)
                nc.vector.tensor_copy(vtok[:, t, :], ps[:, 2 * (t % 2) + 1, :]).then_inc(s["vt_stored"], 1)

            def head_max(u):
                i, h = divmod(u, H)
                n = (i + 1) * P
                for m in range(2):
                    dve.wait_ge(s[("sc0", "sc1")[m]], u + 1)
                    row = score_row(u, m)
                    nc.vector.tensor_tensor(row[:, n - P:n], row[:, n - P:n], mask_q[:, :], ALU.add).then_inc(s["masked"], 1)
                    dve.wait_ge(s["masked"], 2 * u + m + 1)
                    nc.vector.tensor_reduce(st[:, u % 2, m:m + 1], row[:, 0:n], AX.X, ALU.max, negate=True
                                            ).then_inc(s["rmax"], 1)

            def head_weights(u):
                i, h = divmod(u, H)
                n = (i + 1) * P
                dve.wait_ge(s["pexp"], 2 * u + 2)
                nc.vector.reciprocal(st[:, u % 2, 2:4], st[:, u % 2, 2:4]).then_inc(s["w_step"], 1)
                dve.wait_ge(s["w_step"], 2 * u + 1)
                nc.vector.tensor_scalar(pp[:, u % 2, 1, 0:n], pp[:, u % 2, 1, 0:n], st[:, u % 2, 3:4], neg_lam,
                                        ALU.mult, ALU.mult).then_inc(s["w_step"], 1)
                dve.wait_ge(s["w_step"], 2 * u + 2)
                nc.vector.scalar_tensor_tensor(out=pp[:, u % 2, 0, 0:n], in0=pp[:, u % 2, 0, 0:n], scalar=st[:, u % 2, 2:3],
                                               in1=pp[:, u % 2, 1, 0:n], op0=ALU.mult, op1=ALU.add).then_inc(s["w_done"], 1)

            def head_gate(u):
                i, h = divmod(u, H)
                dve.wait_ge(s["onT_ready"], u + 1)
                z = U[:, ZA + h, i * P:(i + 1) * P]
                nc.vector.scalar_tensor_tensor(out=z, in0=ps[:, 7, 0:P], scalar=ag[:, h:h + 1], in1=z,
                                               op0=ALU.mult, op1=ALU.mult).then_inc(s["a_done"], 1)

            head_max(0)
            for u in range(CH * H):
                if u + 1 < NARROW:
                    head_max(u + 1)
                head_weights(u)
                if NARROW <= u + 1 < CH * H:
                    head_max(u + 1)
                if u >= 1:
                    head_gate(u - 1)
            head_gate(CH * H - 1)

            dve.wait_ge(s["g_in"], 32)

            def y_part(j):
                n = XT[j][1]
                dve.wait_ge(s["y_rs"], j + 1)
                dve.wait_ge(xt_in[j % 2], 16 * (j // 2 + 1))
                if j >= 2:
                    dve.wait_ge(y_out[j % 2], 16 * (j // 2))
                nc.vector.scalar_tensor_tensor(out=x1[0:n, j % 2, :], in0=ps[0:n, 0:2, :].rearrange("p a b -> p (a b)"),
                                               scalar=rstd[0:n, j:j + 1], in1=gpost[0:n, :], op0=ALU.mult, op1=ALU.mult
                                               ).then_inc(s["y_n"], 1)
                dve.wait_ge(s["y_n"], j + 1)
                nc.vector.tensor_tensor(x1[0:n, j % 2, :], x1[0:n, j % 2, :], xin[0:n, j % 2, :], ALU.add
                                        ).then_inc(s["y_x"], 1)

            def gated(j):
                n = XT[j][1]
                dve.wait_ge(s["gate_sig"], j + 1)
                dve.wait_ge(s["pw_stored"], j + 1)
                nc.vector.tensor_tensor(sg[0:n, :], sg[0:n, :], pws[0:n, :], ALU.mult).then_inc(s["t_done"], 1)
                dve.wait_ge(s["t_rs"], j + 1)
                nc.vector.scalar_tensor_tensor(out=sg[0:n, :], in0=sg[0:n, :], scalar=st[0:n, 0, 7:8], in1=gple[0:n, :],
                                               op0=ALU.mult, op1=ALU.mult).then_inc(s["t_n"], 1)
                dve.wait_ge(s["t_n"], j + 1)
                nc.vector.tensor_tensor(x1[0:n, j % 2, :], x1[0:n, j % 2, :], sg[0:n, :], ALU.add).then_inc(s["out_ready"], 1)

            y_part(0)
            for j in range(9):
                if j + 1 < 9:
                    y_part(j + 1)
                gated(j)

        @block.tensor
        def _(pe):
            pe.wait_ge(s["ident_ready"], 1)
            for t, (t0, n) in enumerate(XT):
                pe.wait_ge(s["h_ready"], t + 1)
                if t >= 2:
                    pe.wait_ge(s["hlo_ready"], t - 1)
                for k in range(KC):
                    last = nc.tensor.transpose(ps[:, 2 * (t % 2) + k // 4, (k % 4) * P:(k % 4) * P + n],
                                               hrow[0:n, t % 2, k * P:(k + 1) * P], ident[0:n, 0:n])
                last.then_inc(s["hT_ready"], 1)
            pe.wait_ge(s["params_in"], 16 * PARAMS)
            nc.tensor.transpose(ps[:, 4, 0:32], vrow[0:32, :], ident[0:32, 0:32]).then_inc(*signal["vecT_ready"])
            pe.wait_ge(s["hlo_ready"], 9)
            pe.wait_ge(*done["vec_ready"])

            def multiply(q, half, bank):
                pe.wait_ge(s["wlo_ready"], q + 1)
                for k in range(4):
                    kc = 4 * half + k
                    for w, h in ((whi, hhi), (whi, hlo), (wlo, hhi)):
                        for c in range(3):
                            last = nc.tensor.matmul(ps[:, bank + c, 0:THIRD], w[:, half, k, :],
                                                    h[:, kc, c * THIRD:(c + 1) * THIRD],
                                                    start=(kc == 0 and w is whi and h is hhi),
                                                    stop=(kc == KC - 1 and w is wlo))
                last.then_inc(s["w_used"], 1)

            def tiles(b, first):
                for m in range(2):
                    if not first:
                        pe.wait_ge(s["u_stored"], b + (m - 1))
                    for hf in range(2):
                        multiply(2 * b + (2 * m + hf), hf, 3 * m)

            tiles(0, True)
            with pe.Fori(1, NT // 2) as pair:
                tiles(pair * 2, False)

            def mm(out, lhsT, rhs, start=True, stop=True):
                return nc.tensor.matmul(out, lhsT, rhs, start=start, stop=stop)

            def turn(out, in_, name=None):
                ins = nc.tensor.transpose(out, in_, ident[0:in_.shape[0], 0:in_.shape[0]])
                if name:
                    ins.then_inc(*(s[name], 1) if name in s else signal[name])
                return ins

            pe.wait_ge(s["u_stored"], NT)
            for bank, tile, t0, n, name in ((1, KA, SEQ, SMP, "krow_ready"), (2, VA, SEQ, SMP, "vrow_ready"),
                                            (3, XB, SEQ, SMP, "xbrow_ready"), (4, XB, SEQ - 3, 3, "last3_ready")):
                for h in range(H):
                    last = turn(ps[0:n, bank, h * P:(h + 1) * P], U[:, tile + h, t0:t0 + n])
                last.then_inc(*signal[name])
            pe.wait_ge(s["crow_in"], 16)
            for h in range(H):
                last = turn(ps[:, 0, h * 24:(h + 1) * 24], crow[:, h * P:(h + 1) * P])
            last.then_inc(*signal["hist_ready"])
            pe.wait_ge(s["nrow_in"], 16)
            turn(ps[:, 5, 0:SMP], nrow[:, :], "nT_ready")
            pe.wait_ge(s["wqkv_in"], 48)
            pe.wait_ge(s["silu_ready"], H)
            pe.wait_ge(*done["hist_stored"])
            for j, bank in enumerate((6, 7, 0)):
                for h in range(H):
                    src = U[:, XB + h, SEQ:TOK] if j == 2 else xch[:, h, SEQ:TOK]
                    last = mm(ps[:, bank, h * SMP:(h + 1) * SMP], wqkv[:, j, h, :], src)
                last.then_inc(s["s_proj"], 1)
            pe.wait_ge(s["s_qk_stored"], 2)
            pe.wait_ge(*done["s_v_stored"])
            pe.wait_ge(s["wif_in"], 32)
            pe.wait_ge(*done["krow_stored"])
            for c in range(12):
                last = mm(ps[0:36, 1, 0:SMP], wif[:, c, :], (qbT, kbT, vbT)[c % 3][:, c // 3, 0:SMP], c == 0, c == 11)
            last.then_inc(*signal["s_gates"])
            for bank, buf, name in ((2, kbT, "vrow_stored"), (3, vbT, "xbrow_stored")):
                pe.wait_ge(*done[name])
                for h in range(H):
                    last = turn(ps[0:SMP, bank, h * P:(h + 1) * P], buf[:, h, 0:SMP])
                last.then_inc(s["s_kvtok"], 1)
            pe.wait_ge(*done["last3_stored"])
            for h in range(H):
                last = mm(ps[0:SMP, 4, h * SMP:(h + 1) * SMP], kbT[:, h, 0:SMP], qbT[:, h, 0:SMP])
            last.then_inc(*signal["s_sqk"])
            pe.wait_ge(s["s_rows"], 3)
            pe.wait_ge(s["s_gate_step"], 19)
            pe.wait_ge(*done["n_stored"])
            turn(ps[0:SMP, 5, 0:P], G[:, 0:SMP])
            mm(ps[:, 5, P:P + SMP], ones[:, :], DgS[:, :, :].rearrange("p h b -> p (h b)")).then_inc(*signal["s_GT"])
            mm(ps[0:SMP, 6, 0:P], ones[:, 0:SMP], AblkS[:, :, :].rearrange("p h t -> p (h t)")).then_inc(*signal["s_AB"])
            pe.wait_ge(s["q8_ready"], 2 * H + NSEQ)
            pe.wait_ge(s["cs_in"], 32)
            for h in range(H):
                for b in range(NSEQ):
                    last = mm(ps[0:SMP, (7, 0)[h // 2], 129 * (h % 2):129 * (h % 2) + 129], qmask[:, b, h, :],
                              Cs[:, H * b + h, :], b == 0, b == NSEQ - 1)
            last.then_inc(*signal["s_inter"])
            pe.wait_ge(*done["s_W"])
            pe.wait_ge(*done["s_vaug"])
            pe.wait_ge(s["s_GT_stored"], 2)
            for h in range(H):
                last = mm(ps[0:SMP, (3, 5)[h // 2], 129 * (h % 2):129 * (h % 2) + 129], E[0:SMP, h, 0:SMP], vaug[0:SMP, h, :])
            last.then_inc(*signal["s_intra"])
            pe.wait_ge(*done["s_nd_scaled"])
            for h in range(H):
                last = turn(ps[0:SMP, 7, h * P:(h + 1) * P], U[:, OB + h, SEQ:TOK])
            last.then_inc(*signal["s_obT"])
            for b in range(NSEQ):
                pe.wait_ge(s["s_kwm"], b + 1)
                if b >= 2:
                    pe.wait_ge(s["s_C"], b - 1)
                for h in range(H):
                    last = mm(ps[:, ((1, 2), (4, 6))[b % 2][h // 2], 129 * (h % 2):129 * (h % 2) + 129],
                              kwm[:, b % 2, h, :], vaug[0:SMP, h, :])
                last.then_inc(s["s_cu"], 1)
            pe.wait_ge(*done["s_nd"])
            pe.wait_ge(s["s_C"], NSEQ)
            turn(ps[0:SMP, 5, 0:DH], Cs[:, :, DH], "s_nrow")
            pe.wait_ge(*done["s_hn"])
            for h in range(H):
                last = turn(ps[:, 0, h * SMP:(h + 1) * SMP], nd[0:SMP, h, 0:DH])
            last.then_inc(*signal["s_hT"])

            pe.wait_ge(*done["s_bo"])
            pe.wait_ge(*done["s_nout"])
            pe.wait_ge(*done["den_step"])

            def stream_pe(i, first, last):
                G0, t0 = i * GROUPS, i * P
                if not first:
                    pe.wait_ge(s["p_ready"], i)
                    for u in range(5):
                        if u == 0:
                            pe.wait_ge(s["kT_act"], G0)
                        elif u == 1:
                            pe.wait_ge(s["kT_dve"], G0)
                        elif u == 3:
                            pe.wait_ge(s["pT_dve"], (i - 1) * 2 + 1)
                        else:
                            pe.wait_ge(s["pT_act"], (i - 1) * 3 + u // 2)
                        if u < 4:
                            for k in range(4):
                                ins = turn(ps[:, u % 2, k * P:(k + 1) * P], S[:, (4 * u + k) * P:(4 * u + k + 1) * P])
                        else:
                            ins = turn(ps[0:SMP, 0, 0:P], S[:, PAST:PAST + SMP])
                        ins.then_inc(s["pT_ready"], 1)

                def unit(g):
                    if not last:
                        pe.wait_ge(k_in[g % 2], i * 128 + (g // 2 + 1) * 32)
                        if g == 0:
                            if not first:
                                pe.wait_ge(s["pT_act"], i * 3)
                                pe.wait_ge(s["pT_dve"], i * 2)
                        else:
                            pe.wait_ge(s["kT_act"], G0 + g)
                            pe.wait_ge(s["kT_dve"], G0 + g)
                        for h in range(H):
                            for n in range(GP):
                                ins = turn(ps[:, h // 2, ((h % 2) * GP + n) * P:((h % 2) * GP + n + 1) * P],
                                           Kr[:, (GP * g + n) % 4, h * P:(h + 1) * P])
                        ins.then_inc(s["k_used"], 1)
                    if not first:
                        pe.wait_ge(v_in[g % 2], (i - 1) * 128 + (g // 2 + 1) * 32)
                        if g == 0:
                            pe.wait_ge(s["pT_act"], i * 3)
                            pe.wait_ge(s["pT_dve"], i * 2)
                            if not (isinstance(i, int) and i == 1):
                                pe.wait_ge(s["ao_ready"], i - 1)
                        for n in range(GP):
                            k = GP * g + n
                            for h in range(H):
                                ins = mm(ps[32 * h:32 * h + 8, 3, 0:DH], pT[:, k, 8 * h:8 * h + 8],
                                         Vr[:, k % 4, h * DH:(h + 1) * DH], k == 0, False)
                        ins.then_inc(s["v_used"], 1)

                def scores(g):
                    if last:
                        return
                    if g < GROUPS:
                        pe.wait_ge(s["kT_act"], G0 + (g + 1))
                        pe.wait_ge(s["kT_dve"], G0 + (g + 1))
                    if g == 0:
                        pe.wait_ge(s["q8cur_ready"], i + 1)
                        if not first:
                            pe.wait_ge(s["s_stored"], i * 9)
                            if not (isinstance(i, int) and i == 1):
                                pe.wait_ge(s["as_added"], i - 1)
                    else:
                        pe.wait_ge(s["s_stored"], i * 9 + g)
                    for h in range(H):
                        keys = kTs[:, g % 2, h, :] if g < GROUPS else U[:, KA + h, SEQ:TOK]
                        ins = mm(ps[32 * h:32 * h + 32, 2, 0:keys.shape[1]], q8cur[:, h, :], keys)
                    ins.then_inc(s["scores_ready"], 1)

                def project():
                    if not first:
                        pe.wait_ge(s["C_done"], i)
                        pe.wait_ge(s["h_gated"], i * 5)
                    for j in range(3):
                        for h in range(H):
                            src = U[:, XB + h, bass.ds(t0, P)] if j == 2 else xch[:, h, bass.ds(t0, P)]
                            ins = mm(ps[:, 4 + j, h * P:(h + 1) * P], wqkv[:, j, h, :], src)
                        ins.then_inc(s["proj_ready"], 1)

                def gates():
                    pe.wait_ge(s["qk_stored"], 2 * i + 2)
                    pe.wait_ge(s["v_stored"], i + 1)
                    if not first:
                        pe.wait_ge(s["bo_done"], i)
                    for c in range(12):
                        ins = mm(ps[0:36, 7, 0:P], wif[:, c, :], (qbT, kbT, vbT)[c % 3][:, c // 3, :], c == 0, c == 11)
                    ins.then_inc(s["gates_ready"], 1)
                    for bank, buf in ((4, kbT), (5, vbT)):
                        for h in range(H):
                            ins = turn(ps[:, bank, h * P:(h + 1) * P], buf[:, h, :])
                    ins.then_inc(s["kvtok_ready"], 1)
                    for h in range(H):
                        ins = mm(ps[:, 6, h * P:(h + 1) * P], kbT[:, h, :], qbT[:, h, :])
                    ins.then_inc(s["sqk_ready"], 1)

                def rows():
                    pe.wait_ge(s["rows_exp"], 3 * i + 3)
                    pe.wait_ge(s["kw_ready"], 3 * i + 2)
                    turn(ps[:, 7, 0:P], G[:, :])
                    mm(ps[:, 7, P:P + H], ones[:, :], Dg[:, :]).then_inc(s["GT_ready"], 1)
                    pe.wait_ge(s["vaug_stored"], i + 1)
                    mm(ps[:, 5, :], ones[:, :], Ablk[:, :, :].rearrange("p h t -> p (h t)")).then_inc(s["AB_ready"], 1)

                def products():
                    pe.wait_ge(s["kw_ready"], 3 * i + 3)
                    pe.wait_ge(s["arg_ready"], i + 1)
                    if not first:
                        pe.wait_ge(s["C_done"], i)
                    for h in range(H):
                        ins = mm(ps[:, 4 + h // 2, 129 * (h % 2):129 * (h % 2) + 129], qbT[:, h, :], Caug[:, h, :])
                    ins.then_inc(s["inter_ready"], 1)
                    pe.wait_ge(s["W_ready"], i + 1)
                    pe.wait_ge(s["gt_stored"], 2 * i + 2)
                    for h in range(H):
                        ins = mm(ps[:, 6 + h // 2, 129 * (h % 2):129 * (h % 2) + 129], E[:, h, :], vaug[:, h, :])
                    ins.then_inc(s["intra_ready"], 1)

                def update():
                    pe.wait_ge(s["nd_scaled"], i + 1)
                    for h in range(H):
                        ins = mm(ps[:, 4 + h // 2, 129 * (h % 2):129 * (h % 2) + 129], kw[:, h, :], vaug[:, h, :])
                    ins.then_inc(s["cu_ready"], 1)
                    pe.wait_ge(s["nd_ready"], i + 1)
                    pe.wait_ge(s["ob_copied"], i + 1)
                    for h in range(H):
                        ins = turn(ps[:, 6, h * P:(h + 1) * P], kbT[:, h, :])
                    ins.then_inc(s["obT_ready"], 1)

                def finish():
                    pe.wait_ge(s["hn_ready"], i + 1)
                    for h in range(H):
                        ins = turn(ps[:, 7, h * P:(h + 1) * P], nd[:, h, 0:DH])
                    ins.then_inc(s["hTr_ready"], 1)

                if not last:
                    project()
                unit(0)
                unit(1)
                scores(0)
                if not last:
                    gates()
                unit(2)
                scores(1)
                unit(3)
                scores(2)
                if not last:
                    rows()
                unit(4)
                scores(3)
                unit(5)
                scores(4)
                if not last:
                    products()
                unit(6)
                scores(5)
                unit(7)
                scores(6)
                if not last:
                    update()
                scores(7)
                scores(8)
                if not first:
                    for h in range(H):
                        ins = mm(ps[32 * h:32 * h + 8, 3, 0:DH], pT[0:SMP, 16, 8 * h:8 * h + 8],
                                 vS[:, h * DH:(h + 1) * DH], False, True)
                    ins.then_inc(s["o_ready"], 1)
                if not last:
                    finish()
                if not first:
                    pe.wait_ge(s["ao_ready"], i)
                    if not last:
                        pe.wait_ge(s["s_stored"], i * 9 + 9)
                    if not (isinstance(i, int) and i == 1):
                        pe.wait_ge(s["as_added"], i - 1)
                    mm(ps[:, 2, 0:P].rearrange("p (h t) -> p h t", h=H), AO[:, :],
                       place_q[:, :, bass.ds((i - 1) * (-STEPS) + 28, SMP)]).then_inc(s["comb_ready"], 1)

            stream_pe(0, True, False)
            stream_pe(1, False, False)
            with pe.Fori(2, NSEQ) as i:
                stream_pe(i, False, False)
            stream_pe(NSEQ, False, True)

            pe.wait_ge(s["as_added"], NSEQ)
            turn(ps[:, 4, 0:P], AS[:, :], "as_T_ready")
            pe.wait_ge(*done["as_n2"])
            turn(ps[:, 5, 0:P], AO[:, :], "as_T2")

            pe.wait_ge(*done["as_done"])
            pe.wait_ge(s["out_state"], 48)
            for t in range(CH):
                if t >= 2:
                    pe.wait_ge(s["kt_stored"], t - 1)
                for h in range(H):
                    last = turn(ps[:, 2 * (t % 2), h * P:(h + 1) * P], U[:, KA + h, t * P:(t + 1) * P])
                last.then_inc(s["kt_ready"], 1)
                if t >= 2:
                    pe.wait_ge(s["vt_stored"], t - 1)
                for h in range(H):
                    last = turn(ps[:, 2 * (t % 2) + 1, h * P:(h + 1) * P], U[:, VA + h, t * P:(t + 1) * P])
                last.then_inc(s["vt_ready"], 1)
            pe.wait_ge(s["kt_stored"], CH)
            pe.wait_ge(s["vt_stored"], CH)

            def head_scores(u):
                i, h = divmod(u, H)
                n = (i + 1) * P
                for m in range(2):
                    pe.wait_ge(s["qz_ready"], 2 * u + m + 1)
                    if u >= NARROW:
                        pe.wait_ge(s["pexp"], 2 * u - 1 + m)
                    elif u >= 2:
                        pe.wait_ge(s["pexp"], 2 * u - 3 + m)
                    for c in range(0, n, 512):
                        k = min(512, n - c)
                        last = mm(score_row(u, m)[:, c:c + k], qz[:, u % 3, m, :], U[:, KA + h, c:c + k])
                    last.then_inc(s[("sc0", "sc1")[m]], 1)

            def head_turn(u):
                i, h = divmod(u, H)
                pe.wait_ge(s["w_done"], u + 1)
                if u == NARROW:
                    pe.wait_ge(s["on_ready"], u - 1)
                for c in range(0, i + 1, 4):
                    if c == 4 or u >= 1:
                        pe.wait_ge(s["wT_stored"], WT_BEFORE[u])
                    for k in range(c, min(c + 4, i + 1)):
                        last = turn(ps[:, 4 + c // 4, (k - c) * P:(k - c + 1) * P], pp[:, u % 2, 0, k * P:(k + 1) * P])
                    last.then_inc(s["wT_ready"], 1)

            def head_values(u):
                i, h = divmod(u, H)
                pe.wait_ge(s["wT_stored"], WT_BEFORE[u + 1])
                if u >= 2:
                    pe.wait_ge(s["on_ready"], u - (u < NARROW))
                for k in range(i + 1):
                    last = mm(ps[:, head_bank(u), 0:DH], wT[:, k, :], vtok[:, k, h * DH:(h + 1) * DH], k == 0, k == i)
                last.then_inc(s["pv_ready"], 1)

            def head_back(u):
                pe.wait_ge(s["on_ready"], u + 1)
                if u >= 1:
                    pe.wait_ge(s["a_done"], u)
                turn(ps[:, 7, 0:P], on[:, u % 2, :], "onT_ready")

            head_scores(0)
            head_scores(1)
            for u in range(CH * H):
                if u + 2 < NARROW:
                    head_scores(u + 2)
                elif NARROW <= u + 1 < CH * H:
                    head_scores(u + 1)
                head_turn(u)
                head_values(u)
                if u >= 1:
                    head_back(u - 1)
            head_back(CH * H - 1)

            pe.wait_ge(s["a_done"], CH * H)
            pe.wait_ge(s["wout_in"], 16)

            def project_out(j):
                t0, n = XT[j]
                if j >= 1:
                    pe.wait_ge(s["y_x"], j)
                for k in range(KC):
                    cat = U[:, (ZA + k) if k < H else (ZB + k - H), t0:t0 + n]
                    for c in range(2):
                        last = mm(ps[0:n, c, :], cat, wout[:, k, c * 512:(c + 1) * 512], k == 0, k == KC - 1)
                last.then_inc(s["y_ready"], 1)

            def embed(j):
                t0, n = XT[j]
                pe.wait_ge(pr_in, 16 * (j + 1))
                if j >= 1:
                    pe.wait_ge(s["pw_stored"], j)
                for k in range(2):
                    last = turn(ps[:, 6, k * P:k * P + n], prow[0:n, k * P:(k + 1) * P])
                last.then_inc(s["prow_T"], 1)
                pe.wait_ge(s["prow_stored"], j + 1)
                pe.wait_ge(s["plew_in"], 16)
                for k in range(2):
                    for c in range(2):
                        last = mm(ps[0:n, 6 + c, :], pTt[:, k, 0:n], plew[:, k, c * 512:(c + 1) * 512], k == 0, k == 1)
                last.then_inc(s["pw_ready"], 1)
                pe.wait_ge(s["y_x"], j + 1)
                if j >= 1:
                    pe.wait_ge(s["x1T_stored"], j)
                for k in range(KC):
                    last = turn(ps[:, 2 + k // 4, (k % 4) * P:(k % 4) * P + n], x1[0:n, j % 2, k * P:(k + 1) * P])
                last.then_inc(s["x1T_ready"], 1)

            def gate(j):
                t0, n = XT[j]
                pe.wait_ge(s["x1T_stored"], j + 1)
                pe.wait_ge(s["wgate_in"], 16)
                if j >= 1:
                    pe.wait_ge(s["gate_sig"], j)
                for k in range(KC):
                    for c in range(2):
                        last = mm(ps[0:n, 4 + c, :], x1T[:, k, 0:n], wgate[:, k, c * 512:(c + 1) * 512], k == 0, k == KC - 1)
                last.then_inc(s["gate_ready"], 1)

            project_out(0)
            embed(0)
            for j in range(9):
                if j + 1 < 9:
                    project_out(j + 1)
                gate(j)
                if j + 1 < 9:
                    embed(j + 1)


OUTS = [("y_prompt", (1, SEQ, D)), ("y_sample", (NSEQ, STEPS, D)), ("k_prompt", (1, 1, SEQ, H, DH)),
        ("v_prompt", (1, 1, SEQ, H, DH)), ("conv_prompt", (1, 1, 3, H * DH)), ("C_prompt", (1, 1, H, DH, DH)),
        ("n_prompt", (1, 1, H, DH)), ("m_prompt", (1, 1, H)), ("k_sample", (1, NSEQ, STEPS, H, DH)),
        ("v_sample", (1, NSEQ, STEPS, H, DH)), ("conv_sample", (1, NSEQ, 3, H * DH)),
        ("C_sample", (1, NSEQ, H, DH, DH)), ("n_sample", (1, NSEQ, H, DH)), ("m_sample", (1, NSEQ, H))]


def kernel(**inputs):
    import numpy as np
    import concourse.bacc as bacc
    from concourse.bass_utils import run_bass_kernel_spmd

    nc = bacc.Bacc("TRN2", target_bir_lowering=False, num_devices=1)
    arrays, io = {}, {}
    for name, a in inputs.items():
        a = np.ascontiguousarray(a)
        arrays[f"in_{name}"] = a
        io[name] = nc.dram_tensor(f"in_{name}", a.shape, mybir.dt.from_np(a.dtype), kind="ExternalInput").ap()
    for name, shape in OUTS:
        io[name] = nc.dram_tensor(f"out_{name}", shape, F32, kind="ExternalOutput").ap()
    program(nc, io)
    r = run_bass_kernel_spmd(nc, [arrays], core_ids=[0])
    return tuple(r.results[0][f"out_{name}"] for name, _ in OUTS)
```

```python
import concourse.bass as bass
from concourse import mybir
from contextlib import ExitStack

F32 = mybir.dt.float32
F32R = mybir.dt.float32r
I32 = mybir.dt.int32
BF16 = mybir.dt.bfloat16
ALU = mybir.AluOpType
ACT = mybir.ActivationFunctionType
AX = mybir.AxisListType

P = 128
D = 1024
H = 4
DH = 128
SEQ = 1024
NSEQ, STEPS = 8, 4
SMP = NSEQ * STEPS
TOK = SEQ + SMP
KC = D // P
NT = 28
CH = SEQ // P
PAGE = 128
PAGES = 16
PAST = PAGE * PAGES
POOL = 160
GP = 2
GROUPS = PAGES // GP
PLE = 256
EPS = 1e-6
NEG = -1e30
LOWEST = -3.4e38
THIRD = TOK // 3
LAM_INIT = 0.8 - 0.6
KSCALE = DH ** -0.5
QSCALE = 64 ** -0.5
PARAMS = 11
QA, KA, VA, ZA, XB, OB, ZB = (4 * n for n in range(7))
SECTIONS = [(QA, 12, ACT.Copy), (XB, 4, ACT.Copy), (OB, 4, ACT.Sigmoid), (ZA, 4, ACT.Silu), (ZB, 4, ACT.Silu)]
XT = [(t * P, P) for t in range(CH)] + [(SEQ, SMP)]


def bc(ap, n):
    return ap.rearrange("p (h o) -> p h o", o=1).broadcast_to([ap.shape[0], ap.shape[1], n])


def lead(ap, n):
    return ap.rearrange("p (o t) -> p o t", o=1).broadcast_to([ap.shape[0], n, ap.shape[1]])


CONV_STEPS = 2 * 4 * H
NARROW = 4 * H
WT_BEFORE = [sum((v // H + 4) // 4 for v in range(u)) for u in range(CH * H + 1)]


def program(nc, io):
    ctx = ExitStack()
    with ctx:
        def sb(name, shape, dt=F32):
            return ctx.enter_context(nc.sbuf_tensor(name, shape, dt))

        def sem(name):
            return ctx.enter_context(nc.semaphore(name))

        ps = ctx.enter_context(nc.psum_tensor("ps", [P, 8, 512], F32))

        ident = sb("ident", [P, P])
        ones = sb("ones", [P, P])
        mask_t = sb("mask_t", [P, P])
        mask_s = sb("mask_s", [SMP, SMP])
        seqmask = sb("seqmask", [SMP, NSEQ])
        place_q = sb("place_q", [P, H, 60])
        mask_new = sb("mask_new", [P, 60])
        small = sb("small", [P, 160])
        sumsq, rstd, mhalf = small[:, 0:9], small[:, 16:25], small[:, 32:33]
        vec = small[:, 64:96]
        conv_w, conv_b, attn_g, mlstm_g, skip = vec[:, 0:16], vec[:, 16:20], vec[:, 20:24], vec[:, 24:28], vec[:, 28:32]
        bias_i, bias_f = small[0:H, 33:34], small[32:32 + H, 33:34]
        lam_e = small[:, 34:36]
        lam, neg_lam, sign, row_t, row_4 = (small[:, 36 + n:37 + n] for n in range(5))
        ag = small[:, 44:48]
        mcol = small[0:H, 48:48 + CH + 1]
        coef = small[:, 96:104]
        den_s = small[:, 104:112]
        gmax = small[:, 112:121]
        negmax_s = small[:, 121:122]
        ss4, rs4, rd4 = small[:, 124:128], small[:, 128:132], small[:, 132:136]
        map_scale = small[:, 144:146]
        eps = small[:, 146:147]
        aL, dec4 = small[0:H, 136:137], small[:, 140:144]
        wif = sb("wif", [P, 12, 2 * H])
        U = sb("U", [P, NT, TOK])

        base = (nc.sbuf_base + 31) // 32 * 32
        u_base = base - NT * TOK * 4
        top = [base]

        def place(name, shape, dt=F32, offset=None):
            size = 2 if dt == BF16 else 4
            for n in shape[1:]:
                size *= n
            size = (size + 31) // 32 * 32
            if offset is None:
                offset = top[0]
                top[0] += size
            return nc.alloc_sbuf_tensor_at(name, shape, dt, offset=offset)

        hhi = place("hhi", [P, KC, TOK], F32R)
        hlo = place("hlo", [P, KC, TOK], F32R)
        wst = place("wst", [P, 4, 4, P])
        whi = place("whi", [P, 2, 4, P], F32R)
        wlo = place("wlo", [P, 2, 4, P], F32R)
        xrow, hrow, square, gpre = U[:, 0:2, 0:D], U[:, 2:4, 0:D], U[:, 4, 0:D], U[:, 5, 0:D]
        vrow, lamv, lamp = U[0:32, 6, 0:P], U[:, 7, 0:256], U[:, 8, 0:128]
        iot = U[:, 9, 0:8].bitcast(I32)
        iof = U[:, 10, 0:8]

        top[0] = base
        xch = place("xch", [P, H, TOK])
        wqkv = place("wqkv", [P, 3, H, DH])
        qbT = place("qbT", [P, H, P])
        kbT = place("kbT", [P, H, P])
        vbT = place("vbT", [P, H, P])
        vaug = place("vaug", [P, H, DH + 1])
        kw = place("kw", [P, H, DH])
        E = place("E", [P, H, P])
        Ablk = place("Ablk", [P, H, P])
        nd = place("nd", [P, H, DH + 1])
        Caug = place("Caug", [P, H, DH + 1])
        G = place("G", [P, P])
        GT = place("GT", [P, P])
        AS = place("AS", [P, P])
        q8 = place("q8", [P, NSEQ, H, 8])
        q8cur = place("q8cur", [P, H, 32])
        Dg = place("Dg", [P, H])
        gat = place("gat", [H, 8, P])
        AO = place("AO", [P, DH], offset=top[0])
        pT = place("pT", [P, PAGES + 1, 32])
        vS = place("vS", [SMP, 512])
        ptab = place("ptab", [1, NSEQ * PAGES], I32)
        stream_a = top[0]
        kTs = place("kTs", [P, H, GP * PAGE])
        S = place("S", [P, PAST + SMP])
        Kr = place("Kr", [P, 8, 512])
        Vr = place("Vr", [P, 4, 512])
        assert top[0] <= nc.sbuf_usable_end, top[0]
        top[0] = stream_a
        Cs = place("Cs", [P, NSEQ * H, DH + 1])
        history = top[0]
        xpad = place("xpad", [P, H, NSEQ, 7])
        nrow = place("nrow", [SMP, DH])
        kwm = place("kwm", [SMP, 2, H, DH], offset=history)
        crow = place("crow", [24, 512])
        top[0] = max(top[0], history + 2 * H * DH * 4)
        nout = place("nout", [SMP, DH])
        kS = place("kS", [SMP, 512])
        xbS = place("xbS", [SMP, 512])
        xbP = place("xbP", [3, 512])
        qmask = place("qmask", [P, NSEQ, H, SMP])
        AblkS = place("AblkS", [P, H, SMP])
        DgS = place("DgS", [P, H, NSEQ])
        decS = place("decS", [P, H, NSEQ])
        g5 = place("g5", [H, 8, NSEQ, 5])
        gs = place("gs", [H, 6, SMP])
        assert top[0] <= nc.sbuf_usable_end

        top[0] = base
        wout = place("wout", [P, KC, D])
        weights_hi = top[0]
        vtok = place("vtok", [P, CH, 512])
        pp = place("pp", [P, 2, 2, SEQ])
        rest_of_tail = top[0]
        ktok = place("ktok", [P, 2, 512])
        wT = place("wT", [P, CH, P])
        qz = place("qz", [P, 3, 2, P])
        on = place("on", [P, 2, P])
        end_of_prompt = top[0]
        st = place("st", [P, 2, 16])
        plew = place("plew", [P, 2, D])
        assert top[0] <= nc.sbuf_usable_end
        wh = place("wh", [P, KC, D], F32R, offset=weights_hi)
        top[0] = rest_of_tail
        sg = place("sg", [P, D])
        junk = place("junk", [P, D], BF16)
        gple = place("gple", [P, D])
        prow = place("prow", [P, PLE])
        pTt = place("pTt", [P, 2, P])
        assert top[0] <= end_of_prompt
        rh = place("rh", [P, KC, TOK], F32R, offset=u_base + QA * TOK * 4)
        mask_q = place("mask_q", [P, P], offset=u_base + XB * TOK * 4 + KC * D * 4)
        rl = [place(f"rl{n}", [P, H, TOK], F32R, offset=u_base + tile * TOK * 4) for n, tile in enumerate((ZA, ZB))]
        top[0] = u_base + VA * TOK * 4
        rows = place("rows", [P, 3, D])
        gpost = place("gpost", [P, D])
        assert top[0] <= u_base + ZA * TOK * 4
        wgate = place("wgate", [P, KC, D], offset=u_base + XB * TOK * 4)
        wout_lo = place("wout_lo", [P, KC, D], F32R, offset=base)
        wgate_lo = place("wgate_lo", [P, KC, D], F32R, offset=u_base + XB * TOK * 4)

        names = """masks_ready gpre_in sumsq_ready rstd_ready h_ready hT_ready hhi_ready hlo_ready whi_ready wlo_ready w_used
            u_stored ag_ready iota_ready lam_sum wif_in wqkv_in ptab_in cs_in conv_step silu_ready
            zero_ready q8_ready s_proj s_qk_stored s_kvtok s_gate_step s_gate_exp s_kwm s_cu s_C s_h_gated
            s_bo_t pT_ready pT_act pT_dve proj_ready qk_stored v_stored k_used v_used kT_act kT_dve
            scores_ready s_stored negmax_ready p_ready coef_ready o_ready ao_ready comb_ready as_added
            q8cur_ready gates_ready kvtok_ready sqk_ready vaug_stored gate_step gate_exp rows_exp GT_ready
            AB_ready gt_stored kw_ready arg_ready E_ready W_ready inter_ready intra_ready nd_scaled
            nd_ready cu_ready C_done obT_ready ob_copied h_gated sq_ready hrs_ready hn_ready hTr_ready
            bo_t bo_done xsk_ready kt_ready vt_ready kt_stored vt_stored out_v_prompt qz_ready sc0 sc1
            masked rmax pexp w_done wT_ready wT_stored pv_ready psq prs on_ready onT_ready a_done wgate_in
            y_ready y_x prow_T prow_stored pw_ready x1T_ready gate_ready gate_sig t_done out_ready
            params_in out_sample out_state mean_ready w_step soft_step hist_in tail_in row_sq row_rs
            row_step w_hi w_lo cat_hi cat_lo x1T_hi x1T_lo
            gple_in""".split()
        s = {n: sem(n) for n in names}
        once = {"pe": """vecT_ready krow_ready vrow_ready xbrow_ready last3_ready hist_ready nT_ready s_gates s_sqk s_GT
            s_AB s_inter s_intra s_obT s_nrow s_hT as_T_ready as_T2""",
                "act": """lam_exp vec_ready hist_stored krow_stored vrow_stored xbrow_stored last3_stored n_stored s_vaug
            s_E s_nd_scaled s_nout s_sq as_norm as_n2""",
                "dve": """lam_ready xpad_new s_v_stored s_kw s_arg s_W s_nd s_hn s_bo den_step as_done""",
                "pool": """ident_ready s_rs as_hrs mask_q_zero mask_q_ready"""}
        signal, done = {}, {}
        for engine, steps in once.items():
            steps_done = sem(f"{engine}_once")
            for n, name in enumerate(steps.split()):
                signal[name], done[name] = (steps_done, 1), (steps_done, n + 1)
        x_in = [sem("x_in0"), sem("x_in1")]
        w_in = [sem(f"w_in{n}") for n in range(4)]
        k_in = [sem(f"k_in{n}") for n in range(4)]
        v_in = [sem(f"v_in{n}") for n in range(2)]
        k_out = [sem("k_out0"), sem("k_out1")]
        row_in = [sem(f"row_in{n}") for n in range(3)]
        row_out = [sem(f"row_out{n}") for n in range(3)]
        pr_in = sem("pr_in")

        def score_row(u, m):
            first, banks = (2 * (u % 2) + m, 1) if u < NARROW else (2 * m, 2)
            return ps[:, first:first + banks, :].rearrange("p a b -> p (a b)")

        def head_bank(u):
            return 5 + u % 2 if u < NARROW else 6

        block = ctx.enter_context(nc.Block())

        @block.sync
        def _(sp):
            def put(name, out, in_, **more):
                sp.dma_start(out, in_, **more).then_inc(s[name], 16)

            sp.dma_start(gpre, io["norm_pre_g"][0:1, :].broadcast_to([P, D])).then_inc(s["gpre_in"], 16)
            xs = io["x_sample"].rearrange("b t d -> (b t) d")

            def load_x(t):
                t0, n = XT[t]
                src = io["x_prompt"][0, t0:t0 + n, :] if t < CH else xs
                sp.dma_start(xrow[0:n, t % 2, :], src).then_inc(x_in[t % 2], 16)

            load_x(0)
            load_x(1)
            sp.dma_start(vrow[0:16, :], io["conv_w"][0].rearrange("j (c p) -> (j c) p", p=P)).then_inc(s["params_in"], 16)
            for n, name in enumerate(("conv_b", "attn_norm_g", "mlstm_norm_g", "mlstm_skip")):
                sp.dma_start(vrow[16 + 4 * n:20 + 4 * n, :], io[name][0].rearrange("(c p) -> c p", p=P)
                             ).then_inc(s["params_in"], 16)
            for n, name in enumerate(("lam_q1", "lam_k1", "lam_q2", "lam_k2")):
                sp.dma_start(lamv[:, 64 * n:64 * n + 64], io[name][0:1, :].broadcast_to([P, 64])).then_inc(s["params_in"], 16)
            sp.dma_start(bias_i, io["b_if"][0, 0:H].rearrange("(h o) -> h o", o=1)).then_inc(s["params_in"], 16)
            sp.dma_start(bias_f, io["b_if"][0, H:2 * H].rearrange("(h o) -> h o", o=1)).then_inc(s["params_in"], 16)
            for t in range(2, 9):
                sp.wait_ge(s["h_ready"], t - 1)
                load_x(t)

            w_dram = io["w_in"][0].rearrange("(k p) n -> p k n", p=P)

            def load_w(q, tile, hf, slot, wait):
                if wait:
                    sp.wait_ge(s["wlo_ready"], q - 3)
                sp.dma_start(wst[:, slot, :, :], w_dram[:, 4 * hf:4 * hf + 4, bass.ds(tile * P, P)]
                             ).then_inc(w_in[slot], 16)

            n = 0
            for first, count, _ in SECTIONS:
                if n == 0:
                    for m in range(2):
                        for hf in range(2):
                            load_w(0, first + m, hf, 2 * m + hf, False)
                with sp.Fori(n // 2 + (n == 0), (n + count) // 2) as pair:
                    b = pair * 2
                    for m in range(2):
                        for hf in range(2):
                            load_w(2 * (b + m) + hf, b + (m + first - n), hf, 2 * m + hf, True)
                if n == 0:
                    sp.dma_start(wif[:, :, :], io["w_if"][0].rearrange("(c p) n -> p c n", p=P)).then_inc(s["wif_in"], 16)
                n += count

            sp.wait_ge(s["w_used"], 2 * NT)
            sp.dma_start(crow[:, :], io["state_conv"][0].rearrange("b j d -> (b j) d")).then_inc(s["hist_in"], 16)
            for j, name in enumerate(("w_q_b", "w_k_b", "w_v_b")):
                sp.dma_start(wqkv[:, j, :, :], io[name][0].rearrange("h d e -> d h e")).then_inc(s["wqkv_in"], 16)
            sp.dma_start(nrow[:, :], io["state_n"][0].rearrange("b h d -> (b h) d")).then_inc(s["hist_in"], 16)
            sp.dma_start(g5[:, 1, :, 0], io["state_m"][0].rearrange("b h -> h b"), allow_slow_non_contiguous=True).then_inc(s["cs_in"], 16)
            sp.dma_start(Cs[:, :, 0:DH], io["state_C"][0].rearrange("b h d e -> d (b h) e")).then_inc(s["cs_in"], 16)
            sp.dma_start(ptab[:, :], io["page_table"].rearrange("(o b) n -> o (b n)", o=1)).then_inc(s["ptab_in"], 16)

            sp.wait_ge(*done["krow_stored"])
            put("out_sample", io["k_sample"][0].rearrange("b t h d -> (b t) (h d)"), kS[:, :])
            sp.wait_ge(*done["vrow_stored"])
            put("out_sample", io["v_sample"][0].rearrange("b t h d -> (b t) (h d)"), vS[:, :])
            sp.wait_ge(*done["xbrow_stored"])
            for b in range(NSEQ):
                put("out_sample", io["conv_sample"][0, b], xbS[STEPS * b + 1:STEPS * b + STEPS, :])
            sp.wait_ge(*done["last3_stored"])
            put("out_sample", io["conv_prompt"][0, 0], xbP[:, :])
            sp.wait_ge(s["s_gate_step"], 11)
            put("out_sample", io["m_sample"][0].rearrange("b h -> h b"), g5[:, 4, :, STEPS],
                allow_slow_non_contiguous=True)
            sp.wait_ge(s["s_C"], NSEQ)
            put("out_sample", io["C_sample"][0].rearrange("b h d e -> d (b h) e"), Cs[:, :, 0:DH])
            sp.wait_ge(*done["s_nout"])
            put("out_sample", io["n_sample"][0].rearrange("b h d -> (b h) d"), nout[:, :])
            sp.wait_ge(*done["s_bo"])
            sp.wait_ge(s["out_sample"], 16 * (NSEQ + 6))

            sp.wait_ge(s["ptab_in"], 16)
            ck = io["cache_k"][0].rearrange("n p h d -> n p (h d)")
            cv = io["cache_v"][0].rearrange("n p h d -> n p (h d)")

            def numbers(seq, g):
                return [sp.value_load(ptab[0:1, bass.ds(seq * PAGES + (GP * g + n), 1)], min_val=0, max_val=POOL - 1)
                        for n in range(GP)]

            def pages(cache, buf, first_slot, nums, signal):
                for n, num in enumerate(nums):
                    sp.dma_start(buf[:, first_slot + n, :], cache[bass.ds(num, 1), :, :].rearrange("o p d -> (o p) d")
                                 ).then_inc(signal, 16)

            def stream_pages(i, first, last):
                for g in range(GROUPS):
                    k_nums = None if last else numbers(i, g)
                    v_nums = None if first else numbers(i - 1, g)
                    if not last:
                        if not (first and g < 4):
                            sp.wait_ge(s["k_used"], i * GROUPS + (g - 3))
                        pages(ck, Kr, GP * g % 8, k_nums, k_in[g % 4])
                    if not first:
                        if not (isinstance(i, int) and i == 1 and g < 2):
                            sp.wait_ge(s["v_used"], (i - 1) * GROUPS + (g - 1))
                        pages(cv, Vr, GP * g % 4, v_nums, v_in[g % 2])

            stream_pages(0, True, False)
            stream_pages(1, False, False)
            with sp.Fori(2, NSEQ) as i:
                stream_pages(i, False, False)
            stream_pages(NSEQ, False, True)

            sp.wait_ge(s["C_done"], CH)
            put("out_state", io["C_prompt"][0, 0].rearrange("h d e -> d h e"), Caug[:, :, 0:DH])
            put("out_state", io["n_prompt"][0, 0].rearrange("h d -> d h"), Caug[:, :, DH],
                allow_slow_non_contiguous=True)
            put("out_state", io["m_prompt"][0, 0].rearrange("(h o) -> h o", o=1), mcol[:, CH:CH + 1])
            sp.wait_ge(s["out_state"], 48)
            sp.wait_ge(*done["as_done"])
            kp = io["k_prompt"][0, 0].rearrange("t h d -> t (h d)")
            vp = io["v_prompt"][0, 0].rearrange("t h d -> t (h d)")
            for t in range(CH):
                sp.wait_ge(s["kt_stored"], t + 1)
                sp.dma_start(kp[t * P:(t + 1) * P, :], ktok[:, t % 2, :]).then_inc(k_out[t % 2], 16)
                sp.wait_ge(s["vt_stored"], t + 1)
                put("out_v_prompt", vp[t * P:(t + 1) * P, :], vtok[:, t, :])
            put("tail_in", wout[:, :, :], io["w_out"][0].rearrange("(k p) n -> p k n", p=P))
            put("tail_in", gpost[:, :], io["norm_post_g"][0:1, :].broadcast_to([P, D]))

            pin = io["p_sample"][0].rearrange("b t d -> (b t) d")

            def y_rows(q):
                t0, n = XT[q % 9]
                return io["y_prompt"][0, t0:t0 + n, :] if q % 9 < CH else io["y_sample"].rearrange("b t d -> (b t) d")

            def load_rows(q):
                t0, n = XT[q % 9]
                src = y_rows(q) if q >= 9 else io["x_prompt"][0, t0:t0 + n, :] if q < CH else xs
                if q >= 3:
                    sp.wait_ge(row_out[q % 3], 16 * (q // 3))
                sp.dma_start(rows[0:n, q % 3, :], src).then_inc(row_in[q % 3], 16)

            def load_p(j):
                t0, n = XT[j]
                if j >= 1:
                    sp.wait_ge(s["prow_T"], j)
                sp.dma_start(prow[0:n, :], io["p_prompt"][0, 0, t0:t0 + n, :] if j < CH else pin).then_inc(pr_in, 16)

            for q in range(3):
                load_rows(q)
            put("wgate_in", wgate[:, :, :], io["ple_gate_w"][0].rearrange("(k p) n -> p k n", p=P))
            put("tail_in", plew[:, :, :], io["ple_w"][0].rearrange("(k p) n -> p k n", p=P))
            sp.wait_ge(s["a_done"], CH * H)
            put("gple_in", gple[:, :], io["ple_norm_g"][0:1, :].broadcast_to([P, D]))
            load_p(0)
            for q in range(18):
                if q < 9:
                    sp.wait_ge(s["y_x"], q + 1)
                else:
                    if q < 17:
                        load_p(q - 8)
                    sp.wait_ge(s["out_ready"], q - 8)
                sp.dma_start(y_rows(q), rows[0:XT[q % 9][1], q % 3, :]).then_inc(row_out[q % 3], 16)
                if 3 <= q + 2 < 18:
                    load_rows(q + 2)
            for n in range(2):
                sp.wait_ge(k_out[n], 16 * CH // 2)
            sp.wait_ge(s["out_v_prompt"], 16 * CH)
            for n in range(3):
                sp.wait_ge(row_out[n], 16 * 6)

        @block.gpsimd
        def _(pool):
            nc.gpsimd.memset(ident[:, :], 0.0).then_inc(s["zero_ready"], 1)
            nc.gpsimd.memset(ones[:, :], 1.0).then_inc(s["zero_ready"], 1)
            nc.gpsimd.memset(mhalf, -0.5).then_inc(s["zero_ready"], 1)
            nc.gpsimd.memset(eps, EPS).then_inc(s["zero_ready"], 1)
            pool.wait_ge(s["zero_ready"], 4)
            nc.gpsimd.affine_select(out=ident[:, :], in_=ident[:, :], compare_op=ALU.not_equal, fill=1.0, base=0,
                                    pattern=[[-1, P]], channel_multiplier=1).then_inc(*signal["ident_ready"])

            def root(mean, out, wait, count, done):
                rows, cols = out.shape
                pool.wait_ge(*wait)
                nc.gpsimd.tensor_tensor(out, mean, eps[0:rows, :].broadcast_to([rows, cols]), ALU.add
                                        ).then_inc(s["mean_ready"], 1)
                pool.wait_ge(s["mean_ready"], count)
                nc.gpsimd.tensor_tensor(out, out, mhalf[0:rows, :].broadcast_to([rows, cols]), ALU.pow
                                        ).then_inc(*(s[done], 1) if done in s else signal[done])

            for t, (t0, n) in enumerate(XT):
                root(sumsq[0:n, t:t + 1], rstd[0:n, t:t + 1], (s["sumsq_ready"], t + 1), t + 1, "rstd_ready")

            nc.gpsimd.memset(mask_t[:, :], 0.0).then_inc(s["zero_ready"], 1)
            nc.gpsimd.memset(place_q[:, :, :], 0.0).then_inc(s["zero_ready"], 1)
            nc.gpsimd.memset(mask_new[:, :], NEG).then_inc(s["zero_ready"], 1)
            nc.gpsimd.memset(seqmask[:, :], 1.0).then_inc(s["zero_ready"], 1)
            nc.gpsimd.memset(map_scale, QSCALE).then_inc(s["zero_ready"], 1)
            nc.gpsimd.iota(iot[:, 0:1], pattern=[[0, 1]], base=0, channel_multiplier=1).then_inc(s["iota_ready"], 1)
            nc.gpsimd.iota(iot[:, 3:8], pattern=[[1, 5]], base=-1, channel_multiplier=0).then_inc(s["iota_ready"], 1)
            pool.wait_ge(s["zero_ready"], 4 + 5)
            nc.gpsimd.affine_select(out=mask_t[:, :], in_=mask_t[:, :], compare_op=ALU.is_ge, fill=NEG, base=0,
                                    pattern=[[1, P]], channel_multiplier=-1).then_inc(s["masks_ready"], 1)
            nc.gpsimd.affine_select(out=place_q[:, :, 28:32], in_=place_q[:, :, 28:32], compare_op=ALU.not_equal,
                                    fill=1.0, base=0, pattern=[[-32, H], [-1, STEPS]], channel_multiplier=1
                                    ).then_inc(s["masks_ready"], 1)
            nc.gpsimd.affine_select(out=seqmask[:, :], in_=seqmask[:, :], compare_op=ALU.is_ge, fill=0.0, base=0,
                                    pattern=[[-STEPS, NSEQ]], channel_multiplier=1).then_inc(s["masks_ready"], 1)
            pool.wait_ge(s["masks_ready"], 3)
            nc.gpsimd.affine_select(out=place_q[:, :, 28:32], in_=place_q[:, :, 28:32], compare_op=ALU.not_equal,
                                    fill=1.0, base=-STEPS, pattern=[[-32, H], [-1, STEPS]], channel_multiplier=1
                                    ).then_inc(s["masks_ready"], 1)
            nc.gpsimd.affine_select(out=seqmask[:, :], in_=seqmask[:, :], compare_op=ALU.is_ge, fill=0.0,
                                    base=STEPS - 1, pattern=[[STEPS, NSEQ]], channel_multiplier=-1
                                    ).then_inc(s["masks_ready"], 1)
            nc.gpsimd.affine_select(out=mask_s.rearrange("s (b t) -> s b t", t=STEPS),
                                    in_=mask_t[0:SMP, 0:SMP].rearrange("s (b t) -> s b t", t=STEPS),
                                    compare_op=ALU.is_ge, fill=NEG, base=0, pattern=[[-STEPS, NSEQ], [0, STEPS]],
                                    channel_multiplier=1).then_inc(s["masks_ready"], 1)

            nc.gpsimd.affine_select(out=map_scale[:, 0:1], in_=map_scale[:, 0:1], compare_op=ALU.is_ge, fill=0.0,
                                    base=63, pattern=[[0, 1]], channel_multiplier=-1).then_inc(s["masks_ready"], 1)
            nc.gpsimd.affine_select(out=map_scale[:, 1:2], in_=map_scale[:, 1:2], compare_op=ALU.is_ge, fill=0.0,
                                    base=-64, pattern=[[0, 1]], channel_multiplier=1).then_inc(s["masks_ready"], 1)

            pool.wait_ge(s["w_used"], 2 * NT)
            for z in (qmask, Ablk, AblkS, Dg, DgS, G, q8cur, Caug, AS, vaug):
                nc.gpsimd.memset(z[:], 1.0 if z is vaug else 0.0).then_inc(s["zero_ready"], 1)
            pool.wait_ge(s["zero_ready"], 4 + 5 + 10)
            pool.wait_ge(s["u_stored"], NT)
            pool.wait_ge(s["masks_ready"], 8)
            for m in range(2):
                for h in range(H):
                    nc.gpsimd.tensor_scalar(q8[:, :, h, 4 * m:4 * m + 4],
                                            U[:, QA + h, SEQ:TOK].rearrange("p (b t) -> p b t", t=STEPS),
                                            map_scale[:, m:m + 1], 0.0, ALU.mult, ALU.add).then_inc(s["q8_ready"], 1)
            pool.wait_ge(s["s_qk_stored"], 1)
            for b in range(NSEQ):
                nc.gpsimd.tensor_copy(qmask[:, b, :, STEPS * b:STEPS * (b + 1)], qbT[:, :, STEPS * b:STEPS * (b + 1)]
                                      ).then_inc(s["q8_ready"], 1)
            root(ss4[0:SMP, :], rs4[0:SMP, :], done["s_sq"], 10, "s_rs")

            pool.wait_ge(s["q8_ready"], 2 * H)

            def stream_pool(i):
                t0 = i * P
                if not (isinstance(i, int) and i == 0):
                    pool.wait_ge(s["scores_ready"], i * (GROUPS + 1))
                nc.gpsimd.tensor_copy(q8cur[:, :, 0:8], q8[:, bass.ds(i, 1), :, :].rearrange("p o h c -> p (o h) c")
                                      ).then_inc(s["q8cur_ready"], 1)
                pool.wait_ge(s["proj_ready"], 3 * i + 3)
                x = xch[:, :, bass.ds(t0, P)]
                nc.gpsimd.tensor_tensor(x, x, bc(skip, P), ALU.mult).then_inc(s["xsk_ready"], 1)
                pool.wait_ge(s["sqk_ready"], i + 1)
                nc.gpsimd.tensor_copy(kbT[:, :, :], U[:, OB:OB + H, bass.ds(t0, P)]).then_inc(s["ob_copied"], 1)
                root(ss4, rs4, (s["sq_ready"], i + 1), i + 11, "hrs_ready")

            stream_pool(0)
            with pool.Fori(1, CH) as i:
                stream_pool(i)

            root(ss4[:, 0:1], rs4[:, 0:1], done["as_norm"], 11 + CH, "as_hrs")

            pool.wait_ge(*done["as_done"])
            pool.wait_ge(s["out_state"], 48)
            nc.gpsimd.memset(mask_q[:, :], 0.0).then_inc(*signal["mask_q_zero"])
            pool.wait_ge(*done["mask_q_zero"])
            nc.gpsimd.affine_select(out=mask_q[:, :], in_=mask_q[:, :], compare_op=ALU.is_ge, fill=NEG, base=0,
                                    pattern=[[-1, P]], channel_multiplier=1).then_inc(*signal["mask_q_ready"])

            def queries(u):
                i, h = divmod(u, H)
                if u >= 3:
                    pool.wait_ge(s["sc1"], u - 2)
                for m in range(2):
                    nc.gpsimd.tensor_scalar(qz[:, u % 3, m, :], U[:, QA + h, i * P:(i + 1) * P],
                                            map_scale[:, m:m + 1], 0.0, ALU.mult, ALU.add).then_inc(s["qz_ready"], 1)

            queries(0)
            queries(1)
            queries(2)
            for u in range(CH * H):
                if u + 3 < CH * H:
                    queries(u + 3)
                root(st[:, u % 2, 4:5], st[:, u % 2, 5:6], (s["psq"], u + 1), 12 + CH + u, "prs")

            means = 11 + CH + CH * H
            for q in range(18):
                j, n = q % 9, XT[q % 9][1]
                root(sumsq[0:n, j:j + 1], rstd[0:n, j:j + 1], (s["row_sq"], q + 1), means + q + 1, "row_rs")

        @block.scalar
        def _(act):
            def store_hi(t):
                t0, n = XT[t]
                act.wait_ge(s["hT_ready"], t + 1)
                for b in range(2):
                    last = nc.scalar.activation(hhi[:, 4 * b:4 * b + 4, t0:t0 + n],
                                                ps[:, 2 * (t % 2) + b, :].rearrange("p (k t) -> p k t", k=4)[:, :, 0:n],
                                                ACT.Copy)
                last.then_inc(s["hhi_ready"], 1)

            for t, (t0, n) in enumerate(XT):
                act.wait_ge(x_in[t % 2], 16 * (t // 2 + 1))
                if t >= 1:
                    act.wait_ge(s["sumsq_ready"], t)
                nc.scalar.activation(square[0:n, :], xrow[0:n, t % 2, :], ACT.Square, scale=D ** -0.5,
                                     accum_out=sumsq[0:n, t:t + 1]).then_inc(s["sumsq_ready"], 1)
                if t >= 1:
                    store_hi(t - 1)
            store_hi(8)
            act.wait_ge(s["lam_sum"], 2)
            nc.scalar.activation(lam_e, lam_e, ACT.Exp).then_inc(*signal["lam_exp"])
            act.wait_ge(*done["vecT_ready"])
            nc.scalar.activation(vec, ps[:, 4, 0:32], ACT.Copy).then_inc(*signal["vec_ready"])

            def split(q, half, slot, arrived, wait=True):
                act.wait_ge(w_in[slot], arrived)
                if wait:
                    act.wait_ge(s["w_used"], q - 1)
                nc.scalar.activation(whi[:, half, :, :], wst[:, slot, :, :], ACT.Copy).then_inc(s["whi_ready"], 1)

            def store(n, tile, bank, fn):
                act.wait_ge(s["w_used"], 2 * n + 2)
                nc.scalar.activation(U[:, bass.ds(tile, 1), :].rearrange("p a (c t) -> p (a c) t", c=3),
                                     ps[:, bank:bank + 3, 0:THIRD], fn).then_inc(s["u_stored"], 1)

            for m in range(2):
                split(0, m, m, 16, False)
            act.wait_ge(*done["lam_ready"])
            n = 0
            for first, count, fn in SECTIONS:
                last_section = n + count == NT
                with act.Fori(n // 2, (n + count) // 2 - last_section) as pair:
                    b = pair * 2
                    split(2 * b + 2, 0, 2, pair * 16 + 16)
                    split(2 * b + 3, 1, 3, pair * 16 + 16)
                    store(b, b + (first - n), 0, fn)
                    split(2 * b + 4, 0, 0, pair * 16 + 32)
                    split(2 * b + 5, 1, 1, pair * 16 + 32)
                    store(b + 1, b + (1 + first - n), 3, fn)
                n += count
                if last_section:
                    split(2 * NT - 2, 0, 2, NT // 2 * 16)
                    split(2 * NT - 1, 1, 3, NT // 2 * 16)
                    store(NT - 2, first + count - 2, 0, fn)
                    store(NT - 1, first + count - 1, 3, fn)

            def copy(out, in_, name, fn=ACT.Copy, **more):
                nc.scalar.activation(out, in_, fn, **more).then_inc(*(s[name], 1) if name in s else signal[name])

            act.wait_ge(*done["hist_ready"])
            copy(xpad[:, :, :, 0:3], ps[:, 0, 0:96].rearrange("p (h b j) -> p h b j", h=H, b=NSEQ), "hist_stored")
            act.wait_ge(*done["krow_ready"])
            copy(kS[:, :], ps[0:SMP, 1, :], "krow_stored")
            act.wait_ge(*done["vrow_ready"])
            copy(vS[:, :], ps[0:SMP, 2, :], "vrow_stored")
            act.wait_ge(*done["xbrow_ready"])
            copy(xbS[:, :], ps[0:SMP, 3, :], "xbrow_stored")
            act.wait_ge(*done["last3_ready"])
            copy(xbP[:, :], ps[0:3, 4, :], "last3_stored")
            act.wait_ge(*done["nT_ready"])
            act.wait_ge(s["cs_in"], 32)
            copy(Cs[:, :, DH], ps[:, 5, 0:SMP], "n_stored")
            act.wait_ge(s["conv_step"], 4 * H)
            copy(xch[:, :, SEQ:TOK], xch[:, :, SEQ:TOK], "silu_ready", ACT.Silu)
            nc.scalar.preload_act_table_set("natural_log_exp_and_others")
            act.wait_ge(s["s_proj"], 1)
            copy(qbT[:, :, 0:SMP], ps[:, 6, 0:P].rearrange("p (h t) -> p h t", h=H), "s_qk_stored")
            act.wait_ge(s["s_proj"], 2)
            copy(kbT[:, :, 0:SMP], ps[:, 7, 0:P].rearrange("p (h t) -> p h t", h=H), "s_qk_stored", scale=KSCALE)
            act.wait_ge(s["s_kvtok"], 2)
            act.wait_ge(s["zero_ready"], 4 + 5 + 10)
            copy(vaug[0:SMP, :, 0:DH], ps[0:SMP, 3, :].rearrange("p (h d) -> p h d", h=H), "s_vaug")
            act.wait_ge(s["s_gate_step"], 7)
            copy(gs[:, 2, :], gs[:, 1, :], "s_gate_exp", ACT.Exp, scale=-1.0)
            act.wait_ge(s["s_gate_exp"], 1)
            copy(gs[:, 3, :], gs[:, 2, :], "s_gate_exp", ACT.Ln, bias=1.0)
            act.wait_ge(s["s_gate_step"], 15)
            copy(G[32:36, 0:SMP], gs[:, 4, :], "s_gate_exp", ACT.Exp)
            copy(G[64:68, 0:SMP], gs[:, 5, :], "s_gate_exp", ACT.Exp)
            copy(G[96:100, 0:SMP].rearrange("p (b t) -> p b t", t=STEPS), g5[:, 4, :, 1:5], "s_gate_exp", ACT.Exp, scale=-1.0)
            act.wait_ge(*done["s_GT"])
            copy(GT[0:SMP, :], ps[0:SMP, 5, 0:P], "s_gate_exp")
            copy(decS[:, :, :].rearrange("p h b -> p (h b)"), ps[:, 5, P:P + SMP], "s_gate_exp", ACT.Exp)
            act.wait_ge(*done["s_arg"])
            copy(E[0:SMP, :, 0:SMP], E[0:SMP, :, 0:SMP], "s_E", ACT.Exp)
            act.wait_ge(*done["s_inter"])
            act.wait_ge(s["s_gate_exp"], 7)
            for h in range(H):
                last = nc.scalar.activation(nd[0:SMP, h, :], ps[0:SMP, (7, 0)[h // 2], 129 * (h % 2):129 * (h % 2) + 129],
                                            ACT.Copy, scale=GT[0:SMP, 32 + h:33 + h])
            last.then_inc(*signal["s_nd_scaled"])
            act.wait_ge(*done["s_nrow"])
            copy(nout[:, :], ps[0:SMP, 5, 0:DH], "s_nout")
            act.wait_ge(s["s_h_gated"], 5)
            for h in range(H):
                last = nc.scalar.activation(E[0:SMP, h, :], nd[0:SMP, h, 0:DH], ACT.Square, scale=DH ** -0.5,
                                            accum_out=ss4[0:SMP, h:h + 1])
            last.then_inc(*signal["s_sq"])

            act.wait_ge(s["conv_step"], CONV_STEPS)
            for h in range(H):
                copy(xch[:, h, 0:SEQ], xch[:, h, 0:SEQ], "silu_ready", ACT.Silu)
            nc.scalar.preload_act_table_set("natural_log_exp_and_others")

            act.wait_ge(*done["s_bo"])

            def stream_act(i, first, last):
                G0 = i * GROUPS
                def keys(g):
                    if last:
                        return
                    act.wait_ge(s["k_used"], G0 + (g + 1))
                    if g >= 1:
                        act.wait_ge(s["scores_ready"], i * 9 + g)
                    elif not first:
                        act.wait_ge(s["scores_ready"], i * 9 - 1)
                    copy(kTs[:, 0:2, :], ps[:, 0, :].rearrange("p (h k) -> p h k", h=2), "kT_act")

                if not last:
                    act.wait_ge(s["proj_ready"], 3 * i + 1)
                    copy(qbT[:, :, :], ps[:, 4, :].rearrange("p (h t) -> p h t", h=H), "qk_stored")
                    act.wait_ge(s["proj_ready"], 3 * i + 2)
                    if not first:
                        act.wait_ge(s["obT_ready"], i)
                    copy(kbT[:, :, :], ps[:, 5, :].rearrange("p (h t) -> p h t", h=H), "qk_stored", scale=KSCALE)
                if not first:
                    for u in (0, 2, 4):
                        act.wait_ge(s["pT_ready"], (i - 1) * 5 + (u + 1))
                        if u < 4:
                            copy(pT[:, 4 * u:4 * u + 4, :].rearrange("p k (h r) -> p k h r", h=H),
                                 ps[:, 0, :].rearrange("p (k h r) -> p k h r", k=4, h=H)[:, :, :, 0:8], "pT_act")
                        else:
                            copy(pT[0:SMP, 16, :].rearrange("p (h r) -> p h r", h=H),
                                 ps[0:SMP, 0, 0:P].rearrange("p (h r) -> p h r", h=H)[:, :, 0:8], "pT_act")

                keys(0)
                keys(1)
                if not last:
                    act.wait_ge(s["kvtok_ready"], i + 1)
                    if not first:
                        act.wait_ge(s["cu_ready"], i)
                    copy(vaug[:, :, 0:DH], ps[:, 5, :].rearrange("p (h d) -> p h d", h=H), "vaug_stored")
                    act.wait_ge(s["gate_step"], i * 12 + 3)
                    copy(gat[:, 2, :], gat[:, 1, :], "gate_exp", ACT.Exp, scale=-1.0)
                    act.wait_ge(s["gate_exp"], 2 * i + 1)
                    copy(gat[:, 3, :], gat[:, 2, :], "gate_exp", ACT.Ln, bias=1.0)
                keys(2)
                keys(3)
                if not last:
                    act.wait_ge(s["gate_step"], i * 12 + 12)
                    copy(G[32:36, :], gat[:, 6, :], "rows_exp", ACT.Exp, bias=mcol[:, bass.ds(i, 1)])
                    copy(G[64:68, :], gat[:, 7, :], "rows_exp", ACT.Exp, bias=aL)
                    copy(G[96:100, :], gat[:, 4, :], "rows_exp", ACT.Exp, scale=-1.0)
                keys(4)
                if not last:
                    act.wait_ge(s["GT_ready"], i + 1)
                    copy(GT[:, :], ps[:, 7, 0:P], "gt_stored")
                    copy(dec4, ps[:, 7, P:P + H], "gt_stored", ACT.Exp)
                keys(5)
                if not last:
                    act.wait_ge(s["arg_ready"], i + 1)
                    copy(E[:, :, :], E[:, :, :], "E_ready", ACT.Exp)
                keys(6)
                if not last:
                    act.wait_ge(s["inter_ready"], i + 1)
                    if not first:
                        act.wait_ge(s["bo_done"], i)
                    for h in range(H):
                        lastop = nc.scalar.activation(nd[:, h, :], ps[:, 4 + h // 2, 129 * (h % 2):129 * (h % 2) + 129],
                                                      ACT.Copy, scale=GT[:, 32 + h:33 + h])
                    lastop.then_inc(s["nd_scaled"], 1)
                keys(7)
                if not first:
                    act.wait_ge(s["o_ready"], i)
                    act.wait_ge(s["coef_ready"], i)
                    if not (isinstance(i, int) and i == 1):
                        act.wait_ge(s["comb_ready"], i - 1)
                    copy(AO[:, :], ps[:, 3, 0:DH], "ao_ready", scale=coef[:, bass.ds(i - 1, 1)])
                if not last:
                    act.wait_ge(s["negmax_ready"], i + 1)
                    nc.scalar.activation(S[:, :], S[:, :], ACT.Exp, bias=negmax_s, accum_out=den_s[:, bass.ds(i, 1)]
                                         ).then_inc(s["p_ready"], 1)
                    act.wait_ge(s["h_gated"], i * 5 + 5)
                    for h in range(H):
                        lastop = nc.scalar.activation(E[:, h, :], nd[:, h, 0:DH], ACT.Square, scale=DH ** -0.5, accum_out=ss4[:, h:h + 1])
                    lastop.then_inc(s["sq_ready"], 1)

            stream_act(0, True, False)
            stream_act(1, False, False)
            with act.Fori(2, NSEQ) as i:
                stream_act(i, False, False)
            stream_act(NSEQ, False, True)

            act.wait_ge(*done["as_T_ready"])
            nc.scalar.activation(GT[:, :], ps[:, 4, 0:P], ACT.Square, scale=DH ** -0.5, accum_out=ss4[:, 0:1]).then_inc(*signal["as_norm"])
            act.wait_ge(*done["as_hrs"])
            copy(AO[:, :], ps[:, 4, 0:P], "as_n2", scale=rs4[:, 0:1])

            act.wait_ge(*done["as_done"])
            for t in range(CH):
                act.wait_ge(s["kt_ready"], t + 1)
                if t >= 2:
                    act.wait_ge(k_out[t % 2], 16 * (t // 2))
                copy(ktok[:, t % 2, :], ps[:, 2 * (t % 2), :], "kt_stored")

            def head_exp(u):
                i, h = divmod(u, H)
                n = (i + 1) * P
                for m in range(2):
                    act.wait_ge(s["rmax"], 2 * u + m + 1)
                    if u >= 2:
                        act.wait_ge(s["wT_ready"], WT_BEFORE[u - 1])
                    nc.scalar.activation(pp[:, u % 2, m, 0:n], score_row(u, m)[:, 0:n],
                                         ACT.Exp, bias=st[:, u % 2, m:m + 1], accum_out=st[:, u % 2, 2 + m:3 + m]
                                         ).then_inc(s["pexp"], 1)

            def weights_out(u):
                i, h = divmod(u, H)
                for c in range(0, i + 1, 4):
                    k = min(4, i + 1 - c)
                    act.wait_ge(s["wT_ready"], WT_BEFORE[u] + c // 4 + 1)
                    if u >= 1:
                        act.wait_ge(s["pv_ready"], u)
                    copy(wT[:, c:c + k, :], ps[:, 4 + (c // 4), 0:k * P].rearrange("p (k q) -> p k q", k=k), "wT_stored")

            def head_out(u):
                act.wait_ge(s["pv_ready"], u + 1)
                if u >= 2:
                    act.wait_ge(s["onT_ready"], u - 1)
                head = ps[:, head_bank(u), 0:DH]
                nc.scalar.activation(on[:, u % 2, :], head, ACT.Square, scale=DH ** -0.5, accum_out=st[:, u % 2, 4:5]
                                     ).then_inc(s["psq"], 1)
                act.wait_ge(s["prs"], u + 1)
                copy(on[:, u % 2, :], head, "on_ready", scale=st[:, u % 2, 5:6])

            head_exp(0)
            for u in range(CH * H):
                if u + 1 < NARROW:
                    head_exp(u + 1)
                weights_out(u)
                if NARROW <= u + 1 < CH * H:
                    head_exp(u + 1)
                head_out(u)

            act.wait_ge(s["a_done"], CH * H)
            act.wait_ge(s["tail_in"], 16 * 3)

            def cat_part(j):
                t0, n = XT[j]
                nc.scalar.activation(rh[:, 0:H, t0:t0 + n], U[:, ZA:ZA + H, t0:t0 + n], ACT.Copy)
                nc.scalar.activation(rh[:, H:2 * H, t0:t0 + n], U[:, ZB:ZB + H, t0:t0 + n], ACT.Copy).then_inc(s["cat_hi"], 1)

            def x1_part(j):
                t0, n = XT[j]
                act.wait_ge(s["x1T_ready"], j + 1)
                for b in range(2):
                    last = nc.scalar.activation(rh[:, 4 * b:4 * b + 4, t0:t0 + n],
                                                ps[:, 4 + b, :].rearrange("p (k t) -> p k t", k=4)[:, :, 0:n], ACT.Copy)
                last.then_inc(s["x1T_hi"], 1)

            def square_rows(q, src):
                n = XT[q % 9][1]
                if q >= 1:
                    act.wait_ge(s["row_sq"], q)
                nc.scalar.activation(junk[0:n, :], src, ACT.Square, scale=D ** -0.5,
                                     accum_out=sumsq[0:n, q % 9:q % 9 + 1]).then_inc(s["row_sq"], 1)

            cat_part(0)
            for k in range(KC):
                copy(wh[:, k, :], wout[:, k, :], "w_hi")
            cat_part(1)
            for j in range(9):
                act.wait_ge(s["y_ready"], j + 1)
                b = 2 * (j % 2)
                square_rows(j, ps[0:XT[j][1], b:b + 2, :].rearrange("p a b -> p (a b)"))
                if j + 2 < 9:
                    cat_part(j + 2)
                if j == 8:
                    act.wait_ge(s["wgate_in"], 16)
                    for k in range(KC):
                        copy(wh[:, k, :], wgate[:, k, :], "w_hi")
                x1_part(j)

            def p_store(j):
                n = XT[j][1]
                act.wait_ge(s["prow_T"], j + 1)
                if j >= 1:
                    act.wait_ge(s["pw_ready"], j)
                copy(pTt[:, :, 0:n], ps[:, 6, 0:2 * P].rearrange("p (k t) -> p k t", k=2)[:, :, 0:n], "prow_stored")

            p_store(0)
            for j in range(9):
                n, b = XT[j][1], 2 * ((j + 1) % 2)
                act.wait_ge(s["gate_ready"], j + 1)
                if j >= 1:
                    act.wait_ge(s["out_ready"], j)
                copy(sg[0:n, :], ps[0:n, b:b + 2, :].rearrange("p a b -> p (a b)"), "gate_sig", ACT.Sigmoid)
                if j + 1 < 9:
                    p_store(j + 1)
                act.wait_ge(s["t_done"], j + 1)
                square_rows(9 + j, sg[0:n, :])

        @block.vector
        def _(dve):
            dve.wait_ge(s["gpre_in"], 16)

            def store_lo(t):
                t0, n = XT[t]
                dve.wait_ge(s["hhi_ready"], t + 1)
                for b in range(2):
                    last = nc.vector.tensor_tensor(hlo[:, 4 * b:4 * b + 4, t0:t0 + n],
                                                   ps[:, 2 * (t % 2) + b, :].rearrange("p (k t) -> p k t", k=4)[:, :, 0:n],
                                                   hhi[:, 4 * b:4 * b + 4, t0:t0 + n].bitcast(F32), ALU.subtract)
                last.then_inc(s["hlo_ready"], 1)

            for t, (t0, n) in enumerate(XT):
                dve.wait_ge(s["rstd_ready"], t + 1)
                if t >= 2:
                    dve.wait_ge(s["hT_ready"], t - 1)
                nc.vector.scalar_tensor_tensor(out=hrow[0:n, t % 2, :], in0=xrow[0:n, t % 2, :],
                                               scalar=rstd[0:n, t:t + 1], in1=gpre[0:n, :],
                                               op0=ALU.mult, op1=ALU.mult).then_inc(s["h_ready"], 1)
                if t >= 1:
                    store_lo(t - 1)
            store_lo(8)

            dve.wait_ge(s["params_in"], 16 * PARAMS)
            for n in range(2):
                nc.vector.tensor_tensor_reduce(lamp[:, 64 * n:64 * n + 64], lamv[:, 128 * n:128 * n + 64],
                                               lamv[:, 128 * n + 64:128 * n + 128], 1.0, 0.0, ALU.mult, ALU.add,
                                               lam_e[:, n:n + 1]).then_inc(s["lam_sum"], 1)
            dve.wait_ge(s["iota_ready"], 2)
            nc.vector.tensor_scalar(iot[:, 1:2], iot[:, 0:1], 3, None, ALU.bitwise_and).then_inc(s["lam_sum"], 1)
            nc.vector.tensor_scalar(iot[:, 2:3], iot[:, 0:1], 4, None, ALU.bitwise_and).then_inc(s["lam_sum"], 1)
            dve.wait_ge(s["lam_sum"], 4)
            nc.vector.tensor_copy(iof[:, 0:8], iot[:, 0:8]).then_inc(s["lam_sum"], 1)
            dve.wait_ge(*done["lam_exp"])
            nc.vector.tensor_scalar(lam, lam_e[:, 0:1], lam_e[:, 1:2], LAM_INIT, ALU.subtract, ALU.add
                                    ).then_inc(s["lam_sum"], 1)
            dve.wait_ge(s["lam_sum"], 6)
            nc.vector.tensor_scalar(neg_lam, lam, -1.0, None, ALU.mult).then_inc(s["lam_sum"], 1)
            nc.vector.tensor_scalar(row_4, lam, 1.0, -0.25, ALU.add, ALU.mult).then_inc(s["lam_sum"], 1)
            dve.wait_ge(s["lam_sum"], 8)
            nc.vector.tensor_scalar(sign, iof[:, 2:3], row_4, 1.0, ALU.mult, ALU.add).then_inc(s["lam_sum"], 1)
            dve.wait_ge(s["masks_ready"], 6)
            nc.vector.tensor_scalar(mask_new[:, 28:32], iof[:, 4:8], iof[:, 1:2], NEG, ALU.is_gt, ALU.mult
                                    ).then_inc(*signal["lam_ready"])
            dve.wait_ge(*done["vec_ready"])
            nc.vector.tensor_scalar(ag, attn_g, 1.0 - LAM_INIT, None, ALU.mult).then_inc(s["ag_ready"], 1)
            nc.vector.memset(mcol[:, 0:1], 0.0).then_inc(s["ag_ready"], 1)

            def rest(q, half, slot):
                dve.wait_ge(s["whi_ready"], q + 1)
                nc.vector.tensor_tensor(wlo[:, half, :, :], wst[:, slot, :, :], whi[:, half, :, :].bitcast(F32),
                                        ALU.subtract).then_inc(s["wlo_ready"], 1)

            with dve.Fori(0, NT // 2) as pair:
                for n in range(4):
                    rest(pair * 4 + n, n % 2, n)

            dve.wait_ge(s["w_used"], 2 * NT)
            dve.wait_ge(s["u_stored"], NT)
            nc.vector.tensor_copy(xpad[:, :, :, 3:7], U[:, XB:XB + H, SEQ:TOK].rearrange("p h (b t) -> p h b t", t=STEPS)
                                  ).then_inc(*signal["xpad_new"])
            dve.wait_ge(*done["hist_stored"])
            dve.wait_ge(*done["xpad_new"])
            steps = 0
            for j in (3, 2, 1, 0):
                for h in range(H):
                    w = conv_w[:, 4 * j + h:4 * j + h + 1]
                    out = xch[:, h, SEQ:TOK].rearrange("p (b t) -> p b t", t=STEPS)
                    if j == 3:
                        nc.vector.tensor_scalar(out, xpad[:, h, :, 3:7], w, conv_b[:, h:h + 1], ALU.mult, ALU.add
                                                ).then_inc(s["conv_step"], 1)
                    else:
                        dve.wait_ge(s["conv_step"], steps - 3)
                        nc.vector.scalar_tensor_tensor(out=out, in0=xpad[:, h, :, j:j + 4], scalar=w, in1=out,
                                                       op0=ALU.mult, op1=ALU.add).then_inc(s["conv_step"], 1)
                    steps += 1

            def prompt_conv(first, last):
                for n in range(first, last):
                    j, h = 3 - n // H, n % H
                    w, back = conv_w[:, 4 * j + h:4 * j + h + 1], 3 - j
                    if j == 3:
                        nc.vector.tensor_scalar(xch[:, h, 0:SEQ], U[:, XB + h, 0:SEQ], w, conv_b[:, h:h + 1],
                                                ALU.mult, ALU.add).then_inc(s["conv_step"], 1)
                    else:
                        dve.wait_ge(s["conv_step"], 4 * H + n - 3)
                        nc.vector.scalar_tensor_tensor(out=xch[:, h, back:SEQ], in0=U[:, XB + h, 0:SEQ - back], scalar=w,
                                                       in1=xch[:, h, back:SEQ], op0=ALU.mult, op1=ALU.add
                                                       ).then_inc(s["conv_step"], 1)

            prompt_conv(0, 2)

            step = [0]

            def gstep(ins):
                step[0] += 1
                ins.then_inc(s["s_gate_step"], 1)

            def gwait(n):
                dve.wait_ge(s["s_gate_step"], n)

            gstep(nc.vector.memset(g5[:, 0, :, :], 0.0))
            gstep(nc.vector.memset(g5[:, 3, :, :], NEG))
            gstep(nc.vector.memset(g5[:, 2, :, :], 1.0))
            gwait(3)
            gstep(nc.vector.memset(g5[:, 2, :, 0:1], 0.0))
            dve.wait_ge(s["s_proj"], 3)
            nc.vector.tensor_copy(vbT[:, :, 0:SMP], ps[:, 0, 0:P].rearrange("p (h t) -> p h t", h=H)).then_inc(*signal["s_v_stored"])
            prompt_conv(2, 5)
            dve.wait_ge(*done["s_gates"])
            by_seq = lambda ap: ap.rearrange("p (b t) -> p b t", t=STEPS)
            gstep(nc.vector.tensor_scalar(g5[:, 1, :, 1:5], by_seq(ps[0:H, 1, 0:SMP]), bias_i, None, ALU.add))
            gstep(nc.vector.tensor_scalar(gs[:, 0, :], ps[32:32 + H, 1, 0:SMP], bias_f, None, ALU.add))
            gwait(6)
            gstep(nc.vector.scalar_tensor_tensor(out=gs[:, 1, :], in0=gs[:, 0, :], scalar=-1.0, in1=gs[:, 0, :],
                                                 op0=ALU.mult, op1=ALU.max))
            prompt_conv(5, 6)
            dve.wait_ge(s["s_gate_exp"], 2)
            gstep(nc.vector.scalar_tensor_tensor(out=g5[:, 3, :, 1:5], in0=by_seq(gs[:, 0, :]), scalar=0.0,
                                                 in1=by_seq(gs[:, 3, :]), op0=ALU.min, op1=ALU.subtract))
            gwait(8)
            gstep(nc.vector.tensor_copy(g5[:, 0, :, 1:5], g5[:, 3, :, 1:5]))
            gwait(9)
            dve.wait_ge(s["cs_in"], 32)
            flat = lambda r: g5[:, r, :, :].rearrange("p b t -> p (b t)")
            gstep(nc.vector.tensor_tensor_scan(flat(5), flat(2), flat(0), 0.0, ALU.mult, ALU.add))
            gstep(nc.vector.tensor_tensor_scan(flat(4), flat(3), flat(1), 0.0, ALU.add, ALU.max))
            gwait(11)
            gstep(nc.vector.tensor_tensor(flat(6), flat(5), flat(4), ALU.subtract))
            gstep(nc.vector.tensor_tensor(flat(7), flat(1), flat(5), ALU.subtract))
            gwait(13)
            gstep(nc.vector.tensor_tensor(by_seq(gs[:, 4, :]), g5[:, 6, :, 1:5], g5[:, 1, :, 0:1].broadcast_to([H, NSEQ, STEPS]),
                                          ALU.add))
            gstep(nc.vector.tensor_tensor(by_seq(gs[:, 5, :]), g5[:, 7, :, 1:5], g5[:, 6, :, 4:5].broadcast_to([H, NSEQ, STEPS]),
                                          ALU.add))
            dve.wait_ge(s["zero_ready"], 4 + 5 + 10)
            gstep(nc.vector.tensor_copy(by_seq(G[0:H, 0:SMP]), g5[:, 7, :, 1:5]))
            gstep(nc.vector.tensor_copy(by_seq(gs[:, 0, :]), g5[:, 6, :, 1:5]))
            gwait(17)
            gstep(nc.vector.tensor_tensor(AblkS[0:H, :, :], lead(gs[:, 0, :], H), bc(ident[0:H, 0:H], SMP), ALU.mult))
            gstep(nc.vector.tensor_tensor(DgS[0:H, :, :], lead(by_seq(gs[:, 4, :])[:, :, 3], H), bc(ident[0:H, 0:H], NSEQ),
                                          ALU.mult))
            prompt_conv(6, 7)
            dve.wait_ge(s["s_kvtok"], 2)
            dve.wait_ge(s["s_gate_exp"], 7)
            nc.vector.tensor_tensor(kw[0:SMP, :, :], ps[0:SMP, 2, :].rearrange("p (h d) -> p h d", h=H),
                                    bc(GT[0:SMP, 64:68], DH), ALU.mult).then_inc(*signal["s_kw"])
            dve.wait_ge(*done["s_AB"])
            for h in range(H):
                last = nc.vector.scalar_tensor_tensor(out=E[0:SMP, h, 0:SMP], in0=ps[0:SMP, 6, h * SMP:(h + 1) * SMP],
                                                      scalar=GT[0:SMP, h:h + 1], in1=mask_s[:, :], op0=ALU.add, op1=ALU.add)
            last.then_inc(*signal["s_arg"])
            prompt_conv(7, 8)
            dve.wait_ge(*done["s_E"])
            dve.wait_ge(*done["s_sqk"])
            nc.vector.tensor_tensor(E[0:SMP, :, 0:SMP], ps[0:SMP, 4, 0:P].rearrange("p (h t) -> p h t", h=H),
                                    E[0:SMP, :, 0:SMP], ALU.mult).then_inc(*signal["s_W"])
            dve.wait_ge(*done["s_kw"])

            def own_keys(b):
                nc.vector.tensor_scalar(kwm[:, b % 2, :, :], kw[0:SMP, :, :], seqmask[:, b:b + 1], None, ALU.mult
                                        ).then_inc(s["s_kwm"], 1)

            own_keys(0)
            own_keys(1)
            prompt_conv(8, 13)
            dve.wait_ge(*done["s_intra"])
            dve.wait_ge(*done["s_nd_scaled"])
            for n, bank in enumerate((3, 5)):
                half = nd[0:SMP, 2 * n:2 * n + 2, :].rearrange("p h d -> p (h d)")
                last = nc.vector.tensor_tensor(half, half, ps[0:SMP, bank, 0:258], ALU.add)
            last.then_inc(*signal["s_nd"])
            for b in range(NSEQ):
                dve.wait_ge(s["s_cu"], b + 1)
                for h in range(H):
                    bank = ((1, 2), (4, 6))[b % 2][h // 2]
                    c = Cs[:, H * b + h, :]
                    last = nc.vector.scalar_tensor_tensor(out=c, in0=c, scalar=decS[:, h, b:b + 1],
                                                          in1=ps[:, bank, 129 * (h % 2):129 * (h % 2) + 129],
                                                          op0=ALU.mult, op1=ALU.add)
                last.then_inc(s["s_C"], 1)
                if b + 2 < NSEQ:
                    own_keys(b + 2)

            def divide(n, step, base, nd_sem, nd_count, ob_sem, ob_count, bank):
                dve.wait_ge(nd_sem, nd_count)
                nc.vector.scalar_tensor_tensor(out=rd4[0:n, :], in0=nd[0:n, :, DH], scalar=-1.0, in1=GT[0:n, 96:100],
                                               op0=ALU.mult, op1=ALU.max).then_inc(step, 1)
                dve.wait_ge(step, base + 1)
                nc.vector.tensor_tensor(rd4[0:n, :], rd4[0:n, :], nd[0:n, :, DH], ALU.max).then_inc(step, 1)
                dve.wait_ge(step, base + 2)
                nc.vector.reciprocal(rd4[0:n, :], rd4[0:n, :]).then_inc(step, 1)
                dve.wait_ge(step, base + 3)
                nc.vector.tensor_tensor(nd[0:n, :, 0:DH], nd[0:n, :, 0:DH], bc(rd4[0:n, :], DH), ALU.mult).then_inc(step, 1)
                dve.wait_ge(step, base + 4)
                dve.wait_ge(ob_sem, ob_count)
                nc.vector.tensor_tensor(nd[0:n, :, 0:DH], nd[0:n, :, 0:DH],
                                        ps[0:n, bank, :].rearrange("p (h d) -> p h d", h=H), ALU.mult).then_inc(step, 1)

            prompt_conv(13, 4 * H)
            divide(SMP, s["s_h_gated"], 0, *done["s_nd"], *done["s_obT"], 7)
            dve.wait_ge(s["s_proj"], 2)
            for h in range(H):
                nc.vector.tensor_scalar(xch[:, h, SEQ:TOK], xch[:, h, SEQ:TOK], skip[:, h:h + 1], None, ALU.mult
                                        ).then_inc(s["s_bo_t"], 1)
            dve.wait_ge(*done["s_rs"])
            nc.vector.tensor_tensor(nd[0:SMP, :, 0:DH], nd[0:SMP, :, 0:DH], bc(rs4[0:SMP, :], DH), ALU.mult
                                    ).then_inc(*signal["s_hn"])
            dve.wait_ge(*done["s_hT"])
            dve.wait_ge(s["s_bo_t"], H)
            for h in range(H):
                nc.vector.scalar_tensor_tensor(out=AO[:, h * SMP:(h + 1) * SMP], in0=ps[:, 0, h * SMP:(h + 1) * SMP],
                                               scalar=mlstm_g[:, h:h + 1], in1=xch[:, h, SEQ:TOK],
                                               op0=ALU.mult, op1=ALU.add).then_inc(s["s_bo_t"], 1)
            dve.wait_ge(s["s_bo_t"], 2 * H)
            nc.vector.tensor_tensor(U[:, ZB:ZB + H, SEQ:TOK], U[:, ZB:ZB + H, SEQ:TOK],
                                    AO[:, :].rearrange("p (h t) -> p h t", h=H), ALU.mult).then_inc(*signal["s_bo"])

            nc.vector.memset(ps[:, 3, 0:DH], 0.0).then_inc(*signal["den_step"])

            def stream_dve(i, first, last):
                G0, t0 = i * GROUPS, i * P
                def keys(g):
                    if last:
                        return
                    dve.wait_ge(s["k_used"], G0 + (g + 1))
                    if g >= 1:
                        dve.wait_ge(s["scores_ready"], i * 9 + g)
                    elif not first:
                        dve.wait_ge(s["scores_ready"], i * 9 - 1)
                    nc.vector.tensor_copy(kTs[:, 2:4, :], ps[:, 1, :].rearrange("p (h k) -> p h k", h=2)
                                          ).then_inc(s["kT_dve"], 1)

                def scores(g):
                    if last:
                        return
                    dve.wait_ge(s["scores_ready"], i * 9 + (g + 1))
                    k = GP * PAGE
                    nc.vector.tensor_scalar(S[:, g * k:(g + 1) * k], ps[:, 2, 0:k], 1.0, LOWEST, ALU.mult, ALU.max,
                                            accum_out=gmax[:, g:g + 1]).then_inc(s["s_stored"], 1)

                if not last:
                    dve.wait_ge(s["proj_ready"], 3 * i + 3)
                    nc.vector.tensor_copy(vbT[:, :, :], ps[:, 6, :].rearrange("p (h t) -> p h t", h=H)
                                          ).then_inc(s["v_stored"], 1)
                if not first:
                    for u in (1, 3):
                        dve.wait_ge(s["pT_ready"], (i - 1) * 5 + (u + 1))
                        nc.vector.tensor_copy(pT[:, 4 * u:4 * u + 4, :].rearrange("p k (h r) -> p k h r", h=H),
                                              ps[:, 1, :].rearrange("p (k h r) -> p k h r", k=4, h=H)[:, :, :, 0:8]
                                              ).then_inc(s["pT_dve"], 1)

                keys(0)
                if not first:
                    dve.wait_ge(s["p_ready"], i)
                    den = coef[:, bass.ds(i - 1, 1)]
                    nc.vector.reciprocal(den, den_s[:, bass.ds(i - 1, 1)]).then_inc(s["soft_step"], 1)
                    dve.wait_ge(s["soft_step"], 2 * i)
                    nc.vector.tensor_scalar(den, den, sign, None, ALU.mult).then_inc(s["coef_ready"], 1)
                    dve.wait_ge(s["hrs_ready"], i)
                    nc.vector.tensor_tensor(nd[:, :, 0:DH], nd[:, :, 0:DH], bc(rs4, DH), ALU.mult).then_inc(s["hn_ready"], 1)
                keys(1)
                if not first:
                    dve.wait_ge(s["hTr_ready"], i)
                    dve.wait_ge(s["xsk_ready"], i)
                    for h in range(H):
                        lastop = nc.vector.scalar_tensor_tensor(out=nd[:, h, 0:P], in0=ps[:, 6, h * P:(h + 1) * P],
                                                                scalar=mlstm_g[:, h:h + 1],
                                                                in1=xch[:, h, bass.ds((i - 1) * P, P)],
                                                                op0=ALU.mult, op1=ALU.add)
                    lastop.then_inc(s["bo_t"], 1)
                    dve.wait_ge(s["bo_t"], i)
                    z = U[:, ZB:ZB + H, bass.ds((i - 1) * P, P)]
                    nc.vector.tensor_tensor(z, z, nd[:, :, 0:P], ALU.mult).then_inc(s["bo_done"], 1)
                scores(0)
                gs0 = i * 12
                if not last:
                    dve.wait_ge(s["gates_ready"], i + 1)
                    nc.vector.tensor_scalar(gat[:, 7, :], ps[0:H, 7, 0:P], bias_i, None, ALU.add).then_inc(s["gate_step"], 1)
                    nc.vector.tensor_scalar(gat[:, 0, :], ps[32:32 + H, 7, 0:P], bias_f, None, ALU.add
                                            ).then_inc(s["gate_step"], 1)
                    dve.wait_ge(s["gate_step"], gs0 + 2)
                    nc.vector.scalar_tensor_tensor(out=gat[:, 1, :], in0=gat[:, 0, :], scalar=-1.0, in1=gat[:, 0, :],
                                                   op0=ALU.mult, op1=ALU.max).then_inc(s["gate_step"], 1)
                keys(2)
                scores(1)
                if not last:
                    dve.wait_ge(s["gate_exp"], 2 * i + 2)
                    nc.vector.scalar_tensor_tensor(out=gat[:, 1, :], in0=gat[:, 0, :], scalar=0.0, in1=gat[:, 3, :],
                                                   op0=ALU.min, op1=ALU.subtract).then_inc(s["gate_step"], 1)
                    dve.wait_ge(s["gate_step"], gs0 + 4)
                    nc.vector.tensor_tensor_scan(gat[:, 5, :], ones[0:H, :], gat[:, 1, :], 0.0, ALU.mult, ALU.add
                                                 ).then_inc(s["gate_step"], 1)
                    nc.vector.tensor_tensor_scan(gat[:, 4, :], gat[:, 1, :], gat[:, 7, :], mcol[:, bass.ds(i, 1)],
                                                 ALU.add, ALU.max).then_inc(s["gate_step"], 1)
                    dve.wait_ge(s["gate_step"], gs0 + 6)
                    nc.vector.tensor_tensor(gat[:, 6, :], gat[:, 5, :], gat[:, 4, :], ALU.subtract).then_inc(s["gate_step"], 1)
                    nc.vector.tensor_tensor(gat[:, 7, :], gat[:, 7, :], gat[:, 5, :], ALU.subtract).then_inc(s["gate_step"], 1)
                    nc.vector.tensor_copy(mcol[:, bass.ds(i + 1, 1)], gat[:, 4, P - 1:P]).then_inc(s["gate_step"], 1)
                    dve.wait_ge(s["gate_step"], gs0 + 9)
                    if not first:
                        dve.wait_ge(s["AB_ready"], i)
                    nc.vector.tensor_tensor(Ablk[0:H, :, :], lead(gat[:, 6, :], H), bc(ident[0:H, 0:H], P), ALU.mult
                                            ).then_inc(s["gate_step"], 1)
                    nc.vector.tensor_copy(G[0:H, :], gat[:, 7, :]).then_inc(s["gate_step"], 1)
                    nc.vector.tensor_copy(aL, gat[:, 6, P - 1:P]).then_inc(s["gate_step"], 1)
                    dve.wait_ge(s["gate_step"], gs0 + 12)
                    nc.vector.tensor_scalar(Dg[0:H, :], ident[0:H, 0:H], aL, None, ALU.mult).then_inc(s["kw_ready"], 1)
                    dve.wait_ge(s["kw_ready"], 3 * i + 1)
                    nc.vector.scalar_tensor_tensor(out=Dg[0:H, :], in0=ident[0:H, 0:H], scalar=mcol[:, bass.ds(i, 1)],
                                                   in1=Dg[0:H, :], op0=ALU.mult, op1=ALU.add).then_inc(s["kw_ready"], 1)
                keys(3)
                scores(2)
                keys(4)
                scores(3)
                if not last:
                    dve.wait_ge(s["gt_stored"], 2 * i + 2)
                    nc.vector.tensor_tensor(kw[:, :, :], ps[:, 4, :].rearrange("p (h d) -> p h d", h=H), bc(GT[:, 64:68], DH),
                                            ALU.mult).then_inc(s["kw_ready"], 1)
                    dve.wait_ge(s["AB_ready"], i + 1)
                    for h in range(H):
                        lastop = nc.vector.scalar_tensor_tensor(out=E[:, h, :], in0=ps[:, 5, h * P:(h + 1) * P],
                                                                scalar=GT[:, h:h + 1], in1=mask_t[:, :],
                                                                op0=ALU.add, op1=ALU.add)
                    lastop.then_inc(s["arg_ready"], 1)
                keys(5)
                scores(4)
                if not last:
                    dve.wait_ge(s["E_ready"], i + 1)
                    nc.vector.tensor_tensor(E[:, :, :], ps[:, 6, :].rearrange("p (h t) -> p h t", h=H), E[:, :, :], ALU.mult
                                            ).then_inc(s["W_ready"], 1)
                keys(6)
                scores(5)
                if not last:
                    dve.wait_ge(s["intra_ready"], i + 1)
                    dve.wait_ge(s["nd_scaled"], i + 1)
                    for n in range(2):
                        half = nd[:, 2 * n:2 * n + 2, :].rearrange("p h d -> p (h d)")
                        lastop = nc.vector.tensor_tensor(half, half, ps[:, 6 + n, 0:258], ALU.add)
                    lastop.then_inc(s["nd_ready"], 1)
                keys(7)
                scores(6)
                if not last:
                    dve.wait_ge(s["cu_ready"], i + 1)
                    for h in range(H):
                        lastop = nc.vector.scalar_tensor_tensor(out=Caug[:, h, :], in0=Caug[:, h, :], scalar=dec4[:, h:h + 1],
                                                                in1=ps[:, 4 + h // 2, 129 * (h % 2):129 * (h % 2) + 129],
                                                                op0=ALU.mult, op1=ALU.add)
                    lastop.then_inc(s["C_done"], 1)
                    scores(7)
                    dve.wait_ge(s["scores_ready"], i * 9 + 9)
                    nc.vector.tensor_tensor(S[:, PAST:PAST + SMP], ps[:, 2, 0:SMP],
                                            mask_new[:, bass.ds(i * (-STEPS) + 28, SMP)], ALU.add).then_inc(s["s_stored"], 1)
                    dve.wait_ge(s["s_stored"], i * 9 + 9)
                    nc.vector.tensor_reduce(gmax[:, GROUPS:GROUPS + 1], S[:, PAST:PAST + SMP], AX.X, ALU.max
                                            ).then_inc(s["soft_step"], 1)
                    dve.wait_ge(s["soft_step"], 2 * i + 1)
                    nc.vector.tensor_reduce(negmax_s, gmax[:, :], AX.X, ALU.max, negate=True).then_inc(s["negmax_ready"], 1)
                    divide(P, s["h_gated"], i * 5, s["nd_ready"], i + 1, s["obT_ready"], i + 1, 6)
                if not first:
                    dve.wait_ge(s["comb_ready"], i)
                    nc.vector.tensor_tensor(AS[:, :], AS[:, :], ps[:, 2, 0:P], ALU.add).then_inc(s["as_added"], 1)

            stream_dve(0, True, False)
            stream_dve(1, False, False)
            with dve.Fori(2, NSEQ) as i:
                stream_dve(i, False, False)
            stream_dve(NSEQ, False, True)

            dve.wait_ge(*done["as_T2"])
            for h in range(H):
                z = U[:, ZA + h, SEQ:TOK]
                last = nc.vector.scalar_tensor_tensor(out=z, in0=ps[:, 5, h * SMP:(h + 1) * SMP], scalar=ag[:, h:h + 1],
                                                      in1=z, op0=ALU.mult, op1=ALU.mult)
            last.then_inc(*signal["as_done"])

            for t in range(CH):
                dve.wait_ge(s["vt_ready"], t + 1)
                nc.vector.tensor_copy(vtok[:, t, :], ps[:, 2 * (t % 2) + 1, :]).then_inc(s["vt_stored"], 1)

            def head_max(u):
                i, h = divmod(u, H)
                n = (i + 1) * P
                for m in range(2):
                    dve.wait_ge(s[("sc0", "sc1")[m]], u + 1)
                    row = score_row(u, m)
                    nc.vector.tensor_tensor(row[:, n - P:n], row[:, n - P:n], mask_q[:, :], ALU.add).then_inc(s["masked"], 1)
                    dve.wait_ge(s["masked"], 2 * u + m + 1)
                    nc.vector.tensor_reduce(st[:, u % 2, m:m + 1], row[:, 0:n], AX.X, ALU.max, negate=True
                                            ).then_inc(s["rmax"], 1)

            def head_weights(u):
                i, h = divmod(u, H)
                n = (i + 1) * P
                dve.wait_ge(s["pexp"], 2 * u + 2)
                nc.vector.reciprocal(st[:, u % 2, 2:4], st[:, u % 2, 2:4]).then_inc(s["w_step"], 1)
                dve.wait_ge(s["w_step"], 2 * u + 1)
                nc.vector.tensor_scalar(pp[:, u % 2, 1, 0:n], pp[:, u % 2, 1, 0:n], st[:, u % 2, 3:4], neg_lam,
                                        ALU.mult, ALU.mult).then_inc(s["w_step"], 1)
                dve.wait_ge(s["w_step"], 2 * u + 2)
                nc.vector.scalar_tensor_tensor(out=pp[:, u % 2, 0, 0:n], in0=pp[:, u % 2, 0, 0:n], scalar=st[:, u % 2, 2:3],
                                               in1=pp[:, u % 2, 1, 0:n], op0=ALU.mult, op1=ALU.add).then_inc(s["w_done"], 1)

            def head_gate(u):
                i, h = divmod(u, H)
                dve.wait_ge(s["onT_ready"], u + 1)
                z = U[:, ZA + h, i * P:(i + 1) * P]
                nc.vector.scalar_tensor_tensor(out=z, in0=ps[:, 7, 0:P], scalar=ag[:, h:h + 1], in1=z,
                                               op0=ALU.mult, op1=ALU.mult).then_inc(s["a_done"], 1)

            dve.wait_ge(*done["mask_q_ready"])
            head_max(0)
            for u in range(CH * H):
                if u + 1 < NARROW:
                    head_max(u + 1)
                head_weights(u)
                if NARROW <= u + 1 < CH * H:
                    head_max(u + 1)
                if u >= 1:
                    head_gate(u - 1)
            head_gate(CH * H - 1)

            dve.wait_ge(s["tail_in"], 16 * 3)

            def low(out, whole, high):
                return nc.vector.tensor_tensor(out, whole, high.bitcast(F32), ALU.subtract)

            def cat_rest(j):
                t0, n = XT[j]
                dve.wait_ge(s["cat_hi"], j + 1)
                for b, tile in enumerate((ZA, ZB)):
                    z = U[:, tile:tile + H, t0:t0 + n]
                    last = low(rl[b][:, :, t0:t0 + n], z, rh[:, 4 * b:4 * b + 4, t0:t0 + n])
                last.then_inc(s["cat_lo"], 1)

            def x1_rest(j):
                t0, n = XT[j]
                dve.wait_ge(s["x1T_hi"], j + 1)
                for b in range(2):
                    last = low(rl[b][:, :, t0:t0 + n], ps[:, 4 + b, :].rearrange("p (k t) -> p k t", k=4)[:, :, 0:n],
                               rh[:, 4 * b:4 * b + 4, t0:t0 + n])
                last.then_inc(s["x1T_lo"], 1)

            def weights_rest(w, lo, before):
                for k in range(KC):
                    dve.wait_ge(s["w_hi"], before + k + 1)
                    low(lo[:, k, :], w[:, k, :], wh[:, k, :]).then_inc(s["w_lo"], 1)

            cat_rest(0)
            weights_rest(wout, wout_lo, 0)
            cat_rest(1)
            for j in range(9):
                n, b = XT[j][1], 2 * (j % 2)
                x = rows[0:n, j % 3, :]
                dve.wait_ge(s["row_rs"], j + 1)
                dve.wait_ge(row_in[j % 3], 16 * (j // 3 + 1))
                if j >= 1:
                    dve.wait_ge(s["y_x"], j)
                nc.vector.scalar_tensor_tensor(out=sg[0:n, :], in0=ps[0:n, b:b + 2, :].rearrange("p a b -> p (a b)"),
                                               scalar=rstd[0:n, j:j + 1], in1=gpost[0:n, :], op0=ALU.mult, op1=ALU.mult
                                               ).then_inc(s["row_step"], 1)
                dve.wait_ge(s["row_step"], j + 1)
                nc.vector.tensor_tensor(x, x, sg[0:n, :], ALU.add).then_inc(s["y_x"], 1)
                if j + 2 < 9:
                    cat_rest(j + 2)
                if j == 8:
                    weights_rest(wgate, wgate_lo, KC)
                x1_rest(j)
            for j in range(9):
                n, q = XT[j][1], 9 + j
                x = rows[0:n, q % 3, :]
                dve.wait_ge(s["gple_in"], 16)
                dve.wait_ge(s["gate_sig"], j + 1)
                dve.wait_ge(s["pw_ready"], j + 1)
                nc.vector.tensor_tensor(sg[0:n, :], sg[0:n, :], ps[0:n, 4:6, :].rearrange("p a b -> p (a b)"), ALU.mult
                                        ).then_inc(s["t_done"], 1)
                dve.wait_ge(s["row_rs"], q + 1)
                nc.vector.scalar_tensor_tensor(out=sg[0:n, :], in0=sg[0:n, :], scalar=rstd[0:n, j:j + 1], in1=gple[0:n, :],
                                               op0=ALU.mult, op1=ALU.mult).then_inc(s["row_step"], 1)
                dve.wait_ge(s["row_step"], q + 1)
                dve.wait_ge(row_in[q % 3], 16 * (q // 3 + 1))
                nc.vector.tensor_tensor(x, x, sg[0:n, :], ALU.add).then_inc(s["out_ready"], 1)

        @block.tensor
        def _(pe):
            pe.wait_ge(*done["ident_ready"])
            for t, (t0, n) in enumerate(XT):
                pe.wait_ge(s["h_ready"], t + 1)
                if t >= 2:
                    pe.wait_ge(s["hlo_ready"], t - 1)
                for k in range(KC):
                    last = nc.tensor.transpose(ps[:, 2 * (t % 2) + k // 4, (k % 4) * P:(k % 4) * P + n],
                                               hrow[0:n, t % 2, k * P:(k + 1) * P], ident[0:n, 0:n])
                last.then_inc(s["hT_ready"], 1)
            pe.wait_ge(s["params_in"], 16 * PARAMS)
            nc.tensor.transpose(ps[:, 4, 0:32], vrow[0:32, :], ident[0:32, 0:32]).then_inc(*signal["vecT_ready"])
            pe.wait_ge(s["hlo_ready"], 9)
            pe.wait_ge(*done["vec_ready"])

            def multiply(q, half, bank):
                pe.wait_ge(s["wlo_ready"], q + 1)
                for k in range(4):
                    kc = 4 * half + k
                    for w, h in ((whi, hhi), (whi, hlo), (wlo, hhi)):
                        for c in range(3):
                            last = nc.tensor.matmul(ps[:, bank + c, 0:THIRD], w[:, half, k, :],
                                                    h[:, kc, c * THIRD:(c + 1) * THIRD],
                                                    start=(kc == 0 and w is whi and h is hhi),
                                                    stop=(kc == KC - 1 and w is wlo))
                last.then_inc(s["w_used"], 1)

            def tiles(b, first):
                for m in range(2):
                    if not first:
                        pe.wait_ge(s["u_stored"], b + (m - 1))
                    for hf in range(2):
                        multiply(2 * b + (2 * m + hf), hf, 3 * m)

            tiles(0, True)
            with pe.Fori(1, NT // 2) as pair:
                tiles(pair * 2, False)

            def mm(out, lhsT, rhs, start=True, stop=True):
                return nc.tensor.matmul(out, lhsT, rhs, start=start, stop=stop)

            def turn(out, in_, name=None):
                ins = nc.tensor.transpose(out, in_, ident[0:in_.shape[0], 0:in_.shape[0]])
                if name:
                    ins.then_inc(*(s[name], 1) if name in s else signal[name])
                return ins

            pe.wait_ge(s["u_stored"], NT)
            for bank, tile, t0, n, name in ((1, KA, SEQ, SMP, "krow_ready"), (2, VA, SEQ, SMP, "vrow_ready"),
                                            (3, XB, SEQ, SMP, "xbrow_ready"), (4, XB, SEQ - 3, 3, "last3_ready")):
                for h in range(H):
                    last = turn(ps[0:n, bank, h * P:(h + 1) * P], U[:, tile + h, t0:t0 + n])
                last.then_inc(*signal[name])
            pe.wait_ge(s["hist_in"], 32)
            for h in range(H):
                last = turn(ps[:, 0, h * 24:(h + 1) * 24], crow[:, h * P:(h + 1) * P])
            last.then_inc(*signal["hist_ready"])
            pe.wait_ge(s["hist_in"], 32)
            turn(ps[:, 5, 0:SMP], nrow[:, :], "nT_ready")
            pe.wait_ge(s["wqkv_in"], 48)
            pe.wait_ge(s["silu_ready"], 1)
            pe.wait_ge(*done["hist_stored"])
            for j, bank in enumerate((6, 7, 0)):
                for h in range(H):
                    src = U[:, XB + h, SEQ:TOK] if j == 2 else xch[:, h, SEQ:TOK]
                    last = mm(ps[:, bank, h * SMP:(h + 1) * SMP], wqkv[:, j, h, :], src)
                last.then_inc(s["s_proj"], 1)
            pe.wait_ge(s["s_qk_stored"], 2)
            pe.wait_ge(*done["s_v_stored"])
            pe.wait_ge(s["wif_in"], 16)
            pe.wait_ge(*done["krow_stored"])
            for c in range(12):
                for n in range(2):
                    last = mm(ps[32 * n:32 * n + H, 1, 0:SMP], wif[:, c, H * n:H * n + H], (qbT, kbT, vbT)[c % 3][:, c // 3, 0:SMP],
                              c == 0, c == 11)
            last.then_inc(*signal["s_gates"])
            for bank, buf, name in ((2, kbT, "vrow_stored"), (3, vbT, "xbrow_stored")):
                pe.wait_ge(*done[name])
                for h in range(H):
                    last = turn(ps[0:SMP, bank, h * P:(h + 1) * P], buf[:, h, 0:SMP])
                last.then_inc(s["s_kvtok"], 1)
            pe.wait_ge(*done["last3_stored"])
            for h in range(H):
                last = mm(ps[0:SMP, 4, h * SMP:(h + 1) * SMP], kbT[:, h, 0:SMP], qbT[:, h, 0:SMP])
            last.then_inc(*signal["s_sqk"])
            pe.wait_ge(s["s_gate_exp"], 5)
            pe.wait_ge(s["s_gate_step"], 19)
            pe.wait_ge(*done["n_stored"])
            turn(ps[0:SMP, 5, 0:P], G[:, 0:SMP])
            mm(ps[:, 5, P:P + SMP], ones[:, :], DgS[:, :, :].rearrange("p h b -> p (h b)")).then_inc(*signal["s_GT"])
            mm(ps[0:SMP, 6, 0:P], ones[:, 0:SMP], AblkS[:, :, :].rearrange("p h t -> p (h t)")).then_inc(*signal["s_AB"])
            pe.wait_ge(s["q8_ready"], 2 * H + NSEQ)
            pe.wait_ge(s["cs_in"], 32)
            for h in range(H):
                for b in range(NSEQ):
                    last = mm(ps[0:SMP, (7, 0)[h // 2], 129 * (h % 2):129 * (h % 2) + 129], qmask[:, b, h, :],
                              Cs[:, H * b + h, :], b == 0, b == NSEQ - 1)
            last.then_inc(*signal["s_inter"])
            pe.wait_ge(*done["s_W"])
            pe.wait_ge(*done["s_vaug"])
            pe.wait_ge(s["s_gate_exp"], 7)
            for h in range(H):
                last = mm(ps[0:SMP, (3, 5)[h // 2], 129 * (h % 2):129 * (h % 2) + 129], E[0:SMP, h, 0:SMP], vaug[0:SMP, h, :])
            last.then_inc(*signal["s_intra"])
            pe.wait_ge(*done["s_nd_scaled"])
            for h in range(H):
                last = turn(ps[0:SMP, 7, h * P:(h + 1) * P], U[:, OB + h, SEQ:TOK])
            last.then_inc(*signal["s_obT"])
            for b in range(NSEQ):
                pe.wait_ge(s["s_kwm"], b + 1)
                if b >= 2:
                    pe.wait_ge(s["s_C"], b - 1)
                for h in range(H):
                    last = mm(ps[:, ((1, 2), (4, 6))[b % 2][h // 2], 129 * (h % 2):129 * (h % 2) + 129],
                              kwm[:, b % 2, h, :], vaug[0:SMP, h, :])
                last.then_inc(s["s_cu"], 1)
            pe.wait_ge(*done["s_nd"])
            pe.wait_ge(s["s_C"], NSEQ)
            turn(ps[0:SMP, 5, 0:DH], Cs[:, :, DH], "s_nrow")
            pe.wait_ge(*done["s_hn"])
            for h in range(H):
                last = turn(ps[:, 0, h * SMP:(h + 1) * SMP], nd[0:SMP, h, 0:DH])
            last.then_inc(*signal["s_hT"])

            pe.wait_ge(*done["s_bo"])
            pe.wait_ge(s["silu_ready"], 1 + H)
            pe.wait_ge(*done["s_nout"])
            pe.wait_ge(*done["den_step"])

            def stream_pe(i, first, last):
                G0, t0 = i * GROUPS, i * P
                def turn_weights():
                    pe.wait_ge(s["p_ready"], i)
                    for u in range(5):
                        if u == 0:
                            pe.wait_ge(s["kT_act"], G0)
                        elif u == 1:
                            pe.wait_ge(s["kT_dve"], G0)
                        elif u == 3:
                            pe.wait_ge(s["pT_dve"], (i - 1) * 2 + 1)
                        else:
                            pe.wait_ge(s["pT_act"], (i - 1) * 3 + u // 2)
                        if u < 4:
                            for k in range(4):
                                ins = turn(ps[:, u % 2, k * P:(k + 1) * P], S[:, (4 * u + k) * P:(4 * u + k + 1) * P])
                        else:
                            ins = turn(ps[0:SMP, 0, 0:P], S[:, PAST:PAST + SMP])
                        ins.then_inc(s["pT_ready"], 1)

                def unit(g):
                    if not last:
                        pe.wait_ge(k_in[g % 4], i * 64 + (g // 4 + 1) * 32)
                        if g == 0:
                            if not first:
                                pe.wait_ge(s["pT_act"], i * 3)
                                pe.wait_ge(s["pT_dve"], i * 2)
                        else:
                            pe.wait_ge(s["kT_act"], G0 + g)
                            pe.wait_ge(s["kT_dve"], G0 + g)
                        for h in range(H):
                            for n in range(GP):
                                ins = turn(ps[:, h // 2, ((h % 2) * GP + n) * P:((h % 2) * GP + n + 1) * P],
                                           Kr[:, (GP * g + n) % 8, h * P:(h + 1) * P])
                        ins.then_inc(s["k_used"], 1)
                    if g >= 1:
                        scores(g - 1)
                    if not first:
                        pe.wait_ge(v_in[g % 2], (i - 1) * 128 + (g // 2 + 1) * 32)
                        if g == 0:
                            pe.wait_ge(s["pT_act"], i * 3)
                            pe.wait_ge(s["pT_dve"], i * 2)
                            if not (isinstance(i, int) and i == 1):
                                pe.wait_ge(s["ao_ready"], i - 1)
                        for n in range(GP):
                            k = GP * g + n
                            for h in range(H):
                                ins = mm(ps[32 * h:32 * h + 8, 3, 0:DH], pT[:, k, 8 * h:8 * h + 8],
                                         Vr[:, k % 4, h * DH:(h + 1) * DH], k == 0, False)
                        ins.then_inc(s["v_used"], 1)

                def scores(g):
                    if last:
                        return
                    if g < GROUPS:
                        pe.wait_ge(s["kT_act"], G0 + (g + 1))
                        pe.wait_ge(s["kT_dve"], G0 + (g + 1))
                    if g == 0:
                        pe.wait_ge(s["q8cur_ready"], i + 1)
                        if not first:
                            pe.wait_ge(s["s_stored"], i * 9)
                            if not (isinstance(i, int) and i == 1):
                                pe.wait_ge(s["as_added"], i - 1)
                    else:
                        pe.wait_ge(s["s_stored"], i * 9 + g)
                    for h in range(H):
                        keys = kTs[:, h, :] if g < GROUPS else U[:, KA + h, SEQ:TOK]
                        ins = mm(ps[32 * h:32 * h + 32, 2, 0:keys.shape[1]], q8cur[:, h, :], keys)
                    ins.then_inc(s["scores_ready"], 1)

                def project():
                    if not first:
                        pe.wait_ge(s["C_done"], i)
                    for j in range(3):
                        if j == 2 and not first:
                            pe.wait_ge(s["h_gated"], i * 5)
                        for h in range(H):
                            src = U[:, XB + h, bass.ds(t0, P)] if j == 2 else xch[:, h, bass.ds(t0, P)]
                            ins = mm(ps[:, 4 + j, h * P:(h + 1) * P], wqkv[:, j, h, :], src)
                        ins.then_inc(s["proj_ready"], 1)

                def gates():
                    pe.wait_ge(s["qk_stored"], 2 * i + 2)
                    pe.wait_ge(s["v_stored"], i + 1)
                    for c in range(12):
                        for n in range(2):
                            ins = mm(ps[32 * n:32 * n + H, 7, 0:P], wif[:, c, H * n:H * n + H], (qbT, kbT, vbT)[c % 3][:, c // 3, :],
                                      c == 0, c == 11)
                    ins.then_inc(s["gates_ready"], 1)
                    for bank, buf in ((4, kbT), (5, vbT)):
                        for h in range(H):
                            ins = turn(ps[:, bank, h * P:(h + 1) * P], buf[:, h, :])
                    ins.then_inc(s["kvtok_ready"], 1)
                    if not first:
                        pe.wait_ge(s["bo_done"], i)
                    for h in range(H):
                        ins = mm(ps[:, 6, h * P:(h + 1) * P], kbT[:, h, :], qbT[:, h, :])
                    ins.then_inc(s["sqk_ready"], 1)

                def rows():
                    pe.wait_ge(s["rows_exp"], 3 * i + 3)
                    pe.wait_ge(s["kw_ready"], 3 * i + 2)
                    turn(ps[:, 7, 0:P], G[:, :])
                    mm(ps[:, 7, P:P + H], ones[:, :], Dg[:, :]).then_inc(s["GT_ready"], 1)
                    pe.wait_ge(s["vaug_stored"], i + 1)
                    mm(ps[:, 5, :], ones[:, :], Ablk[:, :, :].rearrange("p h t -> p (h t)")).then_inc(s["AB_ready"], 1)

                def products():
                    pe.wait_ge(s["kw_ready"], 3 * i + 3)
                    pe.wait_ge(s["arg_ready"], i + 1)
                    if not first:
                        pe.wait_ge(s["C_done"], i)
                    for h in range(H):
                        ins = mm(ps[:, 4 + h // 2, 129 * (h % 2):129 * (h % 2) + 129], qbT[:, h, :], Caug[:, h, :])
                    ins.then_inc(s["inter_ready"], 1)
                    pe.wait_ge(s["W_ready"], i + 1)
                    pe.wait_ge(s["gt_stored"], 2 * i + 2)
                    for h in range(H):
                        ins = mm(ps[:, 6 + h // 2, 129 * (h % 2):129 * (h % 2) + 129], E[:, h, :], vaug[:, h, :])
                    ins.then_inc(s["intra_ready"], 1)

                def update():
                    pe.wait_ge(s["nd_scaled"], i + 1)
                    for h in range(H):
                        ins = mm(ps[:, 4 + h // 2, 129 * (h % 2):129 * (h % 2) + 129], kw[:, h, :], vaug[:, h, :])
                    ins.then_inc(s["cu_ready"], 1)
                    pe.wait_ge(s["nd_ready"], i + 1)
                    pe.wait_ge(s["ob_copied"], i + 1)
                    for h in range(H):
                        ins = turn(ps[:, 6, h * P:(h + 1) * P], kbT[:, h, :])
                    ins.then_inc(s["obT_ready"], 1)

                def finish():
                    pe.wait_ge(s["hn_ready"], i)
                    if last:
                        pe.wait_ge(s["h_gated"], i * 5)
                    else:
                        pe.wait_ge(s["v_stored"], i + 1)
                    for h in range(H):
                        ins = turn(ps[:, 6, h * P:(h + 1) * P], nd[:, h, 0:DH])
                    ins.then_inc(s["hTr_ready"], 1)

                if not last:
                    project()
                if not first:
                    turn_weights()
                unit(0)
                if not first:
                    finish()
                unit(1)
                if not last:
                    gates()
                unit(2)
                unit(3)
                unit(4)
                if not last:
                    rows()
                unit(5)
                unit(6)
                if not last:
                    products()
                unit(7)
                if not first:
                    for h in range(H):
                        ins = mm(ps[32 * h:32 * h + 8, 3, 0:DH], pT[0:SMP, 16, 8 * h:8 * h + 8],
                                 vS[:, h * DH:(h + 1) * DH], False, True)
                    ins.then_inc(s["o_ready"], 1)
                if not last:
                    update()
                scores(7)
                scores(8)
                if not first:
                    pe.wait_ge(s["ao_ready"], i)
                    if not last:
                        pe.wait_ge(s["s_stored"], i * 9 + 9)
                    if not (isinstance(i, int) and i == 1):
                        pe.wait_ge(s["as_added"], i - 1)
                    mm(ps[:, 2, 0:P].rearrange("p (h t) -> p h t", h=H), AO[:, :],
                       place_q[:, :, bass.ds((i - 1) * (-STEPS) + 28, SMP)]).then_inc(s["comb_ready"], 1)

            stream_pe(0, True, False)
            stream_pe(1, False, False)
            with pe.Fori(2, NSEQ) as i:
                stream_pe(i, False, False)
            stream_pe(NSEQ, False, True)

            pe.wait_ge(s["as_added"], NSEQ)
            turn(ps[:, 4, 0:P], AS[:, :], "as_T_ready")
            pe.wait_ge(*done["as_n2"])
            turn(ps[:, 5, 0:P], AO[:, :], "as_T2")

            pe.wait_ge(*done["as_done"])
            pe.wait_ge(s["out_state"], 48)
            for t in range(CH):
                if t >= 2:
                    pe.wait_ge(s["kt_stored"], t - 1)
                for h in range(H):
                    last = turn(ps[:, 2 * (t % 2), h * P:(h + 1) * P], U[:, KA + h, t * P:(t + 1) * P])
                last.then_inc(s["kt_ready"], 1)
                if t >= 2:
                    pe.wait_ge(s["vt_stored"], t - 1)
                for h in range(H):
                    last = turn(ps[:, 2 * (t % 2) + 1, h * P:(h + 1) * P], U[:, VA + h, t * P:(t + 1) * P])
                last.then_inc(s["vt_ready"], 1)
            pe.wait_ge(s["kt_stored"], CH)
            pe.wait_ge(s["vt_stored"], CH)

            def head_scores(u):
                i, h = divmod(u, H)
                n = (i + 1) * P
                for m in range(2):
                    pe.wait_ge(s["qz_ready"], 2 * u + m + 1)
                    if u >= NARROW:
                        pe.wait_ge(s["pexp"], 2 * u - 1 + m)
                    elif u >= 2:
                        pe.wait_ge(s["pexp"], 2 * u - 3 + m)
                    for c in range(0, n, 512):
                        k = min(512, n - c)
                        last = mm(score_row(u, m)[:, c:c + k], qz[:, u % 3, m, :], U[:, KA + h, c:c + k])
                    last.then_inc(s[("sc0", "sc1")[m]], 1)

            def head_turn(u):
                i, h = divmod(u, H)
                pe.wait_ge(s["w_done"], u + 1)
                if u == NARROW:
                    pe.wait_ge(s["on_ready"], u - 1)
                for c in range(0, i + 1, 4):
                    if c == 4 or u >= 1:
                        pe.wait_ge(s["wT_stored"], WT_BEFORE[u])
                    for k in range(c, min(c + 4, i + 1)):
                        last = turn(ps[:, 4 + c // 4, (k - c) * P:(k - c + 1) * P], pp[:, u % 2, 0, k * P:(k + 1) * P])
                    last.then_inc(s["wT_ready"], 1)

            def head_values(u):
                i, h = divmod(u, H)
                pe.wait_ge(s["wT_stored"], WT_BEFORE[u + 1])
                if u >= 2:
                    pe.wait_ge(s["on_ready"], u - (u < NARROW))
                for k in range(i + 1):
                    last = mm(ps[:, head_bank(u), 0:DH], wT[:, k, :], vtok[:, k, h * DH:(h + 1) * DH], k == 0, k == i)
                last.then_inc(s["pv_ready"], 1)

            def head_back(u):
                pe.wait_ge(s["on_ready"], u + 1)
                if u >= 1:
                    pe.wait_ge(s["a_done"], u)
                turn(ps[:, 7, 0:P], on[:, u % 2, :], "onT_ready")

            head_scores(0)
            head_scores(1)
            for u in range(CH * H):
                if u + 2 < NARROW:
                    head_scores(u + 2)
                elif NARROW <= u + 1 < CH * H:
                    head_scores(u + 1)
                head_turn(u)
                head_values(u)
                if u >= 1:
                    head_back(u - 1)
            head_back(CH * H - 1)

            def by_weights(j, bank, w, fresh, name):
                t0, n = XT[j]
                for k in range(KC):
                    if fresh is not None:
                        pe.wait_ge(s["w_lo"], fresh + k + 1)
                    hi = rh[:, k, t0:t0 + n]
                    lo = rl[k // H][:, k % H, t0:t0 + n]
                    w_hi, w_lo = wh[:, k, :], w[:, k, :]
                    for step, (part, weights) in enumerate(((hi, w_hi), (hi, w_lo), (lo, w_hi))):
                        for c in range(2):
                            last = mm(ps[0:n, bank + c, :], part, weights[:, c * 512:(c + 1) * 512],
                                      k == 0 and step == 0, k == KC - 1 and step == 2)
                last.then_inc(s[name], 1)

            def project_out(j):
                pe.wait_ge(s["cat_lo"], j + 1)
                if j == 0:
                    pe.wait_ge(s["a_done"], CH * H)
                if j >= 2:
                    pe.wait_ge(s["row_step"], j - 1)
                by_weights(j, 2 * (j % 2), wout_lo, 0 if j == 0 else None, "y_ready")

            def turn_x1(j):
                n = XT[j][1]
                pe.wait_ge(s["y_x"], j + 1)
                if j >= 1:
                    pe.wait_ge(s["x1T_lo"], j)
                for k in range(KC):
                    last = turn(ps[:, 4 + k // 4, (k % 4) * P:(k % 4) * P + n], rows[0:n, j % 3, k * P:(k + 1) * P])
                last.then_inc(s["x1T_ready"], 1)

            def turn_p(j):
                n = XT[j][1]
                pe.wait_ge(pr_in, 16 * (j + 1))
                if j >= 1:
                    pe.wait_ge(s["prow_stored"], j)
                for k in range(2):
                    last = turn(ps[:, 6, k * P:k * P + n], prow[0:n, k * P:(k + 1) * P])
                last.then_inc(s["prow_T"], 1)

            def gate(j):
                pe.wait_ge(s["x1T_lo"], j + 1)
                if j < 2:
                    pe.wait_ge(s["row_step"], 8 + j)
                else:
                    pe.wait_ge(s["gate_sig"], j - 1)
                by_weights(j, 2 * ((j + 1) % 2), wgate_lo, KC if j == 0 else None, "gate_ready")

            def embed(j):
                n = XT[j][1]
                pe.wait_ge(s["prow_stored"], j + 1)
                pe.wait_ge(s["tail_in"], 16 * 3)
                if j == 0:
                    pe.wait_ge(s["x1T_lo"], 9)
                else:
                    pe.wait_ge(s["t_done"], j)
                for k in range(2):
                    for c in range(2):
                        last = mm(ps[0:n, 4 + c, :], pTt[:, k, 0:n], plew[:, k, c * 512:(c + 1) * 512], k == 0, k == 1)
                last.then_inc(s["pw_ready"], 1)

            project_out(0)
            for j in range(9):
                if j + 1 < 9:
                    project_out(j + 1)
                turn_x1(j)
            for j in range(9):
                turn_p(j)
                gate(j)
                embed(j)


OUTS = [("y_prompt", (1, SEQ, D)), ("y_sample", (NSEQ, STEPS, D)), ("k_prompt", (1, 1, SEQ, H, DH)),
        ("v_prompt", (1, 1, SEQ, H, DH)), ("conv_prompt", (1, 1, 3, H * DH)), ("C_prompt", (1, 1, H, DH, DH)),
        ("n_prompt", (1, 1, H, DH)), ("m_prompt", (1, 1, H)), ("k_sample", (1, NSEQ, STEPS, H, DH)),
        ("v_sample", (1, NSEQ, STEPS, H, DH)), ("conv_sample", (1, NSEQ, 3, H * DH)),
        ("C_sample", (1, NSEQ, H, DH, DH)), ("n_sample", (1, NSEQ, H, DH)), ("m_sample", (1, NSEQ, H))]


def kernel(**inputs):
    import numpy as np
    import concourse.bacc as bacc
    from concourse.bass_utils import run_bass_kernel_spmd

    nc = bacc.Bacc("TRN2", target_bir_lowering=False, num_devices=1)
    arrays, io = {}, {}
    for name, a in inputs.items():
        a = np.ascontiguousarray(a)
        arrays[f"in_{name}"] = a
        io[name] = nc.dram_tensor(f"in_{name}", a.shape, mybir.dt.from_np(a.dtype), kind="ExternalInput").ap()
    for name, shape in OUTS:
        io[name] = nc.dram_tensor(f"out_{name}", shape, F32, kind="ExternalOutput").ap()
    program(nc, io)
    r = run_bass_kernel_spmd(nc, [arrays], core_ids=[0])
    return tuple(r.results[0][f"out_{name}"] for name, _ in OUTS)
```
